# Optimizing a Trainium2 kernel written in Bass

```python
import math
import jax, jax.numpy as jnp
from jax import lax
import numpy as np

D_MODEL = 1024
BATCH = 1
SEQ = 256
DEPTH = 1

HEAD_DIM = 64
SB_HEADS = 8
MB_HEADS = 8
SB_WIDTH = SB_HEADS * HEAD_DIM
MB_WIDTH = MB_HEADS * HEAD_DIM
SB_QBLOCK = 128
MB_BLOCK = 256
MB_TOPK = 3
MB_QCHUNK = 64
REL_BUCKETS = 32
REL_MAX_DIST = 128
IN_WIDTH = 3 * SB_WIDTH + 3 * MB_WIDTH + 2 * D_MODEL
N_EXPERTS = 64
N_GROUPS = 8
TOPK_GROUPS = 4
TOPK_EXPERTS = 8
EXPERT_FF = 256
SHARED_FF = 256
ROUTED_SCALE = 2.5
MOE_ROW_BLOCK = 256
N_MOD = 6
EPS = 1e-6
NEG = -1e30


def rms_norm(x, g):
    x32 = x.astype(jnp.float32)
    y = x32 * lax.rsqrt(jnp.mean(x32 * x32, axis=-1, keepdims=True) + EPS)
    return (y * g.astype(jnp.float32)).astype(x.dtype)

def modulate(h, shift, scale):
    return h * (1.0 + scale[:, None, :]) + shift[:, None, :]

def split_heads(t, n_heads):
    b, s, _ = t.shape
    return t.reshape(b, s, n_heads, HEAD_DIM).transpose(0, 2, 1, 3)

def merge_heads(t):
    b, h, s, d = t.shape
    return t.transpose(0, 2, 1, 3).reshape(b, s, h * d)

def t5_bucket(dist):
    n = jnp.maximum(dist, 0)
    max_exact = REL_BUCKETS // 2
    nf = jnp.maximum(n, 1).astype(jnp.float32)
    large = max_exact + (jnp.log(nf / max_exact) / math.log(REL_MAX_DIST / max_exact)
                         * (REL_BUCKETS - max_exact)).astype(jnp.int32)
    large = jnp.minimum(large, REL_BUCKETS - 1)
    return jnp.where(n < max_exact, n, large)

def stick_breaking_attention(q, k, v):
    s_len = q.shape[2]
    scale = HEAD_DIM ** -0.5
    outs = []
    for i in range(s_len // SB_QBLOCK):
        q0 = i * SB_QBLOCK
        kend = q0 + SB_QBLOCK
        qb = q[:, :, q0:kend]
        kb = k[:, :, :kend]
        vb = v[:, :, :kend]
        z = jnp.einsum('bhqd,bhkd->bhqk', qb, kb).astype(jnp.float32) * scale
        qpos = q0 + jnp.arange(SB_QBLOCK)
        kpos = jnp.arange(kend)
        past = kpos[None, :] < qpos[:, None]
        log_beta = jax.nn.log_sigmoid(z)
        log_rest = jnp.where(past, jax.nn.log_sigmoid(-z), 0.0)
        log_skip = lax.cumsum(log_rest, axis=3, reverse=True) - log_rest
        a = jnp.where(past, jnp.exp(log_beta + log_skip), 0.0)
        outs.append(jnp.einsum('bhqk,bhkd->bhqd', a.astype(v.dtype), vb))
    return jnp.concatenate(outs, axis=2)

def moba_attention(q, k, v, rel_bias):
    b, h, s_len, dh = q.shape
    nb = -(-s_len // MB_BLOCK)
    sp = nb * MB_BLOCK
    pad = ((0, 0), (0, 0), (0, sp - s_len), (0, 0))
    kp = jnp.pad(k, pad)
    vp = jnp.pad(v, pad)
    kblk = kp.reshape(b, h, nb, MB_BLOCK, dh)
    vblk = vp.reshape(b, h, nb, MB_BLOCK, dh)
    kbar = jnp.mean(kblk.astype(jnp.float32), axis=3)
    topk = min(MB_TOPK, nb)
    scale = dh ** -0.5
    bi = jnp.arange(b)[:, None, None, None]
    hi = jnp.arange(h)[None, :, None, None]
    hi5 = hi[..., None]
    offs = jnp.arange(MB_BLOCK)

    def chunk(ci):
        q0 = ci * MB_QCHUNK
        qc = lax.dynamic_slice_in_dim(q, q0, MB_QCHUNK, axis=2)
        qpos = q0 + jnp.arange(MB_QCHUNK)
        blk = q0 // MB_BLOCK
        gate = jnp.einsum('bhqd,bhnd->bhqn', qc.astype(jnp.float32), kbar)
        gate = jnp.where(jnp.arange(nb) < blk, gate, NEG)
        _, sel = lax.top_k(gate, topk)
        valid = sel < blk
        ksel = kblk[bi, hi, sel]
        vsel = vblk[bi, hi, sel]
        kpos_sel = sel[..., None] * MB_BLOCK + offs
        bias_sel = rel_bias[hi5, t5_bucket(qpos[:, None, None] - kpos_sel)]
        s_sel = jnp.einsum('bhqd,bhqjnd->bhqjn', qc, ksel).astype(jnp.float32) * scale + bias_sel
        s_sel = jnp.where(valid[..., None], s_sel, NEG).reshape(b, h, MB_QCHUNK, topk * MB_BLOCK)
        k_own = lax.dynamic_slice_in_dim(kp, blk * MB_BLOCK, MB_BLOCK, axis=2)
        v_own = lax.dynamic_slice_in_dim(vp, blk * MB_BLOCK, MB_BLOCK, axis=2)
        dist = qpos[:, None] - (blk * MB_BLOCK + offs)[None, :]
        s_own = jnp.einsum('bhqd,bhnd->bhqn', qc, k_own).astype(jnp.float32) * scale
        s_own = jnp.where(dist >= 0, s_own + rel_bias[:, t5_bucket(dist)], NEG)
        p = jax.nn.softmax(jnp.concatenate([s_sel, s_own], axis=-1), axis=-1)
        p_sel = p[..., :topk * MB_BLOCK].reshape(b, h, MB_QCHUNK, topk, MB_BLOCK)
        p_own = p[..., topk * MB_BLOCK:]
        return (jnp.einsum('bhqjn,bhqjnd->bhqd', p_sel.astype(v.dtype), vsel)
                + jnp.einsum('bhqn,bhnd->bhqd', p_own.astype(v.dtype), v_own))

    outs = lax.map(chunk, jnp.arange(s_len // MB_QCHUNK))
    return outs.transpose(1, 2, 0, 3, 4).reshape(b, h, s_len, dh)

def swiglu(x, w_gate, w_up, w_down):
    return (jax.nn.silu(x @ w_gate) * (x @ w_up)) @ w_down

def moe_ffn(xt, w_router, router_bias, w_gate_e, w_up_e, w_down_e, w_gate_sh, w_up_sh, w_down_sh):
    t = xt.shape[0]
    scores = jax.nn.sigmoid((xt @ w_router).astype(jnp.float32))
    choice = scores + router_bias.astype(jnp.float32)
    grp = choice.reshape(t, N_GROUPS, N_EXPERTS // N_GROUPS)
    grp_score = jnp.sum(lax.top_k(grp, 2)[0], axis=-1)
    _, gidx = lax.top_k(grp_score, TOPK_GROUPS)
    gmask = jnp.any(gidx[..., None] == jnp.arange(N_GROUPS), axis=1)
    emask = jnp.repeat(gmask, N_EXPERTS // N_GROUPS, axis=1)
    _, eidx = lax.top_k(jnp.where(emask, choice, NEG), TOPK_EXPERTS)
    wts = jnp.take_along_axis(scores, eidx, axis=1)
    wts = wts / jnp.sum(wts, axis=-1, keepdims=True) * ROUTED_SCALE

    n_assign = t * TOPK_EXPERTS
    e_flat = eidx.reshape(n_assign)
    tok_flat = jnp.repeat(jnp.arange(t, dtype=jnp.int32), TOPK_EXPERTS)
    w_flat = wts.reshape(n_assign)
    order = jnp.argsort(e_flat)
    e_s = e_flat[order]
    counts = jnp.bincount(e_flat, length=N_EXPERTS)
    start = jnp.cumsum(counts) - counts
    pcounts = (counts + MOE_ROW_BLOCK - 1) // MOE_ROW_BLOCK * MOE_ROW_BLOCK
    pend = jnp.cumsum(pcounts)
    pstart = pend - pcounts
    dest = pstart[e_s] + (jnp.arange(n_assign) - start[e_s])
    n_blk = -(-n_assign // MOE_ROW_BLOCK) + N_EXPERTS
    n_rows = n_blk * MOE_ROW_BLOCK
    tok_buf = jnp.zeros((n_rows,), jnp.int32).at[dest].set(tok_flat[order])
    w_buf = jnp.zeros((n_rows,), jnp.float32).at[dest].set(w_flat[order])
    blk_expert = jnp.minimum(
        jnp.searchsorted(pend, jnp.arange(n_blk) * MOE_ROW_BLOCK, side='right'), N_EXPERTS - 1)

    def body(acc, bidx):
        rows = lax.dynamic_slice_in_dim(tok_buf, bidx * MOE_ROW_BLOCK, MOE_ROW_BLOCK)
        wr = lax.dynamic_slice_in_dim(w_buf, bidx * MOE_ROW_BLOCK, MOE_ROW_BLOCK)
        e = blk_expert[bidx]
        ye = swiglu(xt[rows], w_gate_e[e], w_up_e[e], w_down_e[e]) * wr[:, None]
        return acc.at[rows].add(ye.astype(acc.dtype)), None

    routed, _ = lax.scan(body, jnp.zeros_like(xt), jnp.arange(n_blk))
    return routed + swiglu(xt, w_gate_sh, w_up_sh, w_down_sh)

def first_inputs(seed: int = 0) -> dict:
    key = jax.random.key(seed)
    ks = jax.random.split(key, 24)
    f32 = jnp.float32
    L, D, E = DEPTH, D_MODEL, N_EXPERTS

    def nrm(k, shape, s):
        return jax.random.normal(k, shape, f32) * s

    return {
        "x": nrm(ks[0], (BATCH, SEQ, D), 1.0),
        "c": nrm(ks[1], (BATCH, D), 1.0),
        "norm1_g": 1.0 + nrm(ks[2], (L, D), 0.05),
        "norm2_g": 1.0 + nrm(ks[3], (L, D), 0.05),
        "w_ada": nrm(ks[4], (L, D, N_MOD * D), 0.5 * D ** -0.5),
        "b_ada": nrm(ks[5], (L, N_MOD * D), 0.02),
        "w_in": nrm(ks[6], (L, D, IN_WIDTH), D ** -0.5),
        "w_branch_sb": nrm(ks[7], (L, SB_WIDTH, D), SB_WIDTH ** -0.5),
        "w_branch_mb": nrm(ks[8], (L, MB_WIDTH, D), MB_WIDTH ** -0.5),
        "w_out": nrm(ks[9], (L, D, D), D ** -0.5),
        "w_router": nrm(ks[10], (L, D, E), D ** -0.5),
        "router_bias": nrm(ks[11], (L, E), 0.01),
        "w_gate_e": nrm(ks[12], (L, E, D, EXPERT_FF), D ** -0.5),
        "w_up_e": nrm(ks[13], (L, E, D, EXPERT_FF), D ** -0.5),
        "w_down_e": nrm(ks[14], (L, E, EXPERT_FF, D), EXPERT_FF ** -0.5),
        "w_gate_sh": nrm(ks[15], (L, D, SHARED_FF), D ** -0.5),
        "w_up_sh": nrm(ks[16], (L, D, SHARED_FF), D ** -0.5),
        "w_down_sh": nrm(ks[17], (L, SHARED_FF, D), SHARED_FF ** -0.5),
        "rel_bias": nrm(ks[18], (MB_HEADS, REL_BUCKETS), 0.5),
        "final_g": 1.0 + nrm(ks[19], (D,), 0.05),
    }

def first_block(x, c, norm1_g, norm2_g, w_ada, b_ada, w_in, w_branch_sb, w_branch_mb, w_out,
              w_router, router_bias, w_gate_e, w_up_e, w_down_e, w_gate_sh, w_up_sh, w_down_sh,
              rel_bias, final_g):
    b, s, d = x.shape
    cuts = [SB_WIDTH, 2 * SB_WIDTH, 3 * SB_WIDTH,
            3 * SB_WIDTH + MB_WIDTH, 3 * SB_WIDTH + 2 * MB_WIDTH, 3 * SB_WIDTH + 3 * MB_WIDTH,
            3 * SB_WIDTH + 3 * MB_WIDTH + D_MODEL]
    for l in range(DEPTH):
        mod = jax.nn.silu(c) @ w_ada[l] + b_ada[l]
        shift1, scale1, gate1, shift2, scale2, gate2 = jnp.split(mod, N_MOD, axis=-1)

        h = modulate(rms_norm(x, norm1_g[l]), shift1, scale1)
        proj = h @ w_in[l]
        q_sb, k_sb, v_sb, q_mb, k_mb, v_mb, g_sb, g_mb = jnp.split(proj, cuts, axis=-1)
        o_sb = stick_breaking_attention(split_heads(q_sb, SB_HEADS), split_heads(k_sb, SB_HEADS),
                                        split_heads(v_sb, SB_HEADS))
        o_mb = moba_attention(split_heads(q_mb, MB_HEADS), split_heads(k_mb, MB_HEADS),
                              split_heads(v_mb, MB_HEADS), rel_bias)
        merged = (jax.nn.sigmoid(g_sb) * (merge_heads(o_sb) @ w_branch_sb[l])
                  + jax.nn.sigmoid(g_mb) * (merge_heads(o_mb) @ w_branch_mb[l]))
        x = x + gate1[:, None, :] * (merged @ w_out[l])

        h2 = modulate(rms_norm(x, norm2_g[l]), shift2, scale2)
        y = moe_ffn(h2.reshape(b * s, d), w_router[l], router_bias[l], w_gate_e[l], w_up_e[l],
                    w_down_e[l], w_gate_sh[l], w_up_sh[l], w_down_sh[l]).reshape(b, s, d)
        x = x + gate2[:, None, :] * y
    return rms_norm(x, final_g)


GRID_W = 64
NEG_INF = -1e30

NA_HEADS = 8
NA_HEAD_DIM = 64
NA_WIN_H = 8
NA_WIN_W = 16
NA_QBLOCK_W = 16
NA_BAND_W = NA_QBLOCK_W + NA_WIN_W
NA_WIDTH = NA_HEADS * NA_HEAD_DIM

MLA_HEADS = 8
MLA_QK_NOPE = 64
MLA_QK_ROPE = 32
MLA_V_DIM = 64
MLA_Q_LORA = 256
MLA_KV_LORA = 128
MLA_QBLOCK = 128
MLA_WIDTH = MLA_HEADS * MLA_V_DIM
ROPE_THETA = 10000.0

MIX_WIDTH = NA_WIDTH + MLA_WIDTH
D_IN = 3 * NA_WIDTH + MLA_Q_LORA + MLA_KV_LORA + MLA_QK_ROPE
D_FF = 2816


def rms_norm_2(x, g):
    xf = x.astype(jnp.float32)
    y = xf * lax.rsqrt(jnp.mean(xf * xf, axis=-1, keepdims=True) + EPS)
    return (y * g.astype(jnp.float32)).astype(x.dtype)

def swiglu_2(h, w_gu, w_down):
    gate, up = jnp.split(h @ w_gu, 2, axis=-1)
    return (jax.nn.silu(gate) * up) @ w_down

def grid_rope_tables(seq):
    t = jnp.arange(seq)
    row = (t // GRID_W).astype(jnp.float32)
    col = (t % GRID_W).astype(jnp.float32)
    n_freq = MLA_QK_ROPE // 4
    inv_freq = 1.0 / (ROPE_THETA ** (jnp.arange(n_freq, dtype=jnp.float32) / n_freq))
    ang = jnp.concatenate([row[:, None] * inv_freq[None, :], col[:, None] * inv_freq[None, :]], axis=-1)
    return jnp.cos(ang), jnp.sin(ang)

def apply_rope(x, cos, sin):
    xf = x.astype(jnp.float32)
    x1, x2 = jnp.split(xf, 2, axis=-1)
    return jnp.concatenate([x1 * cos - x2 * sin, x2 * cos + x1 * sin], axis=-1).astype(x.dtype)

def neighbourhood_attention(q, k, v, rpb):
    B, S, H, D = q.shape
    R = S // GRID_W
    KH = min(NA_WIN_H, R)
    NCB = GRID_W // NA_QBLOCK_W
    rows = jnp.arange(R)
    row_start = jnp.clip(rows - KH // 2, 0, R - KH)
    key_rows = row_start[:, None] + jnp.arange(KH)
    c0 = jnp.arange(NCB) * NA_QBLOCK_W
    band_start = jnp.clip(c0 - NA_WIN_W // 2, 0, GRID_W - NA_BAND_W)
    key_cols = band_start[:, None] + jnp.arange(NA_BAND_W)
    q_cols = c0[:, None] + jnp.arange(NA_QBLOCK_W)
    win_start = jnp.clip(q_cols - NA_WIN_W // 2, 0, GRID_W - NA_WIN_W)
    kc = key_cols[:, None, :]
    col_mask = (kc >= win_start[..., None]) & (kc < win_start[..., None] + NA_WIN_W)
    row_off = key_rows - rows[:, None] + (NA_WIN_H - 1)
    col_off = jnp.clip(kc - q_cols[:, :, None] + (NA_WIN_W - 1), 0, 2 * NA_WIN_W - 2)
    bias = rpb.astype(jnp.float32)[:, row_off[:, None, None, :, None], col_off[None, :, :, None, :]]
    bias = bias.transpose(1, 2, 0, 3, 4, 5)
    bias = jnp.where(col_mask[:, None, :, None, :], bias, NEG_INF)
    qg = q.reshape(B, R, NCB, NA_QBLOCK_W, H, D)
    ridx = key_rows[:, None, :, None]
    cidx = key_cols[None, :, None, :]
    kg = k.reshape(B, R, GRID_W, H, D)[:, ridx, cidx]
    vg = v.reshape(B, R, GRID_W, H, D)[:, ridx, cidx]
    s = jnp.einsum('brnqhd,brnijhd->brnhqij', qg, kg).astype(jnp.float32) * (D ** -0.5)
    s = s + bias[None]
    sh = s.shape
    p = jax.nn.softmax(s.reshape(sh[:-2] + (sh[-2] * sh[-1],)), axis=-1).reshape(sh)
    o = jnp.einsum('brnhqij,brnijhd->brnqhd', p.astype(v.dtype), vg)
    return o.reshape(B, S, H * D)

def latent_attention(c_q, c_kv, k_rope, q_norm_g, w_uq, kv_norm_g, w_ukv, cos, sin):
    B, S, _ = c_q.shape
    H = MLA_HEADS
    q = (rms_norm_2(c_q, q_norm_g) @ w_uq).reshape(B, S, H, MLA_QK_NOPE + MLA_QK_ROPE)
    q_nope, q_rot = jnp.split(q, [MLA_QK_NOPE], axis=-1)
    kv = (rms_norm_2(c_kv, kv_norm_g) @ w_ukv).reshape(B, S, H, MLA_QK_NOPE + MLA_V_DIM)
    k_nope, v = jnp.split(kv, [MLA_QK_NOPE], axis=-1)
    q_rot = apply_rope(q_rot, cos[:, None, :], sin[:, None, :])
    k_rot = apply_rope(k_rope, cos, sin)
    scale = (MLA_QK_NOPE + MLA_QK_ROPE) ** -0.5
    nqb = S // MLA_QBLOCK

    def block(args):
        qn, qr = args
        s = (jnp.einsum('bqhd,bkhd->bhqk', qn, k_nope)
             + jnp.einsum('bqhd,bkd->bhqk', qr, k_rot)).astype(jnp.float32) * scale
        p = jax.nn.softmax(s, axis=-1)
        return jnp.einsum('bhqk,bkhd->bqhd', p.astype(v.dtype), v)

    qn_b = q_nope.reshape(B, nqb, MLA_QBLOCK, H, MLA_QK_NOPE).swapaxes(0, 1)
    qr_b = q_rot.reshape(B, nqb, MLA_QBLOCK, H, MLA_QK_ROPE).swapaxes(0, 1)
    o = lax.map(block, (qn_b, qr_b))
    return o.swapaxes(0, 1).reshape(B, S, H * MLA_V_DIM)

def second_inputs(seed: int = 0) -> dict:
    key = jax.random.key(seed)
    ks = iter(jax.random.split(key, 32))

    def w(shape, fan_in):
        return jax.random.normal(next(ks), shape, jnp.float32) * (fan_in ** -0.5)

    def gain(n):
        return 1.0 + 0.05 * jax.random.normal(next(ks), (DEPTH, n), jnp.float32)

    L = DEPTH
    return {
        "x": jax.random.normal(next(ks), (BATCH, SEQ, D_MODEL), jnp.float32),
        "ffn1_pre_g": gain(D_MODEL),
        "ffn1_w_gu": w((L, D_MODEL, 2 * D_FF), D_MODEL),
        "ffn1_w_down": w((L, D_FF, D_MODEL), D_FF),
        "ffn1_post_g": gain(D_MODEL),
        "mix_pre_g": gain(D_MODEL),
        "w_in": w((L, D_MODEL, D_IN), D_MODEL),
        "na_rpb": 0.1 * jax.random.normal(next(ks), (L, NA_HEADS, 2 * NA_WIN_H - 1, 2 * NA_WIN_W - 1), jnp.float32),
        "mla_q_norm_g": gain(MLA_Q_LORA),
        "mla_w_uq": w((L, MLA_Q_LORA, MLA_HEADS * (MLA_QK_NOPE + MLA_QK_ROPE)), MLA_Q_LORA),
        "mla_kv_norm_g": gain(MLA_KV_LORA),
        "mla_w_ukv": w((L, MLA_KV_LORA, MLA_HEADS * (MLA_QK_NOPE + MLA_V_DIM)), MLA_KV_LORA),
        "na_out_norm_g": gain(NA_WIDTH),
        "mla_out_norm_g": gain(MLA_WIDTH),
        "w_out": w((L, MIX_WIDTH, D_MODEL), MIX_WIDTH),
        "mix_post_g": gain(D_MODEL),
        "ffn2_pre_g": gain(D_MODEL),
        "ffn2_w_gu": w((L, D_MODEL, 2 * D_FF), D_MODEL),
        "ffn2_w_down": w((L, D_FF, D_MODEL), D_FF),
        "ffn2_post_g": gain(D_MODEL),
    }

def second_block(x, ffn1_pre_g, ffn1_w_gu, ffn1_w_down, ffn1_post_g, mix_pre_g, w_in, na_rpb,
              mla_q_norm_g, mla_w_uq, mla_kv_norm_g, mla_w_ukv, na_out_norm_g, mla_out_norm_g,
              w_out, mix_post_g, ffn2_pre_g, ffn2_w_gu, ffn2_w_down, ffn2_post_g):
    B, S, _ = x.shape
    cos, sin = grid_rope_tables(S)
    split_at = [NA_WIDTH, 2 * NA_WIDTH, 3 * NA_WIDTH,
                3 * NA_WIDTH + MLA_Q_LORA, 3 * NA_WIDTH + MLA_Q_LORA + MLA_KV_LORA]
    h = x
    for l in range(DEPTH):
        f = swiglu_2(rms_norm_2(h, ffn1_pre_g[l]), ffn1_w_gu[l], ffn1_w_down[l])
        h = h + 0.5 * rms_norm_2(f, ffn1_post_g[l])
        z = rms_norm_2(h, mix_pre_g[l]) @ w_in[l]
        q_na, k_na, v_na, c_q, c_kv, k_rope = jnp.split(z, split_at, axis=-1)
        hs = (B, S, NA_HEADS, NA_HEAD_DIM)
        o_na = neighbourhood_attention(q_na.reshape(hs), k_na.reshape(hs), v_na.reshape(hs), na_rpb[l])
        o_mla = latent_attention(c_q, c_kv, k_rope, mla_q_norm_g[l], mla_w_uq[l],
                                 mla_kv_norm_g[l], mla_w_ukv[l], cos, sin)
        mixed = jnp.concatenate([rms_norm_2(o_na, na_out_norm_g[l]),
                                 rms_norm_2(o_mla, mla_out_norm_g[l])], axis=-1) @ w_out[l]
        h = h + rms_norm_2(mixed, mix_post_g[l])
        f = swiglu_2(rms_norm_2(h, ffn2_pre_g[l]), ffn2_w_gu[l], ffn2_w_down[l])
        h = h + 0.5 * rms_norm_2(f, ffn2_post_g[l])
    return h


def setup_inputs(seed=0):
    out = dict(first_inputs(seed))
    for name, value in second_inputs(seed + 1).items():
        if name != "x":
            out[name + "_2"] = value
    return out


def reference(
    x, c, norm1_g, norm2_g, w_ada, b_ada, w_in, w_branch_sb, w_branch_mb, w_out, w_router,
    router_bias, w_gate_e, w_up_e, w_down_e, w_gate_sh, w_up_sh, w_down_sh, rel_bias, final_g,
    ffn1_pre_g_2, ffn1_w_gu_2, ffn1_w_down_2, ffn1_post_g_2, mix_pre_g_2, w_in_2, na_rpb_2,
    mla_q_norm_g_2, mla_w_uq_2, mla_kv_norm_g_2, mla_w_ukv_2, na_out_norm_g_2, mla_out_norm_g_2,
    w_out_2, mix_post_g_2, ffn2_pre_g_2, ffn2_w_gu_2, ffn2_w_down_2, ffn2_post_g_2,
):
    x = first_block(
        x, c, norm1_g, norm2_g, w_ada, b_ada, w_in, w_branch_sb, w_branch_mb, w_out, w_router,
        router_bias, w_gate_e, w_up_e, w_down_e, w_gate_sh, w_up_sh, w_down_sh, rel_bias,
        final_g,
    )
    return second_block(
        x, ffn1_pre_g_2, ffn1_w_gu_2, ffn1_w_down_2, ffn1_post_g_2, mix_pre_g_2, w_in_2,
        na_rpb_2, mla_q_norm_g_2, mla_w_uq_2, mla_kv_norm_g_2, mla_w_ukv_2, na_out_norm_g_2,
        mla_out_norm_g_2, w_out_2, mix_post_g_2, ffn2_pre_g_2, ffn2_w_gu_2, ffn2_w_down_2,
        ffn2_post_g_2,
    )


_drawn_inputs = setup_inputs


def setup_inputs(seed=0):
    import zlib

    import numpy as np

    out = dict(_drawn_inputs(seed))
    spreads = {}
    factors = {'mla_q_norm_g_2': 2.843, 'ffn2_post_g_2': 3.271}
    for name, (base, spread) in spreads.items():
        noise = np.random.default_rng([zlib.crc32(name.encode()), seed]).standard_normal(out[name].shape)
        drawn = base * np.exp(spread * noise) if base else spread * noise
        out[name] = __import__('jax').numpy.asarray(drawn.astype(out[name].dtype))
    for name, factor in factors.items():
        out[name] = (out[name] * factor).astype(out[name].dtype)
    return out
```

```python
import math
from contextlib import ExitStack

import concourse.bass as bass
import numpy as np
from concourse import mybir

ALU = mybir.AluOpType
ACT = mybir.ActivationFunctionType
F32 = mybir.dt.float32
F32R = mybir.dt.float32r
BF16 = mybir.dt.bfloat16
AX = mybir.AxisListType.X

P = 128
T = 256
TB = T // P
D = 1024
DC = D // P
HD = 64
NH = 8
E = 64
NGRP = 8
FF = 256
D_FF = 2816
EPS = 1e-6
BIG = 1e30
QW = 768
KVW = 1024
SMALL = 416
UNIT = 2048

N_ADA, N_WIN, N_FF = 12, 10, D_FF // FF
G_ADA = 0
G_WIN = G_ADA + N_ADA
G_WB = G_WIN + N_WIN
G_WO = G_WB + 2
G_MOE = G_WO + 2
N_MOE = E + 1
G_FF1 = G_MOE + N_MOE
G_WIN2 = G_FF1 + N_FF
G_MLA = G_WIN2 + 4
G_WO2 = G_MLA + 1
G_FF2 = G_WO2 + 2
D_MOE, D_FF1, D_FF2 = 0, N_MOE, N_MOE + N_FF

C_ID, C_TRI, C_MASK, C_MIN, C_NA, C_COS, C_SIN, C_END = 0, 128, 256, 384, 512, 576, 608, 640
BX = 384
NR = 7 * 128


def at(const, it, per):
    return const if it is None else it * per + const


def build(nc, a, out):
    ctx = ExitStack()
    with ctx:
        def sb(name, shape, dt=F32):
            return ctx.enter_context(nc.sbuf_tensor(name, shape, dt))

        def sem(name):
            return ctx.enter_context(nc.semaphore(name))

        raw_g = sb("raw_g", [P, 2, 2 * UNIT])
        raw_d = sb("raw_d", [P, 2, UNIT])
        g_hi = sb("g_hi", [P, 2, UNIT], F32R)
        g_lo = sb("g_lo", [P, 2, UNIT], F32R)
        d_hi = sb("d_hi", [P, UNIT], F32R)
        d_lo = sb("d_lo", [P, UNIT], F32R)
        xt_hi = sb("xt_hi", [P, DC, T], F32R)
        xt_lo = sb("xt_lo", [P, DC, T], F32R)
        at_hi = sb("at_hi", [P, 2, T], F32R)
        at_lo = sb("at_lo", [P, 2, T], F32R)
        x = sb("x_res", [P, TB, D])
        h = sb("h_tok", [P, TB, D])
        att = sb("att", [P, 3072])
        arena = sb("arena", [P, 14 * 1024])
        con = sb("con", [P, C_END])
        ones = sb("ones", [P, P])
        zeros = sb("zeros", [P, 512], BF16)
        st = sb("stats", [P, 64])

        K = 256

        def area(kib, n):
            return arena[:, int(kib * K):int(kib * K) + n]

        shift1, gain1 = area(0, D), area(4, D)
        v_tok = area(0, TB * D).rearrange("p (b n) -> p b n", b=TB)
        gate1, shift2, gain2, gate2 = area(8, D), area(12, D), area(16, D), area(20, D)
        b_ada_row = area(24, 6 * D)
        g1_in, g2_in = area(48, D), area(52, D)
        qT, kT = ([area(24 + 4 * i, 4 * T).rearrange("p (m t) -> p m t", m=4) for i in (0, 2)],
                  [area(28 + 4 * i, 4 * T).rearrange("p (m t) -> p m t", m=4) for i in (0, 2)])
        sig = area(40, TB * 2 * D).rearrange("p (b n) -> p b n", b=TB)
        mb_bias = raw_d[:, 1, :].rearrange("p (h k) -> p h k", h=NH)
        a_sb = area(24, 2 * FF).rearrange("p (b n) -> p b n", b=TB)
        silu = area(26, 2 * FF).rearrange("p (b n) -> p b n", b=TB)
        w_rt = area(28, DC * E).rearrange("p (c e) -> p c e", c=DC)
        rt = area(30, 4 * E * 4)
        wts = area(34, TB * N_MOE).rearrange("p (b e) -> p b e", b=TB)
        rbias = area(35, E)
        final_g, pre1, post1 = area(36, D), area(40, D), area(44, D)
        mixpre, mixpost = area(48, D), area(52, D)
        outg = area(12, D)
        qn_g, kvn_g = area(16, 256), area(17, 128)
        pre2, post2 = area(0, D), area(8, D)
        na_bias = [area(0, NH * T).rearrange("p (h k) -> p h k", h=NH),
                   att[:, 1024:3072].rearrange("p (h k) -> p h k", h=NH)]
        v2 = area(8, TB * 512).rearrange("p (b n) -> p b n", b=TB)
        small = area(18, TB * SMALL).rearrange("p (b n) -> p b n", b=TB)
        qT2 = area(28, 4 * T).rearrange("p (m t) -> p m t", m=4)
        kT2 = area(32, 4 * T).rearrange("p (m t) -> p m t", m=4)
        q_tok = area(36, TB * QW).rearrange("p (b n) -> p b n", b=TB)
        kv_tok = area(42, TB * KVW).rearrange("p (b n) -> p b n", b=TB)
        k_full = area(28, TB * QW).rearrange("p (b n) -> p b n", b=TB)
        qTm = area(0, NH * T).rearrange("p (h t) -> p h t", h=NH)
        kTm = att[:, 1024:3072].rearrange("p (h t) -> p h t", h=NH)
        rope_t = area(24, 4 * TB * NH * 16).rearrange("p (i b n) -> p i b n", i=4, b=TB)

        z_sb = h[:, :, :].rearrange("p b n -> p (b n)")[:, 0:4 * 384]
        l_sb = att[:, 0:1536]
        p_sb = att[:, 1536:3072]
        s_buf = [att[:, 0:T], att[:, T:2 * T]]
        pT_sb = [att[:, 512:768].rearrange("p (c q) -> p c q", c=2),
                 att[:, 768:1024].rearrange("p (c q) -> p c q", c=2)]
        o_mb = att[:, 2048:3072].rearrange("p (b n) -> p b n", b=TB)
        relb_in, bucket_in = att[0:33, 0:NH], att[0:33, 16:16 + BX]
        t_bias = att[0:NH, 512:512 + BX]
        rpb_pad = att[0:NH, 1024:1024 + NR]
        c_col, c_sil = st[:, 0:8], st[:, 8:16]

        ps = [ctx.enter_context(nc.psum_tensor(f"bank{i}_{j}", [P, 2, 512], F32))
              for i, j in ((0, 1), (2, 3), (4, 5), (6, 7))]

        def bank(i):
            return ps[i // 2][:, i % 2, :]

        ident = con[:, C_ID:C_ID + P]
        tri = con[:, C_TRI:C_TRI + P]

        t_dram = nc.dram_tensor("t_scratch", (P, NH, BX), F32, kind="Internal").ap()
        n_dram = nc.dram_tensor("n_scratch", (64, NH, NR), F32, kind="Internal").ap()

        landed_g = [sem("landed_g0"), sem("landed_g1")]
        landed_d = [sem("landed_d0"), sem("landed_d1")]
        hi_g, lo_g, used_g = sem("hi_g"), sem("lo_g"), sem("used_g")
        hi_d, lo_d, used_d = sem("hi_d"), sem("lo_d"), sem("used_d")
        silu_done, gated, tr_done = sem("silu_done"), sem("gated"), sem("tr_done")
        at_hi_s, at_lo_s = sem("at_hi_s"), sem("at_lo_s")
        xt_ps, xt_hi_s, xt_lo_s = sem("xt_ps"), sem("xt_hi_s"), sem("xt_lo_s")
        h_ready, x_ready = sem("h_ready"), sem("x_ready")
        in_ = {n: sem("in_" + n) for n in ("c", "x", "con", "bada", "g1", "g2", "relb", "bucket", "rpb",
                                           "tb", "nb", "tw", "nw", "wrt", "rbias", "gains", "post",
                                           "outg", "ff2g")}
        chain_v, chain_a, chain_p = sem("chain_v"), sem("chain_a"), sem("chain_p")
        set_up = sem("set_up")
        c_silu, c_bc = sem("c_silu"), sem("c_bc")
        ada_ev = sem("ada_ev")
        tb_ps, tb_sb = sem("tb_ps"), sem("tb_sb")
        ev_a, ev_v = sem("ev_a"), sem("ev_v")
        ss_a, ms_v, sd_a = sem("ss_a"), sem("ms_v"), sem("sd_a")
        sb_z, sb_zc, sb_ab, sb_ln, sb_r = sem("sb_z"), sem("sb_zc"), sem("sb_ab"), sem("sb_ln"), sem("sb_r")
        sb_i, sb_t, sb_a, sb_o, sb_oh, sb_ol = (sem("sb_i"), sem("sb_t"), sem("sb_a"), sem("sb_o"),
                                                sem("sb_oh"), sem("sb_ol"))
        s_ps, s_max, s_exp, s_pt, s_ptc, s_o, s_fin = (sem("s_ps"), sem("s_max"), sem("s_exp"),
                                                       sem("s_pt"), sem("s_ptc"), sem("s_o"), sem("s_fin"))
        ot_ps, ot_hi, ot_lo = sem("ot_ps"), sem("ot_hi"), sem("ot_lo")
        rt_ps, rt_sc, rt_w = sem("rt_ps"), sem("rt_sc"), sem("rt_w")
        cn_ready, cn_ps, cn_hi, cn_lo = sem("cn_ready"), sem("cn_ps"), sem("cn_hi"), sem("cn_lo")
        na_ready, roped, mt_ps, mt_ev_a, mt_ev_v = (sem("na_ready"), sem("roped"), sem("mt_ps"),
                                                    sem("mt_ev_a"), sem("mt_ev_v"))
        s_out = sem("s_out")

        block = ctx.enter_context(nc.Block())

        def raw_dense(g, u):
            return raw_g[:, g % 2, u * UNIT:(u + 1) * UNIT]

        def raw_gated(g, u):
            return raw_g[:, g % 2, :].rearrange("p (g c n) -> p c g n", g=2, c=DC)[:, 4 * u:4 * u + 4, :, :]

        def dense_w(buf, u, c4, lo, n):
            return buf[:, u, c4 * 512 + lo:c4 * 512 + lo + n]

        EV_A, EV_V = {}, {}
        n_a = n_v = 0
        for g in [*range(G_WIN, G_WIN + N_WIN), *range(G_WIN2, G_WIN2 + 4), G_MLA]:
            gate = G_WIN + 6 <= g < G_WIN + N_WIN
            n_a += 4 if g == G_MLA else 2 if gate else 1
            n_v += 4 if g == G_MLA else 0 if gate else 1
            EV_A[g], EV_V[g] = n_a, n_v

        FFN_PHASES = {"moe": (G_MOE, D_MOE, N_MOE), "ff1": (G_FF1, D_FF1, N_FF), "ff2": (G_FF2, D_FF2, N_FF)}

        @block.sync
        def _(sp):
            def free_g(g, it=None):
                if g >= 2:
                    sp.wait_ge(lo_g, at(2 * g - 2, it, 4))

            def load_dense(g, src, width=512, chunks=DC):
                free_g(g)
                half = chunks // 2
                for u in range(2):
                    dst = raw_dense(g, u)[:, 0:half * width].rearrange("p (c n) -> p c n", c=half)
                    sp.dma_start(dst, src[:, u * half:(u + 1) * half, :]).then_inc(landed_g[g % 2], 16)

            def load_gated(g, gate, up, it=None):
                free_g(g, it)
                for k, src in enumerate((gate, up)):
                    dst = raw_g[:, g % 2, k * UNIT:(k + 1) * UNIT].rearrange("p (c n) -> p c n", c=DC)
                    sp.dma_start(dst, src.rearrange("(p c) n -> p c n", c=DC)).then_inc(landed_g[g % 2], 16)

            def load_down(d, src, it=None):
                if d >= 2:
                    sp.wait_ge(lo_d, at(d - 1, it, 2))
                dst = raw_d[:, d % 2, :].rearrange("p (c n) -> p c n", c=2)
                sp.dma_start(dst, src.rearrange("(p c) n -> p c n", c=2)).then_inc(landed_d[d % 2], 16)

            def one(src, i):
                return src[bass.ds(i, 1)].rearrange("e k n -> (e k) n") if not isinstance(i, int) else src[i]

            def gated_stream(name, gate_up, down):
                g0, d0, n = FFN_PHASES[name]
                load_gated(g0, *gate_up(0, None))
                load_gated(g0 + 1, *gate_up(1, None))
                load_down(d0, down(0, None))
                load_down(d0 + 1, down(1, None))
                with sp.Fori(0, (n - 3) // 2) as it:
                    for j in range(2):
                        load_gated(g0 + 2 + j, *gate_up(2 + j, it), it)
                        load_down(d0 + 2 + j, down(2 + j, it), it)
                load_gated(g0 + n - 1, *gate_up(n - 1, None))
                load_down(d0 + n - 1, down(n - 1, None))

            w_ada = a["w_ada"][0].rearrange("(p c) n -> p c n", c=DC)
            w_in = a["w_in"][0].rearrange("(p c) n -> p c n", c=DC)
            for t in range(N_ADA):
                load_dense(G_ADA + t, w_ada[:, :, t * 512:(t + 1) * 512])
                if t == 2:
                    sp.wait_ge(in_["tw"], 16)
                    sp.dma_start(mb_bias, bass.AP(t_dram.tensor, 127, [[NH * BX - 1, P], [BX, NH], [1, T]]))\
                        .then_inc(in_["tb"], 16)
            for t in range(N_WIN):
                load_dense(G_WIN + t, w_in[:, :, t * 512:(t + 1) * 512])
            for i, n in enumerate(("w_branch_sb", "w_branch_mb")):
                load_dense(G_WB + i, a[n][0].rearrange("(c p) n -> p c n", p=P), D, 4)
            w_out = a["w_out"][0].rearrange("(p c) n -> p c n", c=DC)
            for i in range(2):
                load_dense(G_WO + i, w_out[:, :, i * 512:(i + 1) * 512])
            sp.wait_ge(h_ready, 2)
            sp.dma_start(w_rt, a["w_router"][0].rearrange("(p c) n -> p c n", c=DC)).then_inc(in_["wrt"], 16)
            sp.dma_start(rbias, a["router_bias"].to_broadcast([P, E])).then_inc(in_["rbias"], 16)
            for dst, n in ((final_g, "final_g"), (pre1, "ffn1_pre_g_2"), (post1, "ffn1_post_g_2"),
                           (mixpre, "mix_pre_g_2"), (mixpost, "mix_post_g_2")):
                src = a[n].rearrange("(o n) -> o n", o=1) if n == "final_g" else a[n]
                sp.dma_start(dst, src.to_broadcast([P, D])).then_inc(in_["gains"], 16)

            def moe_gate_up(s, it):
                if s == E:
                    return a["w_gate_sh"][0], a["w_up_sh"][0]
                i = at(s, it, 2)
                return one(a["w_gate_e"][0], i), one(a["w_up_e"][0], i)

            def moe_down(s, it):
                return a["w_down_sh"][0] if s == E else one(a["w_down_e"][0], at(s, it, 2))

            def ff_stream(w_gu, w_down):
                def gate_up(s, it):
                    if it is None:
                        return w_gu[:, s * FF:(s + 1) * FF], w_gu[:, D_FF + s * FF:D_FF + (s + 1) * FF]
                    return (w_gu[:, bass.ds(it * (2 * FF) + s * FF, FF)],
                            w_gu[:, bass.ds(it * (2 * FF) + (D_FF + s * FF), FF)])

                def down(s, it):
                    if it is None:
                        return w_down[s * FF:(s + 1) * FF, :]
                    return w_down[bass.ds(it * (2 * FF) + s * FF, FF), :]
                return gate_up, down

            gated_stream("moe", moe_gate_up, moe_down)
            gated_stream("ff1", *ff_stream(a["ffn1_w_gu_2"][0], a["ffn1_w_down_2"][0]))
            w_in2 = a["w_in_2"][0].rearrange("(p c) n -> p c n", c=DC)
            for t in range(4):
                w = 512 if t < 3 else SMALL
                load_dense(G_WIN2 + t, w_in2[:, :, t * 512:t * 512 + w], w)
            for b in range(TB):
                for rl in range(2):
                    for r in range(4):
                        off = (3 + r - 2 * b - rl) * P + 63
                        sp.dma_start(na_bias[b][rl * 64:(rl + 1) * 64, :, r * 64:(r + 1) * 64],
                                     bass.AP(n_dram.tensor, off, [[NH * NR - 1, 64], [NR, NH], [1, 64]]))\
                            .then_inc(in_["nb"], 16)
            for i, n in enumerate(("na_out_norm_g_2", "mla_out_norm_g_2")):
                sp.dma_start(outg[:, i * 512:(i + 1) * 512], a[n].to_broadcast([P, 512])).then_inc(in_["outg"], 16)
            sp.dma_start(qn_g, a["mla_q_norm_g_2"].to_broadcast([P, 256])).then_inc(in_["outg"], 16)
            sp.dma_start(kvn_g, a["mla_kv_norm_g_2"].to_broadcast([P, 128])).then_inc(in_["outg"], 16)
            g = G_MLA
            free_g(g)
            sp.dma_start(raw_g[:, g % 2, 0:2 * QW].rearrange("p (c n) -> p c n", c=2),
                         a["mla_w_uq_2"][0].rearrange("(c p) n -> p c n", p=P)).then_inc(landed_g[g % 2], 16)
            sp.dma_start(raw_g[:, g % 2, UNIT:UNIT + KVW], a["mla_w_ukv_2"][0]).then_inc(landed_g[g % 2], 16)
            w_out2 = a["w_out_2"][0].rearrange("(p c) n -> p c n", c=DC)
            for i in range(2):
                load_dense(G_WO2 + i, w_out2[:, :, i * 512:(i + 1) * 512])
            sp.wait_ge(s_fin, 48)
            sp.dma_start(pre2, a["ffn2_pre_g_2"].to_broadcast([P, D])).then_inc(in_["ff2g"], 16)
            sp.dma_start(post2, a["ffn2_post_g_2"].to_broadcast([P, D])).then_inc(in_["ff2g"], 16)
            gated_stream("ff2", *ff_stream(a["ffn2_w_gu_2"][0], a["ffn2_w_down_2"][0]))
            sp.wait_ge(x_ready, 6)
            sp.dma_start(out.rearrange("o (b p) n -> p (o b) n", p=P), x[:, :, :]).then_inc(s_out, 16)
            sp.wait_ge(s_out, 16)

        @block.gpsimd
        def _(pool):
            pool.memset(ones[:, :], 1.0).then_inc(set_up, 1)
            pool.wait_ge(set_up, 1)
            pool.memset(zeros[:, :], 0.0).then_inc(set_up, 1)
            pool.wait_ge(set_up, 2)
            pool.memset(relb_in[32:33, :], 1.0).then_inc(set_up, 1)
            pool.wait_ge(set_up, 3)
            pool.memset(rpb_pad, 0.0).then_inc(chain_p, 1)
            pool.wait_ge(chain_p, 1)
            pool.dma_start(rpb_pad.rearrange("h (r c) -> h r c", r=7)[:, :, 48:79], a["na_rpb_2"][0][:, 4:11, :])\
                .then_inc(in_["rpb"], 16)
            pool.wait_ge(in_["rpb"], 16)
            pool.dma_start(n_dram.rearrange("q h x -> h q x"), rpb_pad.unsqueeze(1).to_broadcast([NH, 64, NR]))\
                .then_inc(in_["nw"], 16)
            pool.wait_ge(in_["nw"], 16)
            pool.wait_ge(tb_sb, 1)
            pool.dma_start(t_dram.rearrange("q h x -> h q x"), t_bias.unsqueeze(1).to_broadcast([NH, P, BX]))\
                .then_inc(in_["tw"], 16)
            pool.wait_ge(in_["tw"], 16)
            pool.wait_ge(in_["nb"], 256)
            for b in range(TB):
                v = na_bias[b].rearrange("p h (r c) -> p (h r) c", r=4)
                m = con[:, C_NA:C_NA + 64].unsqueeze(1).to_broadcast([P, 4 * NH, 64])
                pool.tensor_tensor(v, v, m, ALU.add).then_inc(na_ready, 1)

        @block.scalar
        def _(act):
            chain = [0]

            def link(ins):
                chain[0] += 1
                ins.then_inc(chain_a, 1)
                act.wait_ge(chain_a, chain[0])

            act.dma_start(c_col, a["c"].rearrange("o (p c) -> p (o c)", c=DC)).then_inc(in_["c"], 16)
            act.dma_start(con[:, :], a["con"]).then_inc(in_["con"], 16)
            act.dma_start(x[:, :, :], a["x"].rearrange("o (b p) n -> p (o b) n", p=P)).then_inc(in_["x"], 16)
            act.dma_start(b_ada_row[0:1, :], a["b_ada"]).then_inc(in_["bada"], 16)
            act.dma_start(relb_in[0:32, :], a["rel_bias_t"]).then_inc(in_["relb"], 16)
            act.dma_start(bucket_in, a["buckets"]).then_inc(in_["bucket"], 16)
            act.dma_start(g1_in, a["norm1_g"].to_broadcast([P, D])).then_inc(in_["g1"], 16)
            act.dma_start(g2_in, a["norm2_g"].to_broadcast([P, D])).then_inc(in_["g2"], 16)

            def split_hi(g, u, gated_tile=False, it=None, cols=UNIT):
                act.wait_ge(landed_g[g % 2], at(32 * (g // 2 + 1), it, 32))
                if g:
                    act.wait_ge(used_g, at(2 * g + u - 1, it, 4))
                if gated_tile:
                    dst = g_hi[:, u, :].rearrange("p (c g n) -> p c g n", c=4, g=2)
                    act.activation(dst, raw_gated(g, u), ACT.Copy).then_inc(hi_g, 1)
                else:
                    act.activation(g_hi[:, u, 0:cols], raw_dense(g, u)[:, 0:cols], ACT.Copy).then_inc(hi_g, 1)

            def transposed(k):
                for q in range(4):
                    act.wait_ge(xt_ps, 4 * k + q + 1)
                    act.activation(xt_hi[:, 2 * q:2 * q + 2, :].rearrange("p c t -> p (c t)"), bank(q), ACT.Copy)\
                        .then_inc(xt_hi_s, 1)

            def squares(k, srcs, after, count, scratch):
                for i, src in enumerate(srcs):
                    act.wait_ge(after, count)
                    ins = act.activation(scratch(i), src, ACT.Square, accum_out=st[:, 16 + i:17 + i])
                ins.then_inc(ss_a, 1)
                act.wait_ge(ms_v, k + 1)
                act.activation(st[:, 24:24 + len(srcs)], st[:, 20:20 + len(srcs)], ACT.Sqrt).then_inc(sd_a, 1)

            def gated_phase(name):
                g0, d0, n = FFN_PHASES[name]

                def hi_down(d, it=None):
                    act.wait_ge(landed_d[d % 2], at(16 * (d // 2 + 1), it, 16))
                    act.wait_ge(used_d, at(d + 1, it, 2))
                    act.activation(d_hi[:, :], raw_d[:, d % 2, :], ACT.Copy).then_inc(hi_d, 1)

                def hi_gated(d, it=None):
                    act.wait_ge(tr_done, at(d + 1, it, 2))
                    act.activation(at_hi[:, :, :].rearrange("p c t -> p (c t)"), bank(6), ACT.Copy)\
                        .then_inc(at_hi_s, 1)

                def silus(g, d, it=None):
                    act.wait_ge(used_g, at(2 * g + 2, it, 4))
                    for b in range(TB):
                        if d:
                            act.wait_ge(gated, at(2 * d - 1 + b, it, 4))
                        act.activation(silu[:, b, :], bank(4 + b)[:, 0:FF], ACT.Silu).then_inc(silu_done, 1)

                def body(s, it=None):
                    hi_down(d0 + s, it)
                    hi_gated(d0 + s, it)
                    if s + 2 < n:
                        split_hi(g0 + s + 2, 0, True, it)
                    if s + 1 < n:
                        silus(g0 + s + 1, d0 + s + 1, it)
                    if s + 2 < n:
                        split_hi(g0 + s + 2, 1, True, it)

                split_hi(g0, 0, True)
                split_hi(g0, 1, True)
                split_hi(g0 + 1, 0, True)
                silus(g0, d0)
                split_hi(g0 + 1, 1, True)
                with act.Fori(0, (n - 3) // 2) as it:
                    for j in range(2):
                        body(j, it)
                for s in range(n - 3, n):
                    body(s)

            def softmaxes(k, kw):
                def copy_pt(n):
                    i = n - 16 * k
                    act.wait_ge(s_pt, n + 1)
                    if n >= 2:
                        act.wait_ge(s_o, n - 1)
                    w = kw(i % 2)
                    act.activation(pT_sb[n % 2].rearrange("p c q -> p (c q)")[:, 0:w], bank(4 + n % 2)[:, 0:w],
                                   ACT.Copy).then_inc(s_ptc, 1)

                for i in range(16):
                    n = 16 * k + i
                    w = kw(i % 2)
                    act.wait_ge(s_max, n + 1)
                    if n >= 2:
                        act.wait_ge(s_fin, n - 1)
                    act.activation(s_buf[n % 2][:, 0:w], s_buf[n % 2][:, 0:w], ACT.Exp,
                                   bias=st[:, 32 + n % 2:33 + n % 2], accum_out=st[:, 36 + n % 2:37 + n % 2])\
                        .then_inc(s_exp, 1)
                    if i:
                        copy_pt(n - 1)
                copy_pt(16 * k + 15)

            act.wait_ge(in_["c"], 16)
            act.activation(c_sil, c_col, ACT.Silu).then_inc(c_silu, 1)
            mods = (shift1, gain1, gate1, shift2, gain2, gate2)
            squares(0, [x[:, b, :] for b in range(TB)], in_["x"], 16, lambda i: h[:, i, :])

            def ada_out(t):
                act.wait_ge(used_g, 2 * t + 2)
                act.activation(mods[t // 2][:, (t % 2) * 512:(t % 2 + 1) * 512], bank(4 + t % 4), ACT.Copy)\
                    .then_inc(ada_ev, 1)

            for t in range(N_ADA):
                split_hi(G_ADA + t, 0)
                split_hi(G_ADA + t, 1)
                if t:
                    ada_out(t - 1)
            split_hi(G_WIN, 0)
            ada_out(N_ADA - 1)
            split_hi(G_WIN, 1)
            transposed(0)

            def win_out(j):
                act.wait_ge(used_g, 2 * (G_WIN + j) + 2)
                b0 = 4 + 2 * (j % 2)
                if j in (0, 1, 3, 4):
                    dst = (qT, kT)[j % 3][j // 3][:, 0:2, :].rearrange("p m t -> p (m t)")
                    act.activation(dst, bank(b0), ACT.Copy, scale=0.125 if j % 3 == 0 else 1.0).then_inc(ev_a, 1)
                elif j in (2, 5):
                    act.wait_ge(h_ready, 1)
                    act.activation(v_tok[:, 0, (j // 3) * 512:(j // 3 + 1) * 512], bank(b0), ACT.Copy)\
                        .then_inc(ev_a, 1)
                else:
                    for b in range(TB):
                        act.activation(sig[:, b, (j - 6) * 512:(j - 5) * 512], bank(b0 + b), ACT.Sigmoid)\
                            .then_inc(ev_a, 1)

            for j in range(N_WIN):
                if j:
                    split_hi(G_WIN + j, 0)
                    split_hi(G_WIN + j, 1)
                    win_out(j - 1)
            win_out(N_WIN - 1)

            for half in range(2):
                for i in range(4):
                    act.wait_ge(sb_z, 4 * half + i + 1)
                    act.activation(z_sb[:, i * 384:(i + 1) * 384], bank(i)[:, 0:384], ACT.Copy).then_inc(sb_zc, 1)
                act.wait_ge(sb_ab, half + 1)
                link(act.activation(l_sb, l_sb, ACT.Exp))
                act.activation(l_sb, l_sb, ACT.Ln, bias=1.0).then_inc(sb_ln, 1)
                act.wait_ge(sb_t, half + 1)
                act.activation(p_sb, p_sb, ACT.Exp).then_inc(sb_a, 1)
                for i in range(2):
                    act.wait_ge(sb_o, 2 * half + i + 1)
                    act.activation(xt_hi[:, 2 * half + i, :], bank(i)[:, 0:T], ACT.Copy).then_inc(sb_oh, 1)
            split_hi(G_WB, 0)
            split_hi(G_WB, 1)
            softmaxes(0, lambda b: P * (b + 1))

            def heads_t(k, base, count):
                for q in range(count):
                    act.wait_ge(ot_ps, k + q + 1)
                    act.activation(xt_hi[:, base + 2 * q:base + 2 * q + 2, :].rearrange("p c t -> p (c t)"),
                                   bank(q), ACT.Copy).then_inc(ot_hi, 1)

            heads_t(0, 4, 2)
            split_hi(G_WB + 1, 0)
            split_hi(G_WB + 1, 1)
            split_hi(G_WO, 0)
            split_hi(G_WO, 1)
            transposed(1)
            split_hi(G_WO + 1, 0)
            split_hi(G_WO + 1, 1)
            squares(1, [x[:, b, :] for b in range(TB)], x_ready, 1, lambda i: h[:, i, :])
            transposed(2)
            act.wait_ge(rt_ps, 1)
            act.activation(rt[:, 0:2 * E], bank(7)[:, 0:2 * E], ACT.Sigmoid).then_inc(rt_sc, 1)
            gated_phase("moe")

            squares(2, [x[:, b, :] for b in range(TB)], x_ready, 2, lambda i: h[:, i, :])
            squares(3, [x[:, b, :] for b in range(TB)], x_ready, 3, lambda i: h[:, i, :])
            transposed(3)
            gated_phase("ff1")
            squares(4, [ps[b][:, :, :].rearrange("p a n -> p (a n)") for b in range(TB)], used_d, D_FF1 + N_FF + 1,
                    lambda i: h[:, i, :])
            squares(5, [x[:, b, :] for b in range(TB)], x_ready, 4, lambda i: h[:, i, :])
            transposed(4)

            def win2_out(j):
                act.wait_ge(used_g, 2 * (G_WIN2 + j) + 2)
                b0 = 4 + 2 * (j % 2)
                if j < 2:
                    dst = (qT2, kT2)[j][:, 0:2, :].rearrange("p m t -> p (m t)")
                    act.activation(dst, bank(b0), ACT.Copy, scale=0.125 if j == 0 else 1.0).then_inc(ev_a, 1)
                elif j == 2:
                    act.activation(v2[:, 0, :], bank(b0), ACT.Copy).then_inc(ev_a, 1)
                else:
                    act.activation(small[:, 0, :], bank(b0)[:, 0:SMALL], ACT.Copy).then_inc(ev_a, 1)

            for j in range(4):
                cols = UNIT if j < 3 else 4 * SMALL
                split_hi(G_WIN2 + j, 0, cols=cols)
                split_hi(G_WIN2 + j, 1, cols=cols)
                if j:
                    win2_out(j - 1)
            win2_out(3)
            srcs = [small[:, b, lo:hi] for b in range(TB) for lo, hi in ((0, 256), (256, 384))]
            act.wait_ge(ev_a, EV_A[G_WIN2 + 3])
            squares(6, srcs, ev_v, EV_V[G_WIN2 + 3], lambda i: att[:, i * 256:i * 256 + srcs[i].shape[-1]])
            softmaxes(1, lambda b: T)
            split_hi(G_MLA, 0, cols=2 * QW)
            split_hi(G_MLA, 1, cols=KVW)
            for q in range(2):
                act.wait_ge(cn_ps, q + 1)
                w = 512 if q == 0 else 256
                act.activation(xt_hi[:, 2 * q:2 * q + w // T, :].rearrange("p c t -> p (c t)"), bank(q)[:, 0:w],
                               ACT.Copy).then_inc(cn_hi, 1)
            act.wait_ge(used_g, 2 * G_MLA + 2)
            for i in range(4):
                act.activation(q_tok[:, i // 2, (i % 2) * 384:(i % 2 + 1) * 384], bank(i)[:, 0:384], ACT.Copy)\
                    .then_inc(ev_a, 1)
            for q in range(0, 8, 2):
                act.wait_ge(mt_ps, q + 1)
                dst = (qTm, kTm)[q // 4][0:96, (q % 4) * 2:(q % 4) * 2 + 2, :].rearrange("p h t -> p (h t)")
                act.activation(dst, bank(q % 4)[0:96, :], ACT.Copy).then_inc(mt_ev_a, 1)
            softmaxes(2, lambda b: T)
            srcs2 = [h[:, b, i * 512:(i + 1) * 512] for b in range(TB) for i in range(2)]
            squares(7, srcs2, s_fin, 48, lambda i: att[:, i * 512:(i + 1) * 512])
            split_hi(G_WO2, 0)
            split_hi(G_WO2, 1)
            transposed(5)
            split_hi(G_WO2 + 1, 0)
            split_hi(G_WO2 + 1, 1)
            squares(8, [ps[2 + b][:, :, :].rearrange("p a n -> p (a n)") for b in range(TB)], used_g,
                    2 * (G_WO2 + 1) + 2, lambda i: h[:, i, :])
            squares(9, [x[:, b, :] for b in range(TB)], x_ready, 5, lambda i: h[:, i, :])
            transposed(6)
            gated_phase("ff2")
            squares(10, [ps[b][:, :, :].rearrange("p a n -> p (a n)") for b in range(TB)], used_d, D_FF2 + N_FF + 1,
                    lambda i: h[:, i, :])

        @block.vector
        def _(dve):
            chain = [0]

            def link(ins):
                chain[0] += 1
                ins.then_inc(chain_v, 1)
                dve.wait_ge(chain_v, chain[0])

            def split_lo(g, u, gated_tile=False, it=None, cols=UNIT):
                dve.wait_ge(hi_g, at(2 * g + u + 1, it, 4))
                if gated_tile:
                    hi, lo = (t[:, u, :].rearrange("p (c g n) -> p c g n", c=4, g=2) for t in (g_hi, g_lo))
                    raw = raw_gated(g, u)
                else:
                    hi, lo, raw = g_hi[:, u, 0:cols], g_lo[:, u, 0:cols], raw_dense(g, u)[:, 0:cols]
                dve.tensor_tensor(lo, raw, hi.bitcast(F32), ALU.subtract).then_inc(lo_g, 1)

            def transposed(k):
                for q in range(4):
                    dve.wait_ge(xt_hi_s, 4 * k + q + 1)
                    hi, lo = (t[:, 2 * q:2 * q + 2, :].rearrange("p c t -> p (c t)") for t in (xt_hi, xt_lo))
                    dve.tensor_tensor(lo, bank(q), hi.bitcast(F32), ALU.subtract).then_inc(xt_lo_s, 1)

            def roots(k, widths):
                n = len(widths)
                dve.wait_ge(ss_a, k + 1)
                for i, w in enumerate(widths):
                    ins = dve.tensor_scalar(st[:, 20 + i:21 + i], st[:, 16 + i:17 + i], 1.0 / w, EPS,
                                            ALU.mult, ALU.add)
                ins.then_inc(ms_v, 1)
                dve.wait_ge(sd_a, k + 1)
                link(dve.reciprocal(st[:, 28:28 + n], st[:, 24:24 + n]))

            def scaled(dst, src, i, gain):
                return dve.scalar_tensor_tensor(out=dst, in0=src, scalar=st[:, 28 + i:29 + i], in1=gain,
                                                op0=ALU.mult, op1=ALU.mult)

            def gated_phase(name, weight=None):
                g0, d0, n = FFN_PHASES[name]

                def lo_down(d, it=None):
                    dve.wait_ge(hi_d, at(d + 1, it, 2))
                    dve.tensor_tensor(d_lo[:, :], raw_d[:, d % 2, :], d_hi[:, :].bitcast(F32), ALU.subtract)\
                        .then_inc(lo_d, 1)

                def lo_gated(d, it=None):
                    dve.wait_ge(at_hi_s, at(d + 1, it, 2))
                    hi, lo = (t[:, :, :].rearrange("p c t -> p (c t)") for t in (at_hi, at_lo))
                    dve.tensor_tensor(lo, bank(6), hi.bitcast(F32), ALU.subtract).then_inc(at_lo_s, 1)

                def gate(s, it=None):
                    d = d0 + s
                    for b in range(TB):
                        w = 1.0
                        if weight is not None:
                            w = weight[:, b, s:s + 1] if it is None else weight[:, b, bass.ds(it * 2 + s, 1)]
                        dve.wait_ge(silu_done, at(2 * d + b + 1, it, 4))
                        dve.scalar_tensor_tensor(out=a_sb[:, b, :], in0=silu[:, b, :], scalar=w,
                                                 in1=bank(4 + b)[:, FF:2 * FF], op0=ALU.mult, op1=ALU.mult)\
                            .then_inc(gated, 1)

                def body(s, it=None):
                    lo_down(d0 + s, it)
                    lo_gated(d0 + s, it)
                    if s + 2 < n:
                        split_lo(g0 + s + 2, 0, True, it)
                    if s + 1 < n:
                        gate(s + 1, it)
                    if s + 2 < n:
                        split_lo(g0 + s + 2, 1, True, it)

                split_lo(g0, 0, True)
                split_lo(g0, 1, True)
                split_lo(g0 + 1, 0, True)
                gate(0)
                split_lo(g0 + 1, 1, True)
                with dve.Fori(0, (n - 3) // 2) as it:
                    for j in range(2):
                        body(j, it)
                for s in range(n - 3, n):
                    body(s)

            def softmaxes(k, kw, bias, scale, dest):
                def finish(n):
                    i = n - 16 * k
                    dve.wait_ge(s_o, n + 1)
                    link(dve.reciprocal(st[:, 40 + n % 2:41 + n % 2], st[:, 36 + n % 2:37 + n % 2]))
                    dve.tensor_scalar(dest(i // 2, i % 2), bank(6 + n % 2)[:, 0:HD], st[:, 40 + n % 2:41 + n % 2],
                                      None, ALU.mult).then_inc(s_fin, 1)

                for i in range(16):
                    n = 16 * k + i
                    w = kw(i % 2)
                    dve.wait_ge(s_ps, n + 1)
                    if n >= 2:
                        dve.wait_ge(s_pt, n - 1)
                    s = s_buf[n % 2][:, 0:w]
                    if bias is None:
                        link(dve.tensor_scalar(s, bank(2 + n % 2)[:, 0:w], scale, None, ALU.mult))
                    else:
                        link(dve.scalar_tensor_tensor(out=s, in0=bank(2 + n % 2)[:, 0:w], scalar=scale,
                                                      in1=bias(i // 2, i % 2), op0=ALU.mult, op1=ALU.add))
                    dve.reduce_max(st[:, 32 + n % 2:33 + n % 2], s, AX, negate=True).then_inc(s_max, 1)
                    if i >= 2:
                        finish(n - 2)
                finish(16 * k + 14)
                finish(16 * k + 15)

            dve.wait_ge(c_silu, 1)
            c_all = c_sil.unsqueeze(2).to_broadcast([P, DC, P])
            link(dve.tensor_copy(xt_hi[:, :, 0:P], c_all))
            dve.tensor_tensor(xt_lo[:, :, 0:P], c_all, xt_hi[:, :, 0:P].bitcast(F32), ALU.subtract).then_inc(c_bc, 1)
            dve.wait_ge(tb_ps, 1)
            dve.tensor_copy(t_bias, bank(0)[0:NH, 0:BX]).then_inc(tb_sb, 1)
            roots(0, [D, D])
            for t in range(N_ADA):
                split_lo(G_ADA + t, 0)
                split_lo(G_ADA + t, 1)
                if t == 5:
                    dve.wait_ge(ada_ev, 4)
                    dve.wait_ge(in_["g1"], 16)
                    link(dve.scalar_tensor_tensor(out=gain1, in0=gain1, scalar=1.0, in1=g1_in,
                                                  op0=ALU.add, op1=ALU.mult))
                    for b in range(TB):
                        link(scaled(h[:, b, :], x[:, b, :], b, gain1))
                    for b in range(TB):
                        ins = dve.tensor_tensor(h[:, b, :], h[:, b, :], shift1, ALU.add)
                    ins.then_inc(h_ready, 1)
            dve.wait_ge(ada_ev, 10)
            dve.wait_ge(in_["g2"], 16)
            dve.scalar_tensor_tensor(out=gain2, in0=gain2, scalar=1.0, in1=g2_in, op0=ALU.add, op1=ALU.mult)
            split_lo(G_WIN, 0)
            split_lo(G_WIN, 1)
            transposed(0)

            def win_out(j):
                dve.wait_ge(used_g, 2 * (G_WIN + j) + 2)
                src = bank(5 + 2 * (j % 2))
                if j in (0, 1, 3, 4):
                    dst = (qT, kT)[j % 3][j // 3][:, 2:4, :].rearrange("p m t -> p (m t)")
                    dve.tensor_scalar(dst, src, 0.125 if j % 3 == 0 else 1.0, None, ALU.mult).then_inc(ev_v, 1)
                else:
                    dve.tensor_copy(v_tok[:, 1, (j // 3) * 512:(j // 3 + 1) * 512], src).then_inc(ev_v, 1)

            for j in range(N_WIN):
                if j:
                    split_lo(G_WIN + j, 0)
                    split_lo(G_WIN + j, 1)
                    if j <= 6:
                        win_out(j - 1)

            dve.wait_ge(in_["nw"], 16)
            dve.wait_ge(in_["tw"], 16)
            for half in range(2):
                dve.wait_ge(sb_zc, 4 * half + 4)
                dve.scalar_tensor_tensor(out=l_sb, in0=z_sb, scalar=-1.0, in1=z_sb, op0=ALU.mult, op1=ALU.min)\
                    .then_inc(sb_ab, 1)
                dve.wait_ge(sb_ln, half + 1)
                link(dve.scalar_tensor_tensor(out=l_sb, in0=z_sb, scalar=0.0, in1=l_sb, op0=ALU.max, op1=ALU.add))
                for c in (0, 2):
                    d3 = l_sb.rearrange("p (i c q) -> p i c q", i=4, c=3)[:, :, c, :]
                    ins = dve.tensor_tensor(d3, d3, con[:, C_MASK:C_MASK + P].unsqueeze(1).to_broadcast([P, 4, P]),
                                            ALU.mult)
                ins.then_inc(sb_r, 1)
                for i in range(4):
                    dve.wait_ge(sb_i, 4 * half + i + 1)
                    ins = dve.scalar_tensor_tensor(out=p_sb[:, i * 384:(i + 1) * 384], in0=bank(4 + i)[:, 0:384],
                                                   scalar=-1.0, in1=z_sb[:, i * 384:(i + 1) * 384],
                                                   op0=ALU.mult, op1=ALU.add)
                link(ins)
                for c in (0, 2):
                    d3 = p_sb.rearrange("p (i c q) -> p i c q", i=4, c=3)[:, :, c, :]
                    ins = dve.tensor_tensor(d3, d3, con[:, C_MIN:C_MIN + P].unsqueeze(1).to_broadcast([P, 4, P]),
                                            ALU.min)
                ins.then_inc(sb_t, 1)
                for i in range(2):
                    dve.wait_ge(sb_oh, 2 * half + i + 1)
                    dve.tensor_tensor(xt_lo[:, 2 * half + i, :], bank(i)[:, 0:T],
                                      xt_hi[:, 2 * half + i, :].bitcast(F32), ALU.subtract).then_inc(sb_ol, 1)
            split_lo(G_WB, 0)
            split_lo(G_WB, 1)

            dve.wait_ge(in_["tb"], 16)
            softmaxes(0, lambda b: P * (b + 1), lambda hd, b: mb_bias[:, hd, P * (1 - b):T], 1.0,
                      lambda hd, b: o_mb[:, b, hd * HD:(hd + 1) * HD])
            for q in range(2):
                dve.wait_ge(ot_hi, q + 1)
                hi, lo = (t[:, 4 + 2 * q:6 + 2 * q, :].rearrange("p c t -> p (c t)") for t in (xt_hi, xt_lo))
                dve.tensor_tensor(lo, bank(q), hi.bitcast(F32), ALU.subtract).then_inc(ot_lo, 1)
            split_lo(G_WB + 1, 0)
            split_lo(G_WB + 1, 1)
            split_lo(G_WO, 0)
            dve.wait_ge(used_g, 2 * (G_WB + 1) + 2)
            for b in range(TB):
                for n in range(2):
                    i = 2 * b + n
                    hv = h[:, b, n * 512:(n + 1) * 512]
                    tmp = att[:, (i % 2) * 512:(i % 2 + 1) * 512]
                    dve.tensor_tensor(hv, bank(i), sig[:, b, n * 512:(n + 1) * 512], ALU.mult)
                    link(dve.tensor_tensor(tmp, bank(4 + i), sig[:, b, D + n * 512:D + (n + 1) * 512], ALU.mult))
                    ins = dve.tensor_tensor(hv, hv, tmp, ALU.add)
            ins.then_inc(h_ready, 1)
            split_lo(G_WO, 1)
            transposed(1)
            split_lo(G_WO + 1, 0)
            split_lo(G_WO + 1, 1)

            def add_gated(gate, banks, sem_, count):
                dve.wait_ge(sem_, count)
                for b in range(TB):
                    for n in range(2):
                        hv = h[:, b, n * 512:(n + 1) * 512]
                        link(dve.tensor_tensor(hv, bank(banks + 2 * b + n), gate[:, n * 512:(n + 1) * 512], ALU.mult))
                        xv = x[:, b, n * 512:(n + 1) * 512]
                        ins = dve.tensor_tensor(xv, xv, hv, ALU.add)
                ins.then_inc(x_ready, 1)

            add_gated(gate1, 4, used_g, 2 * (G_WO + 1) + 2)
            roots(1, [D, D])
            for b in range(TB):
                link(scaled(h[:, b, :], x[:, b, :], b, gain2))
            for b in range(TB):
                ins = dve.tensor_tensor(h[:, b, :], h[:, b, :], shift2, ALU.add)
            ins.then_inc(h_ready, 1)
            transposed(2)

            dve.wait_ge(rt_sc, 1)
            dve.wait_ge(in_["rbias"], 16)
            link(dve.memset(wts[:, :, E:E + 1], 1.0))
            for b in range(TB):
                sc = rt[:, b * E:(b + 1) * E]
                ch, cm, sel = (rt[:, i * E:(i + 1) * E] for i in (2, 3, 4))
                top2 = rt[:, 5 * E:6 * E]
                gs, m8, gr = rt[:, 6 * E:6 * E + 12], rt[:, 6 * E + 16:6 * E + 24], rt[:, 6 * E + 32:6 * E + 44]
                pen, tot = rt[:, 7 * E:7 * E + 8], rt[:, 7 * E + 8:7 * E + 10]
                link(dve.tensor_tensor(ch, sc, rbias, ALU.add))
                for i in range(NGRP):
                    ins = dve.max(top2[:, 8 * i:8 * i + 8], ch[:, 8 * i:8 * i + 8])
                link(ins)
                t3 = top2.rearrange("p (g k) -> p g k", g=NGRP)
                dve.tensor_tensor(gs[:, 0:8].unsqueeze(2), t3[:, :, 0:1], t3[:, :, 1:2], ALU.add)
                link(dve.memset(gs[:, 8:12], 3e38))
                link(dve.max(m8, gs))
                link(dve.match_replace(gr, m8, gs, -3e38))
                link(dve.tensor_scalar(pen, gr[:, 0:8], -2e38, BIG, ALU.is_lt, ALU.mult))
                link(dve.tensor_scalar(pen, pen, BIG, None, ALU.subtract))
                link(dve.tensor_tensor(cm.rearrange("p (g k) -> p g k", g=NGRP),
                                       ch.rearrange("p (g k) -> p g k", g=NGRP),
                                       pen.unsqueeze(2).to_broadcast([P, NGRP, 8]), ALU.add))
                link(dve.max(m8, cm))
                link(dve.match_replace(sel, m8, cm, -3e38))
                link(dve.tensor_scalar(sel, sel, -2e38, None, ALU.is_lt))
                link(dve.tensor_tensor(sel, sel, sc, ALU.mult))
                link(dve.reduce_sum(tot[:, 0:1], sel, AX))
                link(dve.reciprocal(tot[:, 1:2], tot[:, 0:1]))
                link(dve.tensor_scalar(wts[:, b, 0:E], sel, tot[:, 1:2], 2.5, ALU.mult, ALU.mult))
            gated_phase("moe", wts)

            add_gated(gate2, 0, used_d, D_MOE + N_MOE + 1)
            dve.wait_ge(in_["gains"], 80)
            roots(2, [D, D])
            for b in range(TB):
                ins = scaled(x[:, b, :], x[:, b, :], b, final_g)
            ins.then_inc(x_ready, 1)

            def normed(k, gain):
                roots(k, [D, D])
                for b in range(TB):
                    ins = scaled(h[:, b, :], x[:, b, :], b, gain)
                ins.then_inc(h_ready, 1)

            def add_normed(k, base, gain, factor):
                roots(k, [D, D])
                for b in range(TB):
                    src = ps[base + b][:, :, :].rearrange("p a n -> p (a n)")
                    link(scaled(h[:, b, :], src, b, gain))
                    ins = dve.scalar_tensor_tensor(out=x[:, b, :], in0=h[:, b, :], scalar=factor, in1=x[:, b, :],
                                                   op0=ALU.mult, op1=ALU.add)
                ins.then_inc(x_ready, 1)

            normed(3, pre1)
            transposed(3)
            gated_phase("ff1")
            add_normed(4, 0, post1, 0.5)
            normed(5, mixpre)
            transposed(4)

            def win2_out(j):
                dve.wait_ge(used_g, 2 * (G_WIN2 + j) + 2)
                src = bank(5 + 2 * (j % 2))
                if j < 2:
                    dst = (qT2, kT2)[j][:, 2:4, :].rearrange("p m t -> p (m t)")
                    dve.tensor_scalar(dst, src, 0.125 if j == 0 else 1.0, None, ALU.mult).then_inc(ev_v, 1)
                elif j == 2:
                    dve.tensor_copy(v2[:, 1, :], src).then_inc(ev_v, 1)
                else:
                    dve.tensor_copy(small[:, 1, :], src[:, 0:SMALL]).then_inc(ev_v, 1)

            for j in range(4):
                cols = UNIT if j < 3 else 4 * SMALL
                split_lo(G_WIN2 + j, 0, cols=cols)
                split_lo(G_WIN2 + j, 1, cols=cols)
                if j:
                    win2_out(j - 1)
            win2_out(3)
            dve.wait_ge(in_["outg"], 64)
            roots(6, [256, 128, 256, 128])
            for b in range(TB):
                scaled(small[:, b, 0:256], small[:, b, 0:256], 2 * b, qn_g)
                ins = scaled(small[:, b, 256:384], small[:, b, 256:384], 2 * b + 1, kvn_g)
            ins.then_inc(cn_ready, 1)
            dve.wait_ge(na_ready, 2)
            softmaxes(1, lambda b: T, lambda hd, b: na_bias[b][:, hd, :], 1.0,
                      lambda hd, b: h[:, b, hd * HD:(hd + 1) * HD])
            split_lo(G_MLA, 0, cols=2 * QW)
            split_lo(G_MLA, 1, cols=KVW)
            for q in range(2):
                dve.wait_ge(cn_hi, q + 1)
                w = 512 if q == 0 else 256
                hi, lo = (t[:, 2 * q:2 * q + w // T, :].rearrange("p c t -> p (c t)") for t in (xt_hi, xt_lo))
                dve.tensor_tensor(lo, bank(q)[:, 0:w], hi.bitcast(F32), ALU.subtract).then_inc(cn_lo, 1)
            dve.wait_ge(used_g, 2 * G_MLA + 2)
            for i in range(4):
                dve.tensor_copy(kv_tok[:, i // 2, (i % 2) * 512:(i % 2 + 1) * 512], bank(4 + i)).then_inc(ev_v, 1)
            dve.wait_ge(ev_a, EV_A[G_MLA])
            dve.wait_ge(ev_v, EV_V[G_MLA])
            for b in range(TB):
                q3 = q_tok[:, b, :].rearrange("p (h n) -> p h n", h=NH)
                k3 = k_full[:, b, :].rearrange("p (h n) -> p h n", h=NH)
                kv3 = kv_tok[:, b, :].rearrange("p (h n) -> p h n", h=NH)
                cos, sin = (con[:, c + 16 * b:c + 16 * b + 16] for c in (C_COS, C_SIN))

                def wide(t):
                    return t.unsqueeze(1).to_broadcast([P, NH, 16])

                tmp = [rope_t[:, i, b, :].rearrange("p (h n) -> p h n", h=NH) for i in range(4)]
                q1, q2 = q3[:, :, 64:80], q3[:, :, 80:96]
                dve.tensor_tensor(tmp[0], q1, wide(cos), ALU.mult)
                dve.tensor_tensor(tmp[1], q2, wide(sin), ALU.mult)
                dve.tensor_tensor(tmp[2], q2, wide(cos), ALU.mult)
                link(dve.tensor_tensor(tmp[3], q1, wide(sin), ALU.mult))
                dve.tensor_tensor(q1, tmp[0], tmp[1], ALU.subtract)
                link(dve.tensor_tensor(q2, tmp[2], tmp[3], ALU.add))
                dve.tensor_copy(k3[:, :, 0:64], kv3[:, :, 0:64])
                k1, k2 = small[:, b, 384:400], small[:, b, 400:416]
                t16 = [rope_t[:, i, b, 0:16] for i in range(4)]
                dve.tensor_tensor(t16[0], k1, cos, ALU.mult)
                dve.tensor_tensor(t16[1], k2, sin, ALU.mult)
                dve.tensor_tensor(t16[2], k2, cos, ALU.mult)
                link(dve.tensor_tensor(t16[3], k1, sin, ALU.mult))
                dve.tensor_tensor(k3[:, :, 64:80], wide(t16[0]), wide(t16[1]), ALU.subtract)
                dve.tensor_tensor(k3[:, :, 80:96], wide(t16[2]), wide(t16[3]), ALU.add).then_inc(roped, 1)
            for q in range(1, 8, 2):
                dve.wait_ge(mt_ps, q + 1)
                dst = (qTm, kTm)[q // 4][0:96, (q % 4) * 2:(q % 4) * 2 + 2, :].rearrange("p h t -> p (h t)")
                dve.tensor_copy(dst, bank(q % 4)[0:96, :]).then_inc(mt_ev_v, 1)
            softmaxes(2, lambda b: T, None, 96.0 ** -0.5, lambda hd, b: h[:, b, 512 + hd * HD:512 + (hd + 1) * HD])
            roots(7, [512] * 4)
            for i in range(4):
                hv = h[:, i // 2, (i % 2) * 512:(i % 2 + 1) * 512]
                ins = scaled(hv, hv, i, outg[:, (i % 2) * 512:(i % 2 + 1) * 512])
            ins.then_inc(h_ready, 1)
            split_lo(G_WO2, 0)
            split_lo(G_WO2, 1)
            transposed(5)
            split_lo(G_WO2 + 1, 0)
            split_lo(G_WO2 + 1, 1)
            add_normed(8, 2, mixpost, 1.0)
            dve.wait_ge(in_["ff2g"], 32)
            normed(9, pre2)
            transposed(6)
            gated_phase("ff2")
            add_normed(10, 0, post2, 0.5)

        @block.tensor
        def _(pe):
            PASSES = ((0, 0), (0, 1), (1, 0))

            def transposes(k):
                pe.wait_ge(h_ready, k + 1)
                for q in range(4):
                    for c in (2 * q, 2 * q + 1):
                        for b in range(TB):
                            o = ((c % 2) * TB + b) * P
                            ins = pe.transpose(bank(q)[:, o:o + P], h[:, b, c:D:DC], ident)
                    ins.then_inc(xt_ps, 1)

            def rows(out_, b, cs, w, n, start, stop):
                last = None
                for i, c in enumerate(cs):
                    for k, (s, m) in enumerate(PASSES):
                        last = pe.matmul(out_, (xt_hi, xt_lo)[s][:, c, b * P:(b + 1) * P], w((g_hi, g_lo)[m], i),
                                         start=start and i == 0 and k == 0,
                                         stop=stop and i == len(cs) - 1 and k == 2, skip_group_check=True)
                return last

            def dense(g, banks, n=512):
                for u in range(2):
                    pe.wait_ge(lo_g, 2 * g + u + 1)
                    for b in range(TB):
                        last = rows(bank(banks[b])[:, 0:n], b, range(4 * u, 4 * u + 4),
                                    lambda t, i: t[:, u, i * n:(i + 1) * n], n, u == 0, u == 1)
                    last.then_inc(used_g, 1)

            def features(g, b0):
                for u in range(2):
                    pe.wait_ge(lo_g, 2 * g + u + 1)
                    for m in range(4):
                        for c in range(4):
                            for k, (s, w) in enumerate(PASSES):
                                last = pe.matmul(bank(b0 + m // 2)[:, (m % 2) * T:(m % 2 + 1) * T],
                                                 (g_hi, g_lo)[w][:, u, c * 512 + m * P:c * 512 + (m + 1) * P],
                                                 (xt_hi, xt_lo)[s][:, 4 * u + c, :],
                                                 start=u == 0 and c == 0 and k == 0 and m % 2 == 0,
                                                 stop=u == 1 and c == 3 and k == 2, skip_group_check=True)
                    last.then_inc(used_g, 1)

            def gated_phase(name):
                g0, d0, n = FFN_PHASES[name]

                def gate_up(s, u, it=None):
                    g, d = g0 + s, d0 + s
                    pe.wait_ge(lo_g, at(2 * g + u + 1, it, 4))
                    if u == 0 and d:
                        pe.wait_ge(gated, at(2 * d, it, 4))
                    for b in range(TB):
                        last = rows(bank(4 + b), b, range(4 * u, 4 * u + 4),
                                    lambda t, i: t[:, u, i * 512:(i + 1) * 512], 512, u == 0, u == 1)
                    last.then_inc(used_g, 1)

                def turn(s, it=None):
                    pe.wait_ge(gated, at(2 * (d0 + s) + 2, it, 4))
                    for c in range(2):
                        for b in range(TB):
                            o = (c * TB + b) * P
                            last = pe.transpose(bank(6)[:, o:o + P], a_sb[:, b, c:FF:2], ident)
                    last.then_inc(tr_done, 1)

                def down(s, it=None, stop=False):
                    pe.wait_ge(at_lo_s, at(d0 + s + 1, it, 2))
                    pe.wait_ge(lo_d, at(d0 + s + 1, it, 2))
                    for b in range(TB):
                        for m in range(2):
                            for c in range(2):
                                for k, (i, w) in enumerate(PASSES):
                                    last = pe.matmul(bank(2 * b + m), (at_hi, at_lo)[i][:, c, b * P:(b + 1) * P],
                                                     (d_hi, d_lo)[w][:, c * D + m * 512:c * D + (m + 1) * 512],
                                                     start=False, stop=stop and c == 1 and k == 2,
                                                     skip_group_check=True)
                    last.then_inc(used_d, 1)

                def body(s, it=None):
                    if s + 1 < n:
                        gate_up(s + 1, 0, it)
                    turn(s, it)
                    if s + 1 < n:
                        gate_up(s + 1, 1, it)
                    down(s, it, stop=s == n - 1)

                for i in range(4):
                    last = pe.matmul(bank(i), zeros[:, 0:P], zeros[:, :], start=True, stop=False,
                                     skip_group_check=True)
                if d0 == 0:
                    last.then_inc(used_d, 1)
                gate_up(0, 0)
                gate_up(0, 1)
                with pe.Fori(0, (n - 3) // 2) as it:
                    for j in range(2):
                        body(j, it)
                for s in range(n - 3, n):
                    body(s)

            def softmaxes(k, kw, scores, values):
                def score(n):
                    i = n - 16 * k
                    if i >= 2:
                        pe.wait_ge(s_max, n - 1)
                    lhsT, rhs = scores(i // 2, i % 2)
                    pe.matmul(bank(2 + n % 2)[:, 0:kw(i % 2)], lhsT, rhs, start=True, stop=True).then_inc(s_ps, 1)

                def turn(n):
                    i = n - 16 * k
                    pe.wait_ge(s_exp, n + 1)
                    if i >= 2:
                        pe.wait_ge(s_ptc, n - 1)
                    for c in range(kw(i % 2) // P):
                        last = pe.transpose(bank(4 + n % 2)[:, c * P:(c + 1) * P], s_buf[n % 2][:, c * P:(c + 1) * P],
                                            ident)
                    last.then_inc(s_pt, 1)

                def output(n):
                    i = n - 16 * k
                    pe.wait_ge(s_ptc, n + 1)
                    if i >= 2:
                        pe.wait_ge(s_fin, n - 1)
                    cs = kw(i % 2) // P
                    for c in range(cs):
                        last = pe.matmul(bank(6 + n % 2)[:, 0:HD], pT_sb[n % 2][:, c, :], values(i // 2, c),
                                         start=c == 0, stop=c == cs - 1)
                    last.then_inc(s_o, 1)

                score(16 * k)
                for i in range(16):
                    if i < 15:
                        score(16 * k + i + 1)
                    turn(16 * k + i)
                    if i:
                        output(16 * k + i - 1)
                output(16 * k + 15)

            pe.wait_ge(in_["relb"], 16)
            pe.wait_ge(in_["bucket"], 16)
            pe.wait_ge(set_up, 3)
            pe.matmul(bank(0)[0:NH, 0:BX], relb_in, bucket_in, start=True, stop=True).then_inc(tb_ps, 1)
            pe.wait_ge(in_["bada"], 16)
            pe.wait_ge(c_bc, 1)
            for t in range(N_ADA):
                out_ = bank(4 + t % 4)
                if t >= 4:
                    pe.wait_ge(ada_ev, t - 3)
                pe.matmul(out_, ones[0:1, :], b_ada_row[0:1, t * 512:(t + 1) * 512], start=True, stop=False,
                          skip_group_check=True)
                for u in range(2):
                    pe.wait_ge(lo_g, 2 * t + u + 1)
                    last = rows(out_, 0, range(4 * u, 4 * u + 4), lambda w, i: w[:, u, i * 512:(i + 1) * 512],
                                512, False, u == 1)
                    last.then_inc(used_g, 1)

            pe.wait_ge(in_["con"], 16)
            pe.wait_ge(tb_sb, 1)
            transposes(0)
            pe.wait_ge(xt_lo_s, 4)
            pe.wait_ge(ada_ev, N_ADA)
            for j in range(N_WIN):
                b0 = 4 + 2 * (j % 2)
                if j >= 2:
                    pe.wait_ge(ev_a, EV_A[G_WIN + j - 2])
                    pe.wait_ge(ev_v, EV_V[G_WIN + j - 2])
                if j in (0, 1, 3, 4):
                    features(G_WIN + j, b0)
                else:
                    dense(G_WIN + j, (b0, b0 + 1))
            pe.wait_ge(ev_a, EV_A[G_WIN + N_WIN - 1])
            pe.wait_ge(ev_v, EV_V[G_WIN + N_WIN - 1])

            for half in range(2):
                if half:
                    pe.wait_ge(sb_ol, 2)
                for i in range(4):
                    hd = 4 * half + i
                    r, m = slice((hd % 2) * 64, (hd % 2) * 64 + 64), hd // 2
                    pe.matmul(bank(i)[:, 0:T], kT[0][r, m, 0:P], qT[0][r, m, :], start=True, stop=True)
                    pe.matmul(bank(i)[:, T:384], kT[0][r, m, P:T], qT[0][r, m, P:T], start=True, stop=True)\
                        .then_inc(sb_z, 1)
                pe.wait_ge(sb_r, half + 1)
                for i in range(4):
                    r0, r1 = l_sb[:, i * 384:i * 384 + T], l_sb[:, i * 384 + T:(i + 1) * 384]
                    pe.matmul(bank(4 + i)[:, T:384], tri, r1, start=True, stop=True)
                    pe.matmul(bank(4 + i)[:, 0:T], tri, r0, start=True, stop=False, skip_group_check=True)
                    pe.matmul(bank(4 + i)[:, P:T], ones[:, :], r1, start=False, stop=True, skip_group_check=True)\
                        .then_inc(sb_i, 1)
                pe.wait_ge(sb_a, half + 1)
                for i in range(4):
                    hd = 4 * half + i
                    out_ = bank(i // 2)[(hd % 2) * 64:(hd % 2) * 64 + 64, :]
                    vs = [v_tok[:, b, hd * HD:(hd + 1) * HD] for b in range(TB)]
                    pe.matmul(out_[:, 0:T], vs[0], p_sb[:, i * 384:i * 384 + T], start=True, stop=False,
                              skip_group_check=True)
                    last = pe.matmul(out_[:, P:T], vs[1], p_sb[:, i * 384 + T:(i + 1) * 384], start=False, stop=True,
                                     skip_group_check=True)
                    if i % 2:
                        last.then_inc(sb_o, 1)

            def mb_scores(hd, b):
                r, m = slice((hd % 2) * 64, (hd % 2) * 64 + 64), hd // 2
                return qT[1][r, m, b * P:(b + 1) * P], kT[1][r, m, 0:P * (b + 1)]

            softmaxes(0, lambda b: P * (b + 1), mb_scores,
                      lambda hd, c: v_tok[:, c, 512 + hd * HD:512 + (hd + 1) * HD])
            pe.wait_ge(s_fin, 16)
            pe.wait_ge(sb_ol, 4)
            for q in range(2):
                for m in (2 * q, 2 * q + 1):
                    for b in range(TB):
                        o = ((m % 2) * TB + b) * P
                        last = pe.transpose(bank(q)[:, o:o + P], o_mb[:, b, m * P:(m + 1) * P], ident)
                last.then_inc(ot_ps, 1)
            pe.wait_ge(ot_lo, 2)
            for t in range(2):
                for u in range(2):
                    pe.wait_ge(lo_g, 2 * (G_WB + t) + u + 1)
                    for b in range(TB):
                        for n in range(2):
                            last = rows(bank(4 * t + 2 * b + n), b, (4 * t + 2 * u, 4 * t + 2 * u + 1),
                                        lambda w, i: w[:, u, i * D + n * 512:i * D + (n + 1) * 512], 512,
                                        u == 0, u == 1)
                    last.then_inc(used_g, 1)
            transposes(1)
            pe.wait_ge(xt_lo_s, 8)
            for i in range(2):
                dense(G_WO + i, (4 + i, 6 + i))
            transposes(2)
            pe.wait_ge(xt_lo_s, 12)
            pe.wait_ge(in_["wrt"], 16)
            for b in range(TB):
                for c in range(DC):
                    for k, t in enumerate((xt_hi, xt_lo)):
                        last = pe.matmul(bank(7)[:, b * E:(b + 1) * E], t[:, c, b * P:(b + 1) * P].bitcast(F32),
                                         w_rt[:, c, :], start=c == 0 and k == 0, stop=c == DC - 1 and k == 1)
            last.then_inc(rt_ps, 1)
            gated_phase("moe")
            transposes(3)
            pe.wait_ge(xt_lo_s, 16)
            gated_phase("ff1")
            transposes(4)
            pe.wait_ge(xt_lo_s, 20)
            for j in range(4):
                b0 = 4 + 2 * (j % 2)
                if j >= 2:
                    pe.wait_ge(ev_a, EV_A[G_WIN2 + j - 2])
                    pe.wait_ge(ev_v, EV_V[G_WIN2 + j - 2])
                if j < 2:
                    features(G_WIN2 + j, b0)
                else:
                    dense(G_WIN2 + j, (b0, b0 + 1), 512 if j == 2 else SMALL)
            pe.wait_ge(ev_a, EV_A[G_WIN2 + 3])
            pe.wait_ge(ev_v, EV_V[G_WIN2 + 3])

            def na_scores(hd, b):
                r, m = slice((hd % 2) * 64, (hd % 2) * 64 + 64), hd // 2
                return qT2[r, m, b * P:(b + 1) * P], kT2[r, m, :]

            softmaxes(1, lambda b: T, na_scores, lambda hd, c: v2[:, c, hd * HD:(hd + 1) * HD])
            pe.wait_ge(cn_ready, 1)
            for q in range(2):
                for c in range(2 * q, min(2 * q + 2, 3)):
                    for b in range(TB):
                        o = ((c % 2) * TB + b) * P
                        last = pe.transpose(bank(q)[:, o:o + P], small[:, b, c * P:(c + 1) * P], ident)
                last.then_inc(cn_ps, 1)
            pe.wait_ge(cn_lo, 2)
            pe.wait_ge(s_fin, 32)
            for u, (base, cs, step, n) in enumerate(((0, (0, 1), QW, 384), (4, (2,), KVW, 512))):
                pe.wait_ge(lo_g, 2 * G_MLA + u + 1)
                for b in range(TB):
                    for j in range(2):
                        last = rows(bank(base + 2 * b + j)[:, 0:n], b, cs,
                                    lambda w, i: w[:, u, i * step + j * n:i * step + (j + 1) * n], n, True, True)
                last.then_inc(used_g, 1)
            pe.wait_ge(roped, 2)
            for q in range(8):
                src = (q_tok, k_full)[q // 4]
                if q >= 4:
                    pe.wait_ge((mt_ev_a, mt_ev_v)[q % 2], (q - 4) // 2 + 1)
                for j in range(2):
                    hd = (q % 4) * 2 + j
                    for b in range(TB):
                        o = (j * TB + b) * P
                        last = pe.transpose(bank(q % 4)[0:96, o:o + P], src[:, b, hd * 96:(hd + 1) * 96], ident)
                last.then_inc(mt_ps, 1)
            pe.wait_ge(mt_ev_a, 4)
            pe.wait_ge(mt_ev_v, 4)
            softmaxes(2, lambda b: T, lambda hd, b: (qTm[0:96, hd, b * P:(b + 1) * P], kTm[0:96, hd, :]),
                      lambda hd, c: kv_tok[:, c, hd * 128 + 64:hd * 128 + 128])
            transposes(5)
            pe.wait_ge(xt_lo_s, 24)
            for i in range(2):
                dense(G_WO2 + i, (4 + i, 6 + i))
            transposes(6)
            pe.wait_ge(xt_lo_s, 28)
            gated_phase("ff2")


def distance_buckets():
    dist = 255 - np.arange(BX)
    n = np.maximum(dist, 0)
    large = 16 + (np.log(np.maximum(n, 1).astype(np.float32) / np.float32(16)) / np.float32(math.log(8.0))
                  * np.float32(16)).astype(np.int32)
    bucket = np.where(n < 16, n, np.minimum(large, 31))
    rows = np.zeros((33, BX), np.float32)
    rows[bucket, np.arange(BX)] = dist >= 0
    rows[32] = np.where(dist >= 0, 0.0, -BIG)
    return rows


def constants():
    con = np.zeros((P, C_END), np.float32)
    i = np.arange(P)
    con[:, C_ID:C_ID + P] = np.eye(P)
    con[:, C_TRI:C_TRI + P] = i[:, None] >= i[None, :]
    past = i[:, None] < i[None, :]
    con[:, C_MASK:C_MASK + P] = past
    con[:, C_MIN:C_MIN + P] = np.where(past, BIG, -BIG)
    c = np.arange(64)
    first = np.clip(c - 8, 0, 48)[:, None]
    inside = (c[None, :] >= first) & (c[None, :] < first + 16)
    con[:, C_NA:C_NA + 64] = np.tile(np.where(inside, 0.0, -BIG), (2, 1))
    freq = (1.0 / (np.float32(10000.0) ** (np.arange(8, dtype=np.float32) / np.float32(8)))).astype(np.float32)
    t = np.arange(T)
    ang = np.concatenate([(t // 64).astype(np.float32)[:, None] * freq, (t % 64).astype(np.float32)[:, None] * freq], 1)
    for b in range(TB):
        con[:, C_COS + 16 * b:C_COS + 16 * (b + 1)] = np.cos(ang[b * P:(b + 1) * P])
        con[:, C_SIN + 16 * b:C_SIN + 16 * (b + 1)] = np.sin(ang[b * P:(b + 1) * P])
    return con


INPUTS = ["x", "c", "norm1_g", "norm2_g", "w_ada", "b_ada", "w_in", "w_branch_sb", "w_branch_mb", "w_out", "w_router",
          "router_bias", "w_gate_e", "w_up_e", "w_down_e", "w_gate_sh", "w_up_sh", "w_down_sh", "final_g",
          "ffn1_pre_g_2", "ffn1_w_gu_2", "ffn1_w_down_2", "ffn1_post_g_2", "mix_pre_g_2", "w_in_2", "na_rpb_2",
          "mla_q_norm_g_2", "mla_w_uq_2", "mla_kv_norm_g_2", "mla_w_ukv_2", "na_out_norm_g_2", "mla_out_norm_g_2",
          "w_out_2", "mix_post_g_2", "ffn2_pre_g_2", "ffn2_w_gu_2", "ffn2_w_down_2", "ffn2_post_g_2"]


def kernel(**inputs):
    from concourse import bacc
    from concourse.bass_utils import run_bass_kernel_spmd

    nc = bacc.Bacc("TRN2", target_bir_lowering=False, num_devices=1)
    arrays = {n: np.ascontiguousarray(inputs[n]) for n in INPUTS}
    arrays["rel_bias_t"] = np.ascontiguousarray(np.asarray(inputs["rel_bias"]).T)
    arrays["con"] = constants()
    arrays["buckets"] = distance_buckets()
    a = {n: nc.dram_tensor("in_" + n, v.shape, mybir.dt.from_np(v.dtype), kind="ExternalInput").ap()
         for n, v in arrays.items()}
    out = nc.dram_tensor("out", (1, T, D), F32, kind="ExternalOutput").ap()
    build(nc, a, out)
    r = run_bass_kernel_spmd(nc, [{"in_" + n: v for n, v in arrays.items()}], core_ids=[0])
    return r.results[0]["out"]
```

```python
import math
from contextlib import ExitStack

import concourse.bass as bass
import numpy as np
from concourse import mybir

ALU = mybir.AluOpType
ACT = mybir.ActivationFunctionType
F32 = mybir.dt.float32
F32R = mybir.dt.float32r
BF16 = mybir.dt.bfloat16
AX = mybir.AxisListType.X

P = 128
T = 256
TB = T // P
D = 1024
DC = D // P
HD = 64
NH = 8
E = 64
NGRP = 8
FF = 256
D_FF = 2816
EPS = 1e-6
BIG = 1e30
QW = 768
KVW = 1024
SMALL = 416
UNIT = 2048

N_ADA, N_WIN, N_FF = 12, 10, D_FF // FF
G_ADA = 0
G_WIN = G_ADA + N_ADA
G_WB = G_WIN + N_WIN
G_WO = G_WB + 2
G_MOE = G_WO + 2
G_SH, G_SP = G_MOE, G_MOE + 1
G_FF1 = G_SP + E
G_WIN2 = G_FF1 + N_FF
G_MLA = G_WIN2 + 4
G_WO2 = G_MLA + 1
G_FF2 = G_WO2 + 2
D_SH, D_SP, D_FF1, D_FF2 = 0, 1, E + 1, E + 1 + N_FF
CAP = 96

C_ID, C_TRI, C_MASK, C_MIN, C_NA, C_COS, C_SIN, C_IOTA, C_END = 0, 128, 256, 384, 512, 576, 608, 640, 768
BX = 384
NR = 7 * 128


def at(const, it, per):
    return const if it is None else it * per + const


def build(nc, a, out):
    ctx = ExitStack()
    with ctx:
        def sb(name, shape, dt=F32):
            return ctx.enter_context(nc.sbuf_tensor(name, shape, dt))

        def sem(name):
            return ctx.enter_context(nc.semaphore(name))

        raw_g = sb("raw_g", [P, 2, 2 * UNIT])
        raw_d = sb("raw_d", [P, 2, UNIT])
        g_hi = sb("g_hi", [P, 2, UNIT], F32R)
        g_lo = sb("g_lo", [P, 2, UNIT], F32R)
        d_hi = sb("d_hi", [P, UNIT], F32R)
        d_lo = sb("d_lo", [P, UNIT], F32R)
        xt_hi = sb("xt_hi", [P, DC, T], F32R)
        xt_lo = sb("xt_lo", [P, DC, T], F32R)
        at_hi = sb("at_hi", [P, 2, T], F32R)
        at_lo = sb("at_lo", [P, 2, T], F32R)
        x = sb("x_res", [P, TB, D])
        h = sb("h_tok", [P, TB, D])
        h_end = nc.sbuf_base
        att = sb("att", [P, 3072])
        att_end = nc.sbuf_base
        arena = sb("arena", [P, 14 * 1024])
        arena_end = nc.sbuf_base
        con = sb("con", [P, C_END])
        ones = sb("ones", [P, P])
        zeros = sb("zeros", [P, 512], BF16)
        over_i = sb("over_i", [1, 4], mybir.dt.int32)
        st = sb("stats", [P, 64])

        def lay(base, end, *wanted):
            made = []
            for name, shape in wanted:
                made.append(nc.alloc_sbuf_tensor_at(name, shape, F32R, offset=base))
                base += 4 * int(np.prod(shape[1:]))
            assert base <= end
            return made

        arena_at = arena_end - 4 * 14 * 1024
        xg_shape = [P, 2, DC, 2, CAP]
        xg_lo, = lay(att_end - 4 * 3072, att_end, ("xg_lo", xg_shape))
        y_hi, y_lo = lay(h_end - 4 * TB * D, h_end, ("y_hi", [P, D]), ("y_lo", [P, D]))
        xg_hi, pick, pickT, w_hl = lay(arena_at, arena_at + 20 * 1024, ("xg_hi", xg_shape),
                                       ("pick", [P, 2, TB, 2, CAP]),
                                       ("pickT", [P, 2, T]),
                                       ("w_hl", [P, TB, E, 2]))

        K = 256

        def area(kib, n):
            return arena[:, int(kib * K):int(kib * K) + n]

        shift1, gain1 = area(0, D), area(4, D)
        v_tok = area(0, TB * D).rearrange("p (b n) -> p b n", b=TB)
        gate1, shift2, gain2, gate2 = area(8, D), area(12, D), area(16, D), area(20, D)
        b_ada_row = area(24, 6 * D)
        g1_in, g2_in = area(48, D), area(52, D)
        qT, kT = ([area(24 + 4 * i, 4 * T).rearrange("p (m t) -> p m t", m=4) for i in (0, 2)],
                  [area(28 + 4 * i, 4 * T).rearrange("p (m t) -> p m t", m=4) for i in (0, 2)])
        sig = area(40, TB * 2 * D).rearrange("p (b n) -> p b n", b=TB)
        mb_bias = raw_d[:, 1, :].rearrange("p (h k) -> p h k", h=NH)
        a_sb = area(24, 2 * FF).rearrange("p (b n) -> p b n", b=TB)
        silu = area(26, 2 * FF).rearrange("p (b n) -> p b n", b=TB)
        w_rt = area(28, DC * E).rearrange("p (c e) -> p c e", c=DC)
        rt = area(30, 4 * E * 4)
        w_over = area(34, TB * E).rearrange("p (b e) -> p b e", b=TB)
        row_of = area(34.5, TB * E).rearrange("p (b e) -> p b e", b=TB)
        rbias = area(35, E)
        final_g, pre1, post1 = area(36, D), area(40, D), area(44, D)
        mixpre, mixpost = area(48, D), area(52, D)
        outg = area(12, D)
        qn_g, kvn_g = area(16, 256), area(17, 128)
        pre2, post2 = area(0, D), area(8, D)
        na_bias = [area(0, NH * T).rearrange("p (h k) -> p h k", h=NH),
                   att[:, 1024:3072].rearrange("p (h k) -> p h k", h=NH)]
        v2 = area(8, TB * 512).rearrange("p (b n) -> p b n", b=TB)
        small = area(18, TB * SMALL).rearrange("p (b n) -> p b n", b=TB)
        qT2 = area(28, 4 * T).rearrange("p (m t) -> p m t", m=4)
        kT2 = area(32, 4 * T).rearrange("p (m t) -> p m t", m=4)
        q_tok = area(36, TB * QW).rearrange("p (b n) -> p b n", b=TB)
        kv_tok = area(42, TB * KVW).rearrange("p (b n) -> p b n", b=TB)
        k_full = area(28, TB * QW).rearrange("p (b n) -> p b n", b=TB)
        qTm = area(0, NH * T).rearrange("p (h t) -> p h t", h=NH)
        kTm = att[:, 1024:3072].rearrange("p (h t) -> p h t", h=NH)
        rope_t = area(24, 4 * TB * NH * 16).rearrange("p (i b n) -> p i b n", i=4, b=TB)

        z_sb = h[:, :, :].rearrange("p b n -> p (b n)")[:, 0:4 * 384]
        l_sb = att[:, 0:1536]
        p_sb = att[:, 1536:3072]
        s_buf = [att[:, 0:T], att[:, T:2 * T]]
        pT_sb = [att[:, 512:768].rearrange("p (c q) -> p c q", c=2),
                 att[:, 768:1024].rearrange("p (c q) -> p c q", c=2)]
        o_mb = att[:, 2048:3072].rearrange("p (b n) -> p b n", b=TB)
        relb_in, bucket_in = att[0:33, 0:NH], att[0:33, 16:16 + BX]
        t_bias = att[0:NH, 512:512 + BX]
        rpb_pad = att[0:NH, 1024:1024 + NR]
        c_col, c_sil = st[:, 0:8], st[:, 8:16]

        ps = [ctx.enter_context(nc.psum_tensor(f"bank{i}_{j}", [P, 2, 512], F32))
              for i, j in ((0, 1), (2, 3), (4, 5), (6, 7))]

        def bank(i):
            return ps[i // 2][:, i % 2, :]

        ident = con[:, C_ID:C_ID + P]
        tri = con[:, C_TRI:C_TRI + P]

        t_dram = nc.dram_tensor("t_scratch", (P, NH, BX), F32, kind="Internal").ap()
        n_dram = nc.dram_tensor("n_scratch", (64, NH, NR), F32, kind="Internal").ap()

        class Stream:

            def __init__(self, tag):
                self.landed_g = [sem(tag + "landed_g0"), sem(tag + "landed_g1")]
                self.landed_d = [sem(tag + "landed_d0"), sem(tag + "landed_d1")]
                self.hi_g, self.lo_g, self.used_g = sem(tag + "hi_g"), sem(tag + "lo_g"), sem(tag + "used_g")
                self.hi_d, self.lo_d, self.used_d = sem(tag + "hi_d"), sem(tag + "lo_d"), sem(tag + "used_d")
                self.silu_done, self.gated, self.tr_done = sem(tag + "silu"), sem(tag + "gated"), sem(tag + "tr")
                self.at_hi, self.at_lo = sem(tag + "at_hi"), sem(tag + "at_lo")
                self.xt_ps, self.xt_hi, self.xt_lo = sem(tag + "xt_ps"), sem(tag + "xt_hi"), sem(tag + "xt_lo")

        M, OV = Stream("m_"), Stream("o_")
        h_ready, x_ready = sem("h_ready"), sem("x_ready")
        in_ = {n: sem("in_" + n) for n in ("c", "x", "con", "bada", "g1", "g2", "relb", "bucket", "rpb",
                                           "tb", "nb", "tw", "nw", "wrt", "rbias", "gains", "post",
                                           "outg", "ff2g")}
        chain_v, chain_a, chain_p = sem("chain_v"), sem("chain_a"), sem("chain_p")
        set_up = sem("set_up")
        c_silu, c_bc = sem("c_silu"), sem("c_bc")
        ada_ev = sem("ada_ev")
        tb_ps, tb_sb = sem("tb_ps"), sem("tb_sb")
        ev_a, ev_v = sem("ev_a"), sem("ev_v")
        ss_a, ms_v, sd_a = sem("ss_a"), sem("ms_v"), sem("sd_a")
        sb_z, sb_zc, sb_ab, sb_ln, sb_r = sem("sb_z"), sem("sb_zc"), sem("sb_ab"), sem("sb_ln"), sem("sb_r")
        sb_i, sb_t, sb_a, sb_o, sb_oh, sb_ol = (sem("sb_i"), sem("sb_t"), sem("sb_a"), sem("sb_o"),
                                                sem("sb_oh"), sem("sb_ol"))
        s_ps, s_max, s_exp, s_pt, s_ptc, s_o, s_fin = (sem("s_ps"), sem("s_max"), sem("s_exp"),
                                                       sem("s_pt"), sem("s_ptc"), sem("s_o"), sem("s_fin"))
        ot_ps, ot_hi, ot_lo = sem("ot_ps"), sem("ot_hi"), sem("ot_lo")
        rt_ps, rt_sc, rt_sel, rt_pos = sem("rt_ps"), sem("rt_sc"), sem("rt_sel"), sem("rt_pos")
        rt_cnt, rt_tot, rt_flag = sem("rt_cnt"), sem("rt_tot"), sem("rt_flag")
        tok_hi, tok_lo = sem("tok_hi"), sem("tok_lo")
        picked, ga_ps, xg_a, xg_v = sem("picked"), sem("ga_ps"), sem("xg_a"), sem("xg_v")
        pt_ps, pt_sb, w_row = sem("pt_ps"), sem("pt_sb"), sem("w_row")
        sp_silu, sp_gate, y_ps, y_a, y_v = sem("sp_silu"), sem("sp_gate"), sem("y_ps"), sem("y_a"), sem("y_v")
        summed, h_again = sem("summed"), sem("h_again")
        cn_ready, cn_ps, cn_hi, cn_lo = sem("cn_ready"), sem("cn_ps"), sem("cn_hi"), sem("cn_lo")
        na_ready, roped, mt_ps, mt_ev_a, mt_ev_v = (sem("na_ready"), sem("roped"), sem("mt_ps"),
                                                    sem("mt_ev_a"), sem("mt_ev_v"))
        s_out = sem("s_out")

        block = ctx.enter_context(nc.Block())

        def raw_dense(g, u):
            return raw_g[:, g % 2, u * UNIT:(u + 1) * UNIT]

        def raw_gated(g, u):
            return raw_g[:, g % 2, :].rearrange("p (g c n) -> p c g n", g=2, c=DC)[:, 4 * u:4 * u + 4, :, :]

        def dense_w(buf, u, c4, lo, n):
            return buf[:, u, c4 * 512 + lo:c4 * 512 + lo + n]

        EV_A, EV_V = {}, {}
        n_a = n_v = 0
        for g in [*range(G_WIN, G_WIN + N_WIN), *range(G_WIN2, G_WIN2 + 4), G_MLA]:
            gate = G_WIN + 6 <= g < G_WIN + N_WIN
            n_a += 4 if g == G_MLA else 2 if gate else 1
            n_v += 4 if g == G_MLA else 0 if gate else 1
            EV_A[g], EV_V[g] = n_a, n_v

        PHASES = {"sh": (M, G_SH, D_SH, 0, 1), "over": (OV, 0, 0, 0, E), "ff1": (M, G_FF1, D_FF1, 1, N_FF),
                  "ff2": (M, G_FF2, D_FF2, 1 + N_FF, N_FF)}
        tok = [t[:, :, :].rearrange("p c t -> p (c t)").rearrange("p (b c n) -> p b c n", b=TB, c=DC)
               for t in (xt_hi, xt_lo)]
        h_chunks = h[:, :, :].rearrange("p b (n c) -> p b c n", c=DC)

        def if_over(eng, body):
            eng.wait_ge(rt_flag, 1)
            beyond = eng.value_load(over_i[0:1, 0:1], min_val=0, max_val=T * E)
            with eng.If(beyond > 0):
                body()

        def turns(eng, n, first=0, by=2, rest=3):
            q = (n - first - rest) // by
            if q > 0:
                with eng.Fori(0, q) as it:
                    for j in range(by):
                        yield first + j, it
            for s in range(first + by * max(q, 0), n):
                yield s, None

        @block.sync
        def _(sp):
            def free_g(g, it=None, S=M):
                if g >= 2:
                    sp.wait_ge(S.lo_g, at(2 * g - 2, it, 4))

            def load_dense(g, src, width=512, chunks=DC):
                free_g(g)
                half = chunks // 2
                for u in range(2):
                    dst = raw_dense(g, u)[:, 0:half * width].rearrange("p (c n) -> p c n", c=half)
                    sp.dma_start(dst, src[:, u * half:(u + 1) * half, :]).then_inc(M.landed_g[g % 2], 16)

            def load_gated(g, gate, up, it=None, S=M):
                free_g(g, it, S)
                for k, src in enumerate((gate, up)):
                    dst = raw_g[:, g % 2, k * UNIT:(k + 1) * UNIT].rearrange("p (c n) -> p c n", c=DC)
                    sp.dma_start(dst, src.rearrange("(p c) n -> p c n", c=DC)).then_inc(S.landed_g[g % 2], 16)

            def load_down(d, src, it=None, S=M):
                if d >= 2:
                    sp.wait_ge(S.lo_d, at(d - 1, it, 2))
                dst = raw_d[:, d % 2, :].rearrange("p (c n) -> p c n", c=2)
                sp.dma_start(dst, src.rearrange("(p c) n -> p c n", c=2)).then_inc(S.landed_d[d % 2], 16)

            def one(src, i):
                return src[bass.ds(i, 1)].rearrange("e k n -> (e k) n") if not isinstance(i, int) else src[i]

            def gated_stream(S, g0, d0, n, gate_up, down):
                for s in range(min(n, 2)):
                    load_gated(g0 + s, *gate_up(s, None), S=S)
                    load_down(d0 + s, down(s, None), S=S)
                if n > 2:
                    for s, it in turns(sp, n, 2):
                        load_gated(g0 + s, *gate_up(s, it), it, S)
                        load_down(d0 + s, down(s, it), it, S)

            w_ada = a["w_ada"][0].rearrange("(p c) n -> p c n", c=DC)
            w_in = a["w_in"][0].rearrange("(p c) n -> p c n", c=DC)
            for t in range(N_ADA):
                load_dense(G_ADA + t, w_ada[:, :, t * 512:(t + 1) * 512])
                if t == 2:
                    sp.wait_ge(in_["tw"], 16)
                    sp.dma_start(mb_bias, bass.AP(t_dram.tensor, 127, [[NH * BX - 1, P], [BX, NH], [1, T]]))\
                        .then_inc(in_["tb"], 16)
            for t in range(N_WIN):
                load_dense(G_WIN + t, w_in[:, :, t * 512:(t + 1) * 512])
            for i, n in enumerate(("w_branch_sb", "w_branch_mb")):
                load_dense(G_WB + i, a[n][0].rearrange("(c p) n -> p c n", p=P), D, 4)
            w_out = a["w_out"][0].rearrange("(p c) n -> p c n", c=DC)
            for i in range(2):
                load_dense(G_WO + i, w_out[:, :, i * 512:(i + 1) * 512])
            sp.wait_ge(h_ready, 2)
            sp.dma_start(w_rt, a["w_router"][0].rearrange("(p c) n -> p c n", c=DC)).then_inc(in_["wrt"], 16)
            sp.dma_start(rbias, a["router_bias"].to_broadcast([P, E])).then_inc(in_["rbias"], 16)
            for dst, n in ((final_g, "final_g"), (pre1, "ffn1_pre_g_2"), (post1, "ffn1_post_g_2"),
                           (mixpre, "mix_pre_g_2"), (mixpost, "mix_post_g_2")):
                src = a[n].rearrange("(o n) -> o n", o=1) if n == "final_g" else a[n]
                sp.dma_start(dst, src.to_broadcast([P, D])).then_inc(in_["gains"], 16)

            def moe_gate_up(s, it):
                i = at(s, it, 2)
                return one(a["w_gate_e"][0], i), one(a["w_up_e"][0], i)

            def moe_down(s, it):
                return one(a["w_down_e"][0], at(s, it, 2))

            def ff_stream(w_gu, w_down):
                def gate_up(s, it):
                    if it is None:
                        return w_gu[:, s * FF:(s + 1) * FF], w_gu[:, D_FF + s * FF:D_FF + (s + 1) * FF]
                    return (w_gu[:, bass.ds(it * (2 * FF) + s * FF, FF)],
                            w_gu[:, bass.ds(it * (2 * FF) + (D_FF + s * FF), FF)])

                def down(s, it):
                    if it is None:
                        return w_down[s * FF:(s + 1) * FF, :]
                    return w_down[bass.ds(it * (2 * FF) + s * FF, FF), :]
                return gate_up, down

            gated_stream(M, G_SH, D_SH, 1, lambda s, it: (a["w_gate_sh"][0], a["w_up_sh"][0]),
                         lambda s, it: a["w_down_sh"][0])
            gated_stream(M, G_SP, D_SP, E, moe_gate_up, moe_down)

            def over():
                sp.wait_ge(summed, E)
                gated_stream(OV, 0, 0, E, moe_gate_up, moe_down)
                sp.wait_ge(OV.used_d, E + 1)

            if_over(sp, over)
            gated_stream(M, G_FF1, D_FF1, N_FF, *ff_stream(a["ffn1_w_gu_2"][0], a["ffn1_w_down_2"][0]))
            w_in2 = a["w_in_2"][0].rearrange("(p c) n -> p c n", c=DC)
            for t in range(4):
                w = 512 if t < 3 else SMALL
                load_dense(G_WIN2 + t, w_in2[:, :, t * 512:t * 512 + w], w)
            for b in range(TB):
                for rl in range(2):
                    for r in range(4):
                        off = (3 + r - 2 * b - rl) * P + 63
                        sp.dma_start(na_bias[b][rl * 64:(rl + 1) * 64, :, r * 64:(r + 1) * 64],
                                     bass.AP(n_dram.tensor, off, [[NH * NR - 1, 64], [NR, NH], [1, 64]]))\
                            .then_inc(in_["nb"], 16)
            for i, n in enumerate(("na_out_norm_g_2", "mla_out_norm_g_2")):
                sp.dma_start(outg[:, i * 512:(i + 1) * 512], a[n].to_broadcast([P, 512])).then_inc(in_["outg"], 16)
            sp.dma_start(qn_g, a["mla_q_norm_g_2"].to_broadcast([P, 256])).then_inc(in_["outg"], 16)
            sp.dma_start(kvn_g, a["mla_kv_norm_g_2"].to_broadcast([P, 128])).then_inc(in_["outg"], 16)
            g = G_MLA
            free_g(g)
            sp.dma_start(raw_g[:, g % 2, 0:2 * QW].rearrange("p (c n) -> p c n", c=2),
                         a["mla_w_uq_2"][0].rearrange("(c p) n -> p c n", p=P)).then_inc(M.landed_g[g % 2], 16)
            sp.dma_start(raw_g[:, g % 2, UNIT:UNIT + KVW], a["mla_w_ukv_2"][0]).then_inc(M.landed_g[g % 2], 16)
            w_out2 = a["w_out_2"][0].rearrange("(p c) n -> p c n", c=DC)
            for i in range(2):
                load_dense(G_WO2 + i, w_out2[:, :, i * 512:(i + 1) * 512])
            sp.wait_ge(s_fin, 48)
            sp.dma_start(pre2, a["ffn2_pre_g_2"].to_broadcast([P, D])).then_inc(in_["ff2g"], 16)
            sp.dma_start(post2, a["ffn2_post_g_2"].to_broadcast([P, D])).then_inc(in_["ff2g"], 16)
            gated_stream(M, G_FF2, D_FF2, N_FF, *ff_stream(a["ffn2_w_gu_2"][0], a["ffn2_w_down_2"][0]))
            sp.wait_ge(x_ready, 6)
            sp.dma_start(out.rearrange("o (b p) n -> p (o b) n", p=P), x[:, :, :]).then_inc(s_out, 16)
            sp.wait_ge(s_out, 16)

        @block.gpsimd
        def _(pool):
            pool.memset(ones[:, :], 1.0).then_inc(set_up, 1)
            pool.wait_ge(set_up, 1)
            pool.memset(zeros[:, :], 0.0).then_inc(set_up, 1)
            pool.wait_ge(set_up, 2)
            pool.memset(relb_in[32:33, :], 1.0).then_inc(set_up, 1)
            pool.wait_ge(set_up, 3)
            pool.memset(rpb_pad, 0.0).then_inc(chain_p, 1)
            pool.wait_ge(chain_p, 1)
            pool.dma_start(rpb_pad.rearrange("h (r c) -> h r c", r=7)[:, :, 48:79], a["na_rpb_2"][0][:, 4:11, :])\
                .then_inc(in_["rpb"], 16)
            pool.wait_ge(in_["rpb"], 16)
            pool.dma_start(n_dram.rearrange("q h x -> h q x"), rpb_pad.unsqueeze(1).to_broadcast([NH, 64, NR]))\
                .then_inc(in_["nw"], 16)
            pool.wait_ge(in_["nw"], 16)
            pool.wait_ge(tb_sb, 1)
            pool.dma_start(t_dram.rearrange("q h x -> h q x"), t_bias.unsqueeze(1).to_broadcast([NH, P, BX]))\
                .then_inc(in_["tw"], 16)
            pool.wait_ge(in_["tw"], 16)
            pool.wait_ge(in_["nb"], 256)
            for b in range(TB):
                v = na_bias[b].rearrange("p h (r c) -> p (h r) c", r=4)
                m = con[:, C_NA:C_NA + 64].unsqueeze(1).to_broadcast([P, 4 * NH, 64])
                pool.tensor_tensor(v, v, m, ALU.add).then_inc(na_ready, 1)

        @block.scalar
        def _(act):
            chain = [0]

            def link(ins):
                chain[0] += 1
                ins.then_inc(chain_a, 1)
                act.wait_ge(chain_a, chain[0])

            act.dma_start(c_col, a["c"].rearrange("o (p c) -> p (o c)", c=DC)).then_inc(in_["c"], 16)
            act.dma_start(con[:, :], a["con"]).then_inc(in_["con"], 16)
            act.dma_start(x[:, :, :], a["x"].rearrange("o (b p) n -> p (o b) n", p=P)).then_inc(in_["x"], 16)
            act.dma_start(b_ada_row[0:1, :], a["b_ada"]).then_inc(in_["bada"], 16)
            act.dma_start(relb_in[0:32, :], a["rel_bias_t"]).then_inc(in_["relb"], 16)
            act.dma_start(bucket_in, a["buckets"]).then_inc(in_["bucket"], 16)
            act.dma_start(g1_in, a["norm1_g"].to_broadcast([P, D])).then_inc(in_["g1"], 16)
            act.dma_start(g2_in, a["norm2_g"].to_broadcast([P, D])).then_inc(in_["g2"], 16)

            def split_hi(g, u, gated_tile=False, it=None, cols=UNIT, S=M, by=2):
                act.wait_ge(S.landed_g[g % 2], at(32 * (g // 2 + 1), it, 16 * by))
                if g:
                    act.wait_ge(S.used_g, at(2 * g + u - 1, it, 2 * by))
                if gated_tile:
                    dst = g_hi[:, u, :].rearrange("p (c g n) -> p c g n", c=4, g=2)
                    act.activation(dst, raw_gated(g, u), ACT.Copy).then_inc(S.hi_g, 1)
                else:
                    act.activation(g_hi[:, u, 0:cols], raw_dense(g, u)[:, 0:cols], ACT.Copy).then_inc(S.hi_g, 1)

            def transposed(k, S=M, base=0):
                for q in range(4):
                    act.wait_ge(S.xt_ps, 4 * k + q + 1)
                    act.activation(xt_hi[:, 2 * q:2 * q + 2, :].rearrange("p c t -> p (c t)"), bank(base + q),
                                   ACT.Copy).then_inc(S.xt_hi, 1)

            def squares(k, srcs, after, count, scratch):
                for i, src in enumerate(srcs):
                    act.wait_ge(after, count)
                    ins = act.activation(scratch(i), src, ACT.Square, accum_out=st[:, 16 + i:17 + i])
                ins.then_inc(ss_a, 1)
                act.wait_ge(ms_v, k + 1)
                act.activation(st[:, 24:24 + len(srcs)], st[:, 20:20 + len(srcs)], ACT.Sqrt).then_inc(sd_a, 1)

            def hi_down(d, it=None, S=M, by=2):
                act.wait_ge(S.landed_d[d % 2], at(16 * (d // 2 + 1), it, 8 * by))
                act.wait_ge(S.used_d, at(d + 1, it, by))
                act.activation(d_hi[:, :], raw_d[:, d % 2, :], ACT.Copy).then_inc(S.hi_d, 1)

            def hi_gated(d, it=None, S=M):
                act.wait_ge(S.tr_done, at(d + 1, it, 2))
                act.activation(at_hi[:, :, :].rearrange("p c t -> p (c t)"), bank(6), ACT.Copy)\
                    .then_inc(S.at_hi, 1)

            def gated_phase(name, last_down=True):
                S, g0, d0, q0, n = PHASES[name]

                def silus(s, it=None):
                    act.wait_ge(S.used_g, at(2 * (g0 + s) + 2, it, 4))
                    for b in range(TB):
                        if q0 + s:
                            act.wait_ge(S.gated, at(2 * (q0 + s) - 1 + b, it, 4))
                        act.activation(silu[:, b, :], bank(4 + b)[:, 0:FF], ACT.Silu).then_inc(S.silu_done, 1)

                split_hi(g0, 0, True, S=S)
                split_hi(g0, 1, True, S=S)
                if n > 1:
                    split_hi(g0 + 1, 0, True, S=S)
                silus(0)
                if n > 1:
                    split_hi(g0 + 1, 1, True, S=S)
                for s, it in turns(act, n):
                    hi_down(d0 + s, it, S)
                    hi_gated(d0 + s, it, S)
                    if s + 2 < n:
                        split_hi(g0 + s + 2, 0, True, it, S=S)
                    if s + 1 < n:
                        silus(s + 1, it)
                    if s + 2 < n:
                        split_hi(g0 + s + 2, 1, True, it, S=S)

            def sparse_phase():
                def gathered(s, k, it=None):
                    act.wait_ge(ga_ps, at(8 + 4 * s + k + 1, it, 16))
                    pair, c = s // 2 + 1, 4 * (s % 2) + k
                    act.activation(xg_hi[:, pair % 2, c:c + 2, :, :].rearrange("p c e r -> p (c e r)"),
                                   bank(7)[:, 0:4 * CAP], ACT.Copy).then_inc(xg_a, 1)

                act.wait_ge(M.used_g, 2 * G_SH + 2)
                for b in range(TB):
                    ins = act.activation(tok[0][:, b, :, :], h_chunks[:, b, :, :], ACT.Copy)
                ins.then_inc(tok_hi, 1)
                hi_gated(D_SH)
                hi_down(D_SH)
                split_hi(G_SP, 0, True)
                split_hi(G_SP, 1, True)
                for s in (-2, -1):
                    for k in (0, 2):
                        gathered(s, k)

                def rows_down(s, it=None):
                    for n in range(2):
                        if n:
                            act.wait_ge(M.used_d, at(D_SP + s + 2, it, 4))
                        else:
                            act.wait_ge(y_ps, at(s + 1, it, 4))
                        act.activation(y_hi[0:CAP, n * 512:(n + 1) * 512], bank(5 + n)[0:CAP, :], ACT.Copy)\
                            .then_inc(y_a, 1)

                def rows_t(s, it=None):
                    act.wait_ge(M.tr_done, at(D_SP + s + 1, it, 4))
                    act.activation(at_hi[:, :, 0:CAP], bank(5)[:, 0:2 * CAP].rearrange("p (c r) -> p c r", c=2),
                                   ACT.Copy).then_inc(M.at_hi, 1)

                def body(s, it=None):
                    g = G_SP + s
                    if s + 1 < E:
                        split_hi(g + 1, 0, True, it, by=4)
                    if s:
                        rows_t(s - 1, it)
                    act.wait_ge(w_row, at(s + 1, it, 4))
                    act.activation(pickT[0:CAP, s % 2, :], bank(6)[0:CAP, 0:T], ACT.Copy).then_inc(pt_sb, 1)
                    if s + 2 < E or it is not None:
                        gathered(s, 0, it)
                    act.wait_ge(M.used_g, at(2 * g + 2, it, 8))
                    act.activation(silu[0:CAP, 0, :], bank(4)[0:CAP, 0:FF], ACT.Silu).then_inc(sp_silu, 1)
                    if s + 1 < E:
                        split_hi(g + 1, 1, True, it, by=4)
                    if s:
                        rows_down(s - 1, it)
                    if s + 2 < E or it is not None:
                        gathered(s, 2, it)
                    hi_down(D_SP + s, it, by=4)

                body(0)
                for s, it in turns(act, E, 1, 4):
                    body(s, it)
                rows_t(E - 1)
                rows_down(E - 1)

            def softmaxes(k, kw):
                def copy_pt(n):
                    i = n - 16 * k
                    act.wait_ge(s_pt, n + 1)
                    if n >= 2:
                        act.wait_ge(s_o, n - 1)
                    w = kw(i % 2)
                    act.activation(pT_sb[n % 2].rearrange("p c q -> p (c q)")[:, 0:w], bank(4 + n % 2)[:, 0:w],
                                   ACT.Copy).then_inc(s_ptc, 1)

                for i in range(16):
                    n = 16 * k + i
                    w = kw(i % 2)
                    act.wait_ge(s_max, n + 1)
                    if n >= 2:
                        act.wait_ge(s_fin, n - 1)
                    act.activation(s_buf[n % 2][:, 0:w], s_buf[n % 2][:, 0:w], ACT.Exp,
                                   bias=st[:, 32 + n % 2:33 + n % 2], accum_out=st[:, 36 + n % 2:37 + n % 2])\
                        .then_inc(s_exp, 1)
                    if i:
                        copy_pt(n - 1)
                copy_pt(16 * k + 15)

            act.wait_ge(in_["c"], 16)
            act.activation(c_sil, c_col, ACT.Silu).then_inc(c_silu, 1)
            mods = (shift1, gain1, gate1, shift2, gain2, gate2)
            squares(0, [x[:, b, :] for b in range(TB)], in_["x"], 16, lambda i: h[:, i, :])

            def ada_out(t):
                act.wait_ge(M.used_g, 2 * t + 2)
                act.activation(mods[t // 2][:, (t % 2) * 512:(t % 2 + 1) * 512], bank(4 + t % 4), ACT.Copy)\
                    .then_inc(ada_ev, 1)

            for t in range(N_ADA):
                split_hi(G_ADA + t, 0)
                split_hi(G_ADA + t, 1)
                if t:
                    ada_out(t - 1)
            split_hi(G_WIN, 0)
            ada_out(N_ADA - 1)
            split_hi(G_WIN, 1)
            transposed(0)

            def win_out(j):
                act.wait_ge(M.used_g, 2 * (G_WIN + j) + 2)
                b0 = 4 + 2 * (j % 2)
                if j in (0, 1, 3, 4):
                    dst = (qT, kT)[j % 3][j // 3][:, 0:2, :].rearrange("p m t -> p (m t)")
                    act.activation(dst, bank(b0), ACT.Copy, scale=0.125 if j % 3 == 0 else 1.0).then_inc(ev_a, 1)
                elif j in (2, 5):
                    act.wait_ge(h_ready, 1)
                    act.activation(v_tok[:, 0, (j // 3) * 512:(j // 3 + 1) * 512], bank(b0), ACT.Copy)\
                        .then_inc(ev_a, 1)
                else:
                    for b in range(TB):
                        act.activation(sig[:, b, (j - 6) * 512:(j - 5) * 512], bank(b0 + b), ACT.Sigmoid)\
                            .then_inc(ev_a, 1)

            for j in range(N_WIN):
                if j:
                    split_hi(G_WIN + j, 0)
                    split_hi(G_WIN + j, 1)
                    win_out(j - 1)
            win_out(N_WIN - 1)

            for half in range(2):
                for i in range(4):
                    act.wait_ge(sb_z, 4 * half + i + 1)
                    act.activation(z_sb[:, i * 384:(i + 1) * 384], bank(i)[:, 0:384], ACT.Copy).then_inc(sb_zc, 1)
                act.wait_ge(sb_ab, half + 1)
                link(act.activation(l_sb, l_sb, ACT.Exp))
                act.activation(l_sb, l_sb, ACT.Ln, bias=1.0).then_inc(sb_ln, 1)
                act.wait_ge(sb_t, half + 1)
                act.activation(p_sb, p_sb, ACT.Exp).then_inc(sb_a, 1)
                for i in range(2):
                    act.wait_ge(sb_o, 2 * half + i + 1)
                    act.activation(xt_hi[:, 2 * half + i, :], bank(i)[:, 0:T], ACT.Copy).then_inc(sb_oh, 1)
            split_hi(G_WB, 0)
            split_hi(G_WB, 1)
            softmaxes(0, lambda b: P * (b + 1))

            def heads_t(k, base, count):
                for q in range(count):
                    act.wait_ge(ot_ps, k + q + 1)
                    act.activation(xt_hi[:, base + 2 * q:base + 2 * q + 2, :].rearrange("p c t -> p (c t)"),
                                   bank(q), ACT.Copy).then_inc(ot_hi, 1)

            heads_t(0, 4, 2)
            split_hi(G_WB + 1, 0)
            split_hi(G_WB + 1, 1)
            split_hi(G_WO, 0)
            split_hi(G_WO, 1)
            transposed(1)
            split_hi(G_WO + 1, 0)
            split_hi(G_WO + 1, 1)
            squares(1, [x[:, b, :] for b in range(TB)], x_ready, 1, lambda i: h[:, i, :])
            transposed(2)
            act.wait_ge(rt_ps, 1)
            act.activation(rt[:, 0:2 * E], bank(7)[:, 0:2 * E], ACT.Sigmoid).then_inc(rt_sc, 1)
            split_hi(G_SH, 0, True)
            split_hi(G_SH, 1, True)
            act.wait_ge(M.used_g, 2 * G_SH + 2)
            for b in range(TB):
                act.activation(silu[:, b, :], bank(4 + b)[:, 0:FF], ACT.Silu).then_inc(M.silu_done, 1)
            sparse_phase()

            def over():
                act.wait_ge(summed, E)
                transposed(0, OV, 4)
                gated_phase("over")
                act.wait_ge(OV.used_d, E + 1)

            if_over(act, over)
            squares(2, [x[:, b, :] for b in range(TB)], x_ready, 2, lambda i: h[:, i, :])
            squares(3, [x[:, b, :] for b in range(TB)], x_ready, 3, lambda i: h[:, i, :])
            transposed(3)
            gated_phase("ff1")
            squares(4, [ps[b][:, :, :].rearrange("p a n -> p (a n)") for b in range(TB)], M.used_d, D_FF1 + N_FF + 1,
                    lambda i: h[:, i, :])
            squares(5, [x[:, b, :] for b in range(TB)], x_ready, 4, lambda i: h[:, i, :])
            transposed(4)

            def win2_out(j):
                act.wait_ge(M.used_g, 2 * (G_WIN2 + j) + 2)
                b0 = 4 + 2 * (j % 2)
                if j < 2:
                    dst = (qT2, kT2)[j][:, 0:2, :].rearrange("p m t -> p (m t)")
                    act.activation(dst, bank(b0), ACT.Copy, scale=0.125 if j == 0 else 1.0).then_inc(ev_a, 1)
                elif j == 2:
                    act.activation(v2[:, 0, :], bank(b0), ACT.Copy).then_inc(ev_a, 1)
                else:
                    act.activation(small[:, 0, :], bank(b0)[:, 0:SMALL], ACT.Copy).then_inc(ev_a, 1)

            for j in range(4):
                cols = UNIT if j < 3 else 4 * SMALL
                split_hi(G_WIN2 + j, 0, cols=cols)
                split_hi(G_WIN2 + j, 1, cols=cols)
                if j:
                    win2_out(j - 1)
            win2_out(3)
            srcs = [small[:, b, lo:hi] for b in range(TB) for lo, hi in ((0, 256), (256, 384))]
            act.wait_ge(ev_a, EV_A[G_WIN2 + 3])
            squares(6, srcs, ev_v, EV_V[G_WIN2 + 3], lambda i: att[:, i * 256:i * 256 + srcs[i].shape[-1]])
            softmaxes(1, lambda b: T)
            split_hi(G_MLA, 0, cols=2 * QW)
            split_hi(G_MLA, 1, cols=KVW)
            for q in range(2):
                act.wait_ge(cn_ps, q + 1)
                w = 512 if q == 0 else 256
                act.activation(xt_hi[:, 2 * q:2 * q + w // T, :].rearrange("p c t -> p (c t)"), bank(q)[:, 0:w],
                               ACT.Copy).then_inc(cn_hi, 1)
            act.wait_ge(M.used_g, 2 * G_MLA + 2)
            for i in range(4):
                act.activation(q_tok[:, i // 2, (i % 2) * 384:(i % 2 + 1) * 384], bank(i)[:, 0:384], ACT.Copy)\
                    .then_inc(ev_a, 1)
            for q in range(0, 8, 2):
                act.wait_ge(mt_ps, q + 1)
                dst = (qTm, kTm)[q // 4][0:96, (q % 4) * 2:(q % 4) * 2 + 2, :].rearrange("p h t -> p (h t)")
                act.activation(dst, bank(q % 4)[0:96, :], ACT.Copy).then_inc(mt_ev_a, 1)
            softmaxes(2, lambda b: T)
            srcs2 = [h[:, b, i * 512:(i + 1) * 512] for b in range(TB) for i in range(2)]
            squares(7, srcs2, s_fin, 48, lambda i: att[:, i * 512:(i + 1) * 512])
            split_hi(G_WO2, 0)
            split_hi(G_WO2, 1)
            transposed(5)
            split_hi(G_WO2 + 1, 0)
            split_hi(G_WO2 + 1, 1)
            squares(8, [ps[2 + b][:, :, :].rearrange("p a n -> p (a n)") for b in range(TB)], M.used_g,
                    2 * (G_WO2 + 1) + 2, lambda i: h[:, i, :])
            squares(9, [x[:, b, :] for b in range(TB)], x_ready, 5, lambda i: h[:, i, :])
            transposed(6)
            gated_phase("ff2")
            squares(10, [ps[b][:, :, :].rearrange("p a n -> p (a n)") for b in range(TB)], M.used_d, D_FF2 + N_FF + 1,
                    lambda i: h[:, i, :])

        @block.vector
        def _(dve):
            chain = [0]

            def link(ins):
                chain[0] += 1
                ins.then_inc(chain_v, 1)
                dve.wait_ge(chain_v, chain[0])

            def split_lo(g, u, gated_tile=False, it=None, cols=UNIT, S=M, by=2):
                dve.wait_ge(S.hi_g, at(2 * g + u + 1, it, 2 * by))
                if gated_tile:
                    hi, lo = (t[:, u, :].rearrange("p (c g n) -> p c g n", c=4, g=2) for t in (g_hi, g_lo))
                    raw = raw_gated(g, u)
                else:
                    hi, lo, raw = g_hi[:, u, 0:cols], g_lo[:, u, 0:cols], raw_dense(g, u)[:, 0:cols]
                dve.tensor_tensor(lo, raw, hi.bitcast(F32), ALU.subtract).then_inc(S.lo_g, 1)

            def transposed(k, S=M, base=0):
                for q in range(4):
                    dve.wait_ge(S.xt_hi, 4 * k + q + 1)
                    hi, lo = (t[:, 2 * q:2 * q + 2, :].rearrange("p c t -> p (c t)") for t in (xt_hi, xt_lo))
                    dve.tensor_tensor(lo, bank(base + q), hi.bitcast(F32), ALU.subtract).then_inc(S.xt_lo, 1)

            def roots(k, widths):
                n = len(widths)
                dve.wait_ge(ss_a, k + 1)
                for i, w in enumerate(widths):
                    ins = dve.tensor_scalar(st[:, 20 + i:21 + i], st[:, 16 + i:17 + i], 1.0 / w, EPS,
                                            ALU.mult, ALU.add)
                ins.then_inc(ms_v, 1)
                dve.wait_ge(sd_a, k + 1)
                link(dve.reciprocal(st[:, 28:28 + n], st[:, 24:24 + n]))

            def scaled(dst, src, i, gain):
                return dve.scalar_tensor_tensor(out=dst, in0=src, scalar=st[:, 28 + i:29 + i], in1=gain,
                                                op0=ALU.mult, op1=ALU.mult)

            def lo_down(d, it=None, S=M, by=2):
                dve.wait_ge(S.hi_d, at(d + 1, it, by))
                dve.tensor_tensor(d_lo[:, :], raw_d[:, d % 2, :], d_hi[:, :].bitcast(F32), ALU.subtract)\
                    .then_inc(S.lo_d, 1)

            def lo_gated(d, it=None, S=M):
                dve.wait_ge(S.at_hi, at(d + 1, it, 2))
                hi, lo = (t[:, :, :].rearrange("p c t -> p (c t)") for t in (at_hi, at_lo))
                dve.tensor_tensor(lo, bank(6), hi.bitcast(F32), ALU.subtract).then_inc(S.at_lo, 1)

            def gate(S, q, s, weight=None, it=None):
                for b in range(TB):
                    w = 1.0
                    if weight is not None:
                        w = weight[:, b, s:s + 1] if it is None else weight[:, b, bass.ds(it * 2 + s, 1)]
                    dve.wait_ge(S.silu_done, at(2 * q + b + 1, it, 4))
                    dve.scalar_tensor_tensor(out=a_sb[:, b, :], in0=silu[:, b, :], scalar=w,
                                             in1=bank(4 + b)[:, FF:2 * FF], op0=ALU.mult, op1=ALU.mult)\
                        .then_inc(S.gated, 1)

            def gated_phase(name, weight=None):
                S, g0, d0, q0, n = PHASES[name]
                split_lo(g0, 0, True, S=S)
                split_lo(g0, 1, True, S=S)
                split_lo(g0 + 1, 0, True, S=S)
                gate(S, q0, 0, weight)
                split_lo(g0 + 1, 1, True, S=S)
                for s, it in turns(dve, n):
                    lo_down(d0 + s, it, S)
                    lo_gated(d0 + s, it, S)
                    if s + 2 < n:
                        split_lo(g0 + s + 2, 0, True, it, S=S)
                    if s + 1 < n:
                        gate(S, q0 + s + 1, s + 1, weight, it)
                    if s + 2 < n:
                        split_lo(g0 + s + 2, 1, True, it, S=S)

            def pick_rows(pair, it=None):
                if pair >= 2:
                    dve.wait_ge(pt_ps, at(2 * pair - 2, it, 4))
                for e in range(2):
                    for b in range(TB):
                        s = 2 * pair + e
                        r = row_of[:, b, s:s + 1] if it is None else row_of[:, b, bass.ds(it * 4 + s, 1)]
                        ins = dve.tensor_scalar(pick[:, pair % 2, b, e, :], con[:, C_IOTA:C_IOTA + CAP], r, None,
                                                ALU.is_equal)
                ins.then_inc(picked, 1)

            def sparse_phase():
                def gathered(s, k, it=None):
                    dve.wait_ge(ga_ps, at(8 + 4 * s + k + 1, it, 16))
                    pair, c = s // 2 + 1, 4 * (s % 2) + k - 1
                    dve.tensor_copy(xg_lo[:, pair % 2, c:c + 2, :, :].rearrange("p c e r -> p (c e r)"),
                                    bank(7)[:, 0:4 * CAP]).then_inc(xg_v, 1)

                pick_rows(0)
                lo_gated(D_SH)
                lo_down(D_SH)
                split_lo(G_SP, 0, True)
                split_lo(G_SP, 1, True)
                for s in (-2, -1):
                    for k in (1, 3):
                        gathered(s, k)
                pick_rows(1)

                def rows_down(s, it=None):
                    for n in range(2):
                        dve.wait_ge(y_a, at(2 * s + n + 1, it, 8))
                        hi, lo = (t[0:CAP, n * 512:(n + 1) * 512] for t in (y_hi, y_lo))
                        dve.tensor_tensor(lo, bank(5 + n)[0:CAP, :], hi.bitcast(F32), ALU.subtract).then_inc(y_v, 1)

                def rows_t(s, it=None):
                    dve.wait_ge(M.at_hi, at(D_SP + s + 1, it, 4))
                    dve.tensor_tensor(at_lo[:, :, 0:CAP], bank(5)[:, 0:2 * CAP].rearrange("p (c r) -> p c r", c=2),
                                      at_hi[:, :, 0:CAP].bitcast(F32), ALU.subtract).then_inc(M.at_lo, 1)

                def body(s, it=None):
                    g = G_SP + s
                    dve.wait_ge(pt_ps, at(s + 1, it, 4))
                    dve.reduce_sum(st[0:CAP, 48 + s % 2:49 + s % 2], bank(6)[0:CAP, T:T + 2], AX).then_inc(w_row, 1)
                    if s:
                        rows_t(s - 1, it)
                    if s + 1 < E:
                        split_lo(g + 1, 0, True, it, by=4)
                    if s + 2 < E or it is not None:
                        gathered(s, 1, it)
                    dve.wait_ge(sp_silu, at(s + 1, it, 4))
                    dve.wait_ge(w_row, at(s + 1, it, 4))
                    dve.scalar_tensor_tensor(out=a_sb[0:CAP, 0, :], in0=silu[0:CAP, 0, :],
                                             scalar=st[0:CAP, 48 + s % 2:49 + s % 2], in1=bank(4)[0:CAP, FF:2 * FF],
                                             op0=ALU.mult, op1=ALU.mult).then_inc(sp_gate, 1)
                    if s % 2 and (s + 3 < E or it is not None):
                        pick_rows(s // 2 + 2, it)
                    if s:
                        rows_down(s - 1, it)
                    if s + 1 < E:
                        split_lo(g + 1, 1, True, it, by=4)
                    if s + 2 < E or it is not None:
                        gathered(s, 3, it)
                    lo_down(D_SP + s, it, by=4)

                body(0)
                for s, it in turns(dve, E, 1, 4):
                    body(s, it)
                rows_t(E - 1)
                rows_down(E - 1)

            def softmaxes(k, kw, bias, scale, dest):
                def finish(n):
                    i = n - 16 * k
                    dve.wait_ge(s_o, n + 1)
                    link(dve.reciprocal(st[:, 40 + n % 2:41 + n % 2], st[:, 36 + n % 2:37 + n % 2]))
                    dve.tensor_scalar(dest(i // 2, i % 2), bank(6 + n % 2)[:, 0:HD], st[:, 40 + n % 2:41 + n % 2],
                                      None, ALU.mult).then_inc(s_fin, 1)

                for i in range(16):
                    n = 16 * k + i
                    w = kw(i % 2)
                    dve.wait_ge(s_ps, n + 1)
                    if n >= 2:
                        dve.wait_ge(s_pt, n - 1)
                    s = s_buf[n % 2][:, 0:w]
                    if bias is None:
                        link(dve.tensor_scalar(s, bank(2 + n % 2)[:, 0:w], scale, None, ALU.mult))
                    else:
                        link(dve.scalar_tensor_tensor(out=s, in0=bank(2 + n % 2)[:, 0:w], scalar=scale,
                                                      in1=bias(i // 2, i % 2), op0=ALU.mult, op1=ALU.add))
                    dve.reduce_max(st[:, 32 + n % 2:33 + n % 2], s, AX, negate=True).then_inc(s_max, 1)
                    if i >= 2:
                        finish(n - 2)
                finish(16 * k + 14)
                finish(16 * k + 15)

            dve.wait_ge(c_silu, 1)
            c_all = c_sil.unsqueeze(2).to_broadcast([P, DC, P])
            link(dve.tensor_copy(xt_hi[:, :, 0:P], c_all))
            dve.tensor_tensor(xt_lo[:, :, 0:P], c_all, xt_hi[:, :, 0:P].bitcast(F32), ALU.subtract).then_inc(c_bc, 1)
            dve.wait_ge(tb_ps, 1)
            dve.tensor_copy(t_bias, bank(0)[0:NH, 0:BX]).then_inc(tb_sb, 1)
            roots(0, [D, D])
            for t in range(N_ADA):
                split_lo(G_ADA + t, 0)
                split_lo(G_ADA + t, 1)
                if t == 5:
                    dve.wait_ge(ada_ev, 4)
                    dve.wait_ge(in_["g1"], 16)
                    link(dve.scalar_tensor_tensor(out=gain1, in0=gain1, scalar=1.0, in1=g1_in,
                                                  op0=ALU.add, op1=ALU.mult))
                    for b in range(TB):
                        link(scaled(h[:, b, :], x[:, b, :], b, gain1))
                    for b in range(TB):
                        ins = dve.tensor_tensor(h[:, b, :], h[:, b, :], shift1, ALU.add)
                    ins.then_inc(h_ready, 1)
            dve.wait_ge(ada_ev, 10)
            dve.wait_ge(in_["g2"], 16)
            dve.scalar_tensor_tensor(out=gain2, in0=gain2, scalar=1.0, in1=g2_in, op0=ALU.add, op1=ALU.mult)
            split_lo(G_WIN, 0)
            split_lo(G_WIN, 1)
            transposed(0)

            def win_out(j):
                dve.wait_ge(M.used_g, 2 * (G_WIN + j) + 2)
                src = bank(5 + 2 * (j % 2))
                if j in (0, 1, 3, 4):
                    dst = (qT, kT)[j % 3][j // 3][:, 2:4, :].rearrange("p m t -> p (m t)")
                    dve.tensor_scalar(dst, src, 0.125 if j % 3 == 0 else 1.0, None, ALU.mult).then_inc(ev_v, 1)
                else:
                    dve.tensor_copy(v_tok[:, 1, (j // 3) * 512:(j // 3 + 1) * 512], src).then_inc(ev_v, 1)

            for j in range(N_WIN):
                if j:
                    split_lo(G_WIN + j, 0)
                    split_lo(G_WIN + j, 1)
                    if j <= 6:
                        win_out(j - 1)

            dve.wait_ge(in_["nw"], 16)
            dve.wait_ge(in_["tw"], 16)
            for half in range(2):
                dve.wait_ge(sb_zc, 4 * half + 4)
                dve.scalar_tensor_tensor(out=l_sb, in0=z_sb, scalar=-1.0, in1=z_sb, op0=ALU.mult, op1=ALU.min)\
                    .then_inc(sb_ab, 1)
                dve.wait_ge(sb_ln, half + 1)
                link(dve.scalar_tensor_tensor(out=l_sb, in0=z_sb, scalar=0.0, in1=l_sb, op0=ALU.max, op1=ALU.add))
                for c in (0, 2):
                    d3 = l_sb.rearrange("p (i c q) -> p i c q", i=4, c=3)[:, :, c, :]
                    ins = dve.tensor_tensor(d3, d3, con[:, C_MASK:C_MASK + P].unsqueeze(1).to_broadcast([P, 4, P]),
                                            ALU.mult)
                ins.then_inc(sb_r, 1)
                for i in range(4):
                    dve.wait_ge(sb_i, 4 * half + i + 1)
                    ins = dve.scalar_tensor_tensor(out=p_sb[:, i * 384:(i + 1) * 384], in0=bank(4 + i)[:, 0:384],
                                                   scalar=-1.0, in1=z_sb[:, i * 384:(i + 1) * 384],
                                                   op0=ALU.mult, op1=ALU.add)
                link(ins)
                for c in (0, 2):
                    d3 = p_sb.rearrange("p (i c q) -> p i c q", i=4, c=3)[:, :, c, :]
                    ins = dve.tensor_tensor(d3, d3, con[:, C_MIN:C_MIN + P].unsqueeze(1).to_broadcast([P, 4, P]),
                                            ALU.min)
                ins.then_inc(sb_t, 1)
                for i in range(2):
                    dve.wait_ge(sb_oh, 2 * half + i + 1)
                    dve.tensor_tensor(xt_lo[:, 2 * half + i, :], bank(i)[:, 0:T],
                                      xt_hi[:, 2 * half + i, :].bitcast(F32), ALU.subtract).then_inc(sb_ol, 1)
            split_lo(G_WB, 0)
            split_lo(G_WB, 1)

            dve.wait_ge(in_["tb"], 16)
            softmaxes(0, lambda b: P * (b + 1), lambda hd, b: mb_bias[:, hd, P * (1 - b):T], 1.0,
                      lambda hd, b: o_mb[:, b, hd * HD:(hd + 1) * HD])
            for q in range(2):
                dve.wait_ge(ot_hi, q + 1)
                hi, lo = (t[:, 4 + 2 * q:6 + 2 * q, :].rearrange("p c t -> p (c t)") for t in (xt_hi, xt_lo))
                dve.tensor_tensor(lo, bank(q), hi.bitcast(F32), ALU.subtract).then_inc(ot_lo, 1)
            split_lo(G_WB + 1, 0)
            split_lo(G_WB + 1, 1)
            split_lo(G_WO, 0)
            dve.wait_ge(M.used_g, 2 * (G_WB + 1) + 2)
            for b in range(TB):
                for n in range(2):
                    i = 2 * b + n
                    hv = h[:, b, n * 512:(n + 1) * 512]
                    tmp = att[:, (i % 2) * 512:(i % 2 + 1) * 512]
                    dve.tensor_tensor(hv, bank(i), sig[:, b, n * 512:(n + 1) * 512], ALU.mult)
                    link(dve.tensor_tensor(tmp, bank(4 + i), sig[:, b, D + n * 512:D + (n + 1) * 512], ALU.mult))
                    ins = dve.tensor_tensor(hv, hv, tmp, ALU.add)
            ins.then_inc(h_ready, 1)
            split_lo(G_WO, 1)
            transposed(1)
            split_lo(G_WO + 1, 0)
            split_lo(G_WO + 1, 1)

            def add_gated(gate, banks, sem_, count):
                dve.wait_ge(sem_, count)
                for b in range(TB):
                    for n in range(2):
                        hv = h[:, b, n * 512:(n + 1) * 512]
                        link(dve.tensor_tensor(hv, bank(banks + 2 * b + n), gate[:, n * 512:(n + 1) * 512], ALU.mult))
                        xv = x[:, b, n * 512:(n + 1) * 512]
                        ins = dve.tensor_tensor(xv, xv, hv, ALU.add)
                ins.then_inc(x_ready, 1)

            add_gated(gate1, 4, M.used_g, 2 * (G_WO + 1) + 2)
            roots(1, [D, D])
            for b in range(TB):
                link(scaled(h[:, b, :], x[:, b, :], b, gain2))
            for b in range(TB):
                ins = dve.tensor_tensor(h[:, b, :], h[:, b, :], shift2, ALU.add)
            ins.then_inc(h_ready, 1)
            transposed(2)

            split_lo(G_SH, 0, True)
            split_lo(G_SH, 1, True)
            dve.wait_ge(rt_sc, 1)
            dve.wait_ge(in_["rbias"], 16)

            def sel01(b):
                return rt[:, (8 + b) * E:(9 + b) * E]

            def weight(b):
                return rt[:, (10 + b) * E:(11 + b) * E]

            def route(b):
                sc = rt[:, b * E:(b + 1) * E]
                ch, cm, sel = (rt[:, i * E:(i + 1) * E] for i in (2, 3, 4))
                top2 = rt[:, 5 * E:6 * E]
                gs, m8, gr = rt[:, 6 * E:6 * E + 12], rt[:, 6 * E + 16:6 * E + 24], rt[:, 6 * E + 32:6 * E + 44]
                pen, tot = rt[:, 7 * E:7 * E + 8], rt[:, 7 * E + 8:7 * E + 10]
                link(dve.tensor_tensor(ch, sc, rbias, ALU.add))
                for i in range(NGRP):
                    ins = dve.max(top2[:, 8 * i:8 * i + 8], ch[:, 8 * i:8 * i + 8])
                link(ins)
                t3 = top2.rearrange("p (g k) -> p g k", g=NGRP)
                dve.tensor_tensor(gs[:, 0:8].unsqueeze(2), t3[:, :, 0:1], t3[:, :, 1:2], ALU.add)
                link(dve.memset(gs[:, 8:12], 3e38))
                link(dve.max(m8, gs))
                link(dve.match_replace(gr, m8, gs, -3e38))
                link(dve.tensor_scalar(pen, gr[:, 0:8], -2e38, BIG, ALU.is_lt, ALU.mult))
                link(dve.tensor_scalar(pen, pen, BIG, None, ALU.subtract))
                link(dve.tensor_tensor(cm.rearrange("p (g k) -> p g k", g=NGRP),
                                       ch.rearrange("p (g k) -> p g k", g=NGRP),
                                       pen.unsqueeze(2).to_broadcast([P, NGRP, 8]), ALU.add))
                link(dve.max(m8, cm))
                link(dve.match_replace(sel, m8, cm, -3e38))
                link(dve.tensor_scalar(sel01(b), sel, -2e38, None, ALU.is_lt))
                link(dve.tensor_tensor(sel, sel01(b), sc, ALU.mult))
                link(dve.reduce_sum(tot[:, 0:1], sel, AX))
                link(dve.reciprocal(tot[:, 1:2], tot[:, 0:1]))
                return dve.tensor_scalar(weight(b), sel, tot[:, 1:2], 2.5, ALU.mult, ALU.mult)

            link(route(0))
            route(1).then_inc(rt_sel, 1)
            gate(M, 0, 0)
            dve.wait_ge(tok_hi, 1)
            for b in range(TB):
                ins = dve.tensor_tensor(tok[1][:, b, :, :], h_chunks[:, b, :, :], tok[0][:, b, :, :].bitcast(F32),
                                        ALU.subtract)
            ins.then_inc(tok_lo, 1)
            dve.wait_ge(rt_pos, 1)
            for b in range(TB):
                pos = bank(7)[:, b * E:(b + 1) * E]
                fits, beyond = rt[:, (12 + b) * E:(13 + b) * E], rt[:, (14 + b) * E:(15 + b) * E]
                row, w, wf = row_of[:, b, :], weight(b), rt[:, (2 + b) * E:(3 + b) * E]
                link(dve.scalar_tensor_tensor(out=fits, in0=pos, scalar=float(CAP), in1=sel01(b),
                                              op0=ALU.is_lt, op1=ALU.mult))
                dve.tensor_tensor(beyond, sel01(b), fits, ALU.subtract)
                dve.tensor_tensor(wf, w, fits, ALU.mult)
                link(dve.scalar_tensor_tensor(out=row, in0=pos, scalar=1.0, in1=fits, op0=ALU.add, op1=ALU.mult))
                dve.tensor_scalar(row, row, 1.0, None, ALU.subtract)
                link(dve.tensor_copy(w_hl[:, b, :, 0:1], wf.unsqueeze(2)))
                dve.tensor_tensor(w_hl[:, b, :, 1:2], wf.unsqueeze(2), w_hl[:, b, :, 0:1].bitcast(F32), ALU.subtract)
                ins = dve.tensor_tensor(w_over[:, b, :], w, wf, ALU.subtract)
            link(ins)
            dve.reduce_sum(st[:, 52:53], rt[:, 14 * E:16 * E], AX).then_inc(rt_cnt, 1)
            dve.wait_ge(rt_tot, 1)
            dve.tensor_copy(over_i[0:1, 0:1], bank(5)[0:1, 0:1]).then_inc(rt_flag, 1)
            sparse_phase()

            def over():
                dve.wait_ge(summed, E)
                for b in range(TB):
                    ins = dve.tensor_tensor(h_chunks[:, b, :, :], tok[0][:, b, :, :].bitcast(F32),
                                            tok[1][:, b, :, :].bitcast(F32), ALU.add)
                ins.then_inc(h_again, 1)
                transposed(0, OV, 4)
                gated_phase("over", w_over)
                dve.wait_ge(OV.used_d, E + 1)

            if_over(dve, over)

            add_gated(gate2, 0, summed, E)
            dve.wait_ge(in_["gains"], 80)
            roots(2, [D, D])
            for b in range(TB):
                ins = scaled(x[:, b, :], x[:, b, :], b, final_g)
            ins.then_inc(x_ready, 1)

            def normed(k, gain):
                roots(k, [D, D])
                for b in range(TB):
                    ins = scaled(h[:, b, :], x[:, b, :], b, gain)
                ins.then_inc(h_ready, 1)

            def add_normed(k, base, gain, factor):
                roots(k, [D, D])
                for b in range(TB):
                    src = ps[base + b][:, :, :].rearrange("p a n -> p (a n)")
                    link(scaled(h[:, b, :], src, b, gain))
                    ins = dve.scalar_tensor_tensor(out=x[:, b, :], in0=h[:, b, :], scalar=factor, in1=x[:, b, :],
                                                   op0=ALU.mult, op1=ALU.add)
                ins.then_inc(x_ready, 1)

            normed(3, pre1)
            transposed(3)
            gated_phase("ff1")
            add_normed(4, 0, post1, 0.5)
            normed(5, mixpre)
            transposed(4)

            def win2_out(j):
                dve.wait_ge(M.used_g, 2 * (G_WIN2 + j) + 2)
                src = bank(5 + 2 * (j % 2))
                if j < 2:
                    dst = (qT2, kT2)[j][:, 2:4, :].rearrange("p m t -> p (m t)")
                    dve.tensor_scalar(dst, src, 0.125 if j == 0 else 1.0, None, ALU.mult).then_inc(ev_v, 1)
                elif j == 2:
                    dve.tensor_copy(v2[:, 1, :], src).then_inc(ev_v, 1)
                else:
                    dve.tensor_copy(small[:, 1, :], src[:, 0:SMALL]).then_inc(ev_v, 1)

            for j in range(4):
                cols = UNIT if j < 3 else 4 * SMALL
                split_lo(G_WIN2 + j, 0, cols=cols)
                split_lo(G_WIN2 + j, 1, cols=cols)
                if j:
                    win2_out(j - 1)
            win2_out(3)
            dve.wait_ge(in_["outg"], 64)
            roots(6, [256, 128, 256, 128])
            for b in range(TB):
                scaled(small[:, b, 0:256], small[:, b, 0:256], 2 * b, qn_g)
                ins = scaled(small[:, b, 256:384], small[:, b, 256:384], 2 * b + 1, kvn_g)
            ins.then_inc(cn_ready, 1)
            dve.wait_ge(na_ready, 2)
            softmaxes(1, lambda b: T, lambda hd, b: na_bias[b][:, hd, :], 1.0,
                      lambda hd, b: h[:, b, hd * HD:(hd + 1) * HD])
            split_lo(G_MLA, 0, cols=2 * QW)
            split_lo(G_MLA, 1, cols=KVW)
            for q in range(2):
                dve.wait_ge(cn_hi, q + 1)
                w = 512 if q == 0 else 256
                hi, lo = (t[:, 2 * q:2 * q + w // T, :].rearrange("p c t -> p (c t)") for t in (xt_hi, xt_lo))
                dve.tensor_tensor(lo, bank(q)[:, 0:w], hi.bitcast(F32), ALU.subtract).then_inc(cn_lo, 1)
            dve.wait_ge(M.used_g, 2 * G_MLA + 2)
            for i in range(4):
                dve.tensor_copy(kv_tok[:, i // 2, (i % 2) * 512:(i % 2 + 1) * 512], bank(4 + i)).then_inc(ev_v, 1)
            dve.wait_ge(ev_a, EV_A[G_MLA])
            dve.wait_ge(ev_v, EV_V[G_MLA])
            for b in range(TB):
                q3 = q_tok[:, b, :].rearrange("p (h n) -> p h n", h=NH)
                k3 = k_full[:, b, :].rearrange("p (h n) -> p h n", h=NH)
                kv3 = kv_tok[:, b, :].rearrange("p (h n) -> p h n", h=NH)
                cos, sin = (con[:, c + 16 * b:c + 16 * b + 16] for c in (C_COS, C_SIN))

                def wide(t):
                    return t.unsqueeze(1).to_broadcast([P, NH, 16])

                tmp = [rope_t[:, i, b, :].rearrange("p (h n) -> p h n", h=NH) for i in range(4)]
                q1, q2 = q3[:, :, 64:80], q3[:, :, 80:96]
                dve.tensor_tensor(tmp[0], q1, wide(cos), ALU.mult)
                dve.tensor_tensor(tmp[1], q2, wide(sin), ALU.mult)
                dve.tensor_tensor(tmp[2], q2, wide(cos), ALU.mult)
                link(dve.tensor_tensor(tmp[3], q1, wide(sin), ALU.mult))
                dve.tensor_tensor(q1, tmp[0], tmp[1], ALU.subtract)
                link(dve.tensor_tensor(q2, tmp[2], tmp[3], ALU.add))
                dve.tensor_copy(k3[:, :, 0:64], kv3[:, :, 0:64])
                k1, k2 = small[:, b, 384:400], small[:, b, 400:416]
                t16 = [rope_t[:, i, b, 0:16] for i in range(4)]
                dve.tensor_tensor(t16[0], k1, cos, ALU.mult)
                dve.tensor_tensor(t16[1], k2, sin, ALU.mult)
                dve.tensor_tensor(t16[2], k2, cos, ALU.mult)
                link(dve.tensor_tensor(t16[3], k1, sin, ALU.mult))
                dve.tensor_tensor(k3[:, :, 64:80], wide(t16[0]), wide(t16[1]), ALU.subtract)
                dve.tensor_tensor(k3[:, :, 80:96], wide(t16[2]), wide(t16[3]), ALU.add).then_inc(roped, 1)
            for q in range(1, 8, 2):
                dve.wait_ge(mt_ps, q + 1)
                dst = (qTm, kTm)[q // 4][0:96, (q % 4) * 2:(q % 4) * 2 + 2, :].rearrange("p h t -> p (h t)")
                dve.tensor_copy(dst, bank(q % 4)[0:96, :]).then_inc(mt_ev_v, 1)
            softmaxes(2, lambda b: T, None, 96.0 ** -0.5, lambda hd, b: h[:, b, 512 + hd * HD:512 + (hd + 1) * HD])
            roots(7, [512] * 4)
            for i in range(4):
                hv = h[:, i // 2, (i % 2) * 512:(i % 2 + 1) * 512]
                ins = scaled(hv, hv, i, outg[:, (i % 2) * 512:(i % 2 + 1) * 512])
            ins.then_inc(h_ready, 1)
            split_lo(G_WO2, 0)
            split_lo(G_WO2, 1)
            transposed(5)
            split_lo(G_WO2 + 1, 0)
            split_lo(G_WO2 + 1, 1)
            add_normed(8, 2, mixpost, 1.0)
            dve.wait_ge(in_["ff2g"], 32)
            normed(9, pre2)
            transposed(6)
            gated_phase("ff2")
            add_normed(10, 0, post2, 0.5)

        @block.tensor
        def _(pe):
            PASSES = ((0, 0), (0, 1), (1, 0))

            def transposes(k, S=M, base=0):
                if S is M:
                    pe.wait_ge(h_ready, k + 1)
                for q in range(4):
                    for c in (2 * q, 2 * q + 1):
                        for b in range(TB):
                            o = ((c % 2) * TB + b) * P
                            ins = pe.transpose(bank(base + q)[:, o:o + P], h[:, b, c:D:DC], ident)
                    ins.then_inc(S.xt_ps, 1)

            def rows(out_, b, cs, w, n, start, stop):
                last = None
                for i, c in enumerate(cs):
                    for k, (s, m) in enumerate(PASSES):
                        last = pe.matmul(out_, (xt_hi, xt_lo)[s][:, c, b * P:(b + 1) * P], w((g_hi, g_lo)[m], i),
                                         start=start and i == 0 and k == 0,
                                         stop=stop and i == len(cs) - 1 and k == 2, skip_group_check=True)
                return last

            def dense(g, banks, n=512):
                for u in range(2):
                    pe.wait_ge(M.lo_g, 2 * g + u + 1)
                    for b in range(TB):
                        last = rows(bank(banks[b])[:, 0:n], b, range(4 * u, 4 * u + 4),
                                    lambda t, i: t[:, u, i * n:(i + 1) * n], n, u == 0, u == 1)
                    last.then_inc(M.used_g, 1)

            def features(g, b0):
                for u in range(2):
                    pe.wait_ge(M.lo_g, 2 * g + u + 1)
                    for m in range(4):
                        for c in range(4):
                            for k, (s, w) in enumerate(PASSES):
                                last = pe.matmul(bank(b0 + m // 2)[:, (m % 2) * T:(m % 2 + 1) * T],
                                                 (g_hi, g_lo)[w][:, u, c * 512 + m * P:c * 512 + (m + 1) * P],
                                                 (xt_hi, xt_lo)[s][:, 4 * u + c, :],
                                                 start=u == 0 and c == 0 and k == 0 and m % 2 == 0,
                                                 stop=u == 1 and c == 3 and k == 2, skip_group_check=True)
                    last.then_inc(M.used_g, 1)

            def gate_up(S, g, q, u, it=None):
                pe.wait_ge(S.lo_g, at(2 * g + u + 1, it, 4))
                if u == 0 and q:
                    pe.wait_ge(S.gated, at(2 * q, it, 4))
                for b in range(TB):
                    last = rows(bank(4 + b), b, range(4 * u, 4 * u + 4),
                                lambda t, i: t[:, u, i * 512:(i + 1) * 512], 512, u == 0, u == 1)
                last.then_inc(S.used_g, 1)

            def turn(S, q, it=None):
                pe.wait_ge(S.gated, at(2 * q + 2, it, 4))
                for c in range(2):
                    for b in range(TB):
                        o = (c * TB + b) * P
                        last = pe.transpose(bank(6)[:, o:o + P], a_sb[:, b, c:FF:2], ident)
                last.then_inc(S.tr_done, 1)

            def down(S, d, b, it=None, stop=False):
                pe.wait_ge(S.at_lo, at(d + 1, it, 2))
                pe.wait_ge(S.lo_d, at(d + 1, it, 2))
                for m in range(2):
                    for c in range(2):
                        for k, (i, w) in enumerate(PASSES):
                            last = pe.matmul(bank(2 * b + m), (at_hi, at_lo)[i][:, c, b * P:(b + 1) * P],
                                             (d_hi, d_lo)[w][:, c * D + m * 512:c * D + (m + 1) * 512],
                                             start=False, stop=stop and c == 1 and k == 2, skip_group_check=True)
                if b == TB - 1:
                    last.then_inc(S.used_d, 1)

            def zero_sums():
                for i in range(4):
                    last = pe.matmul(bank(i), zeros[:, 0:P], zeros[:, :], start=True, stop=False,
                                     skip_group_check=True)
                return last

            def gated_phase(name):
                S, g0, d0, q0, n = PHASES[name]
                gate_up(S, g0, q0, 0)
                gate_up(S, g0, q0, 1)
                for s, it in turns(pe, n):
                    if s + 1 < n:
                        gate_up(S, g0 + s + 1, q0 + s + 1, 0, it)
                    turn(S, q0 + s, it)
                    if s + 1 < n:
                        gate_up(S, g0 + s + 1, q0 + s + 1, 1, it)
                    for b in range(TB):
                        down(S, d0 + s, b, it, stop=s == n - 1)

            def sparse_phase():
                def fill(s, k, it=None):
                    pair, c = s // 2 + 1, 4 * (s % 2) + k - k % 2
                    n = 8 + 4 * s + k
                    if k % 2:
                        pe.wait_ge(xg_a, at((n + 1) // 2, it, 8))
                    elif n:
                        pe.wait_ge(xg_v, at(n // 2, it, 8))
                    if s % 2 == 0 and k == 0:
                        pe.wait_ge(picked, at(pair + 1, it, 2))
                    for i in range(2):
                        for b in range(TB):
                            last = pe.matmul(bank(7)[:, i * 2 * CAP:(i + 1) * 2 * CAP], tok[k % 2][:, b, c + i, :],
                                             pick[:, pair % 2, b, :, :].rearrange("p e r -> p (e r)"),
                                             start=b == 0, stop=b == TB - 1)
                    last.then_inc(ga_ps, 1)

                def rows_t(s, it=None):
                    pe.wait_ge(sp_gate, at(s + 1, it, 4))
                    if s:
                        pe.wait_ge(y_v, at(2 * s, it, 8))
                    for c in range(2):
                        last = pe.transpose(bank(5)[:, c * CAP:(c + 1) * CAP], a_sb[0:CAP, 0, c:FF:2],
                                            ident[0:CAP, 0:CAP])
                    last.then_inc(M.tr_done, 1)

                def rows_down(s, it=None):
                    pe.wait_ge(M.at_lo, at(D_SP + s + 1, it, 4))
                    pe.wait_ge(M.lo_d, at(D_SP + s + 1, it, 4))
                    for m in range(2):
                        for c in range(2):
                            for k, (i, w) in enumerate(PASSES):
                                last = pe.matmul(bank(5 + m)[0:CAP, :], (at_hi, at_lo)[i][:, c, 0:CAP],
                                                 (d_hi, d_lo)[w][:, c * D + m * 512:c * D + (m + 1) * 512],
                                                 start=c == 0 and k == 0, stop=c == 1 and k == 2)
                        last.then_inc(M.used_d if m else y_ps, 1)

                def scatter(s, it=None):
                    for m in range(2):
                        pe.wait_ge(y_v, at(2 * s + m + 1, it, 8))
                        for b in range(TB):
                            for k, t in enumerate((y_hi, y_lo)):
                                last = pe.matmul(bank(2 * b + m), pickT[0:CAP, s % 2, b * P:(b + 1) * P],
                                                 t[0:CAP, m * 512:(m + 1) * 512], start=False,
                                                 stop=it is None and s == E - 1 and k == 1, skip_group_check=True)
                    last.then_inc(summed, 1)

                def body(s, it=None):
                    g = G_SP + s
                    more = s + 2 < E or it is not None
                    for u in range(2):
                        pe.wait_ge(M.lo_g, at(2 * g + u + 1, it, 8))
                        if s % 2 == 0:
                            pe.wait_ge(xg_a, at(2 * s + 2 + 2 * u, it, 8))
                            pe.wait_ge(xg_v, at(2 * s + 2 + 2 * u, it, 8))
                        if u == 0:
                            if s:
                                pe.wait_ge(sp_gate, at(s, it, 4))
                        for i in range(4):
                            for k, (j, w) in enumerate(PASSES):
                                last = pe.matmul(bank(4)[0:CAP, :], (xg_hi, xg_lo)[j][:, s // 2 % 2, 4 * u + i, s % 2, :],
                                                 (g_hi, g_lo)[w][:, u, i * 512:(i + 1) * 512],
                                                 start=u == 0 and i == 0 and k == 0, stop=u == 1 and i == 3 and k == 2)
                        last.then_inc(M.used_g, 1)
                        if u == 0:
                            if s and (s + 1 < E or it is not None):
                                fill(s - 1, 3, it)
                            if s >= 2:
                                scatter(s - 2, it)
                            if s:
                                rows_t(s - 1, it)
                            if s:
                                pe.wait_ge(pt_sb, at(s, it, 4))
                            for b in range(TB):
                                pe.transpose(bank(6)[0:CAP, b * P:(b + 1) * P],
                                             pick[:, s // 2 % 2, b, s % 2, :].bitcast(F32), ident)
                            for b in range(TB):
                                w = w_hl[:, b, s, :] if it is None else \
                                    w_hl[:, b, bass.ds(it * 4 + s, 1), :].rearrange("p e k -> p (e k)")
                                last = pe.matmul(bank(6)[0:CAP, T:T + 2], pick[:, s // 2 % 2, b, s % 2, :], w,
                                                 start=b == 0, stop=b == TB - 1)
                            last.then_inc(pt_ps, 1)
                        if more:
                            fill(s, u, it)
                    if s:
                        pe.wait_ge(pt_sb, at(s + 1, it, 4))
                        rows_down(s - 1, it)
                    if more:
                        fill(s, 2, it)

                pe.wait_ge(tok_lo, 1)
                for b in range(TB):
                    down(M, D_SH, b)
                for s in (-2, -1):
                    for k in range(4):
                        fill(s, k)
                body(0)
                body(1)
                for s, it in turns(pe, E, 2, 4, 2):
                    body(s, it)
                scatter(E - 2)
                rows_t(E - 1)
                rows_down(E - 1)
                scatter(E - 1)

            def softmaxes(k, kw, scores, values):
                def score(n):
                    i = n - 16 * k
                    if i >= 2:
                        pe.wait_ge(s_max, n - 1)
                    lhsT, rhs = scores(i // 2, i % 2)
                    pe.matmul(bank(2 + n % 2)[:, 0:kw(i % 2)], lhsT, rhs, start=True, stop=True).then_inc(s_ps, 1)

                def turn(n):
                    i = n - 16 * k
                    pe.wait_ge(s_exp, n + 1)
                    if i >= 2:
                        pe.wait_ge(s_ptc, n - 1)
                    for c in range(kw(i % 2) // P):
                        last = pe.transpose(bank(4 + n % 2)[:, c * P:(c + 1) * P], s_buf[n % 2][:, c * P:(c + 1) * P],
                                            ident)
                    last.then_inc(s_pt, 1)

                def output(n):
                    i = n - 16 * k
                    pe.wait_ge(s_ptc, n + 1)
                    if i >= 2:
                        pe.wait_ge(s_fin, n - 1)
                    cs = kw(i % 2) // P
                    for c in range(cs):
                        last = pe.matmul(bank(6 + n % 2)[:, 0:HD], pT_sb[n % 2][:, c, :], values(i // 2, c),
                                         start=c == 0, stop=c == cs - 1)
                    last.then_inc(s_o, 1)

                score(16 * k)
                for i in range(16):
                    if i < 15:
                        score(16 * k + i + 1)
                    turn(16 * k + i)
                    if i:
                        output(16 * k + i - 1)
                output(16 * k + 15)

            pe.wait_ge(in_["relb"], 16)
            pe.wait_ge(in_["bucket"], 16)
            pe.wait_ge(set_up, 3)
            pe.matmul(bank(0)[0:NH, 0:BX], relb_in, bucket_in, start=True, stop=True).then_inc(tb_ps, 1)
            pe.wait_ge(in_["bada"], 16)
            pe.wait_ge(c_bc, 1)
            for t in range(N_ADA):
                out_ = bank(4 + t % 4)
                if t >= 4:
                    pe.wait_ge(ada_ev, t - 3)
                pe.matmul(out_, ones[0:1, :], b_ada_row[0:1, t * 512:(t + 1) * 512], start=True, stop=False,
                          skip_group_check=True)
                for u in range(2):
                    pe.wait_ge(M.lo_g, 2 * t + u + 1)
                    last = rows(out_, 0, range(4 * u, 4 * u + 4), lambda w, i: w[:, u, i * 512:(i + 1) * 512],
                                512, False, u == 1)
                    last.then_inc(M.used_g, 1)

            pe.wait_ge(in_["con"], 16)
            pe.wait_ge(tb_sb, 1)
            transposes(0)
            pe.wait_ge(M.xt_lo, 4)
            pe.wait_ge(ada_ev, N_ADA)
            for j in range(N_WIN):
                b0 = 4 + 2 * (j % 2)
                if j >= 2:
                    pe.wait_ge(ev_a, EV_A[G_WIN + j - 2])
                    pe.wait_ge(ev_v, EV_V[G_WIN + j - 2])
                if j in (0, 1, 3, 4):
                    features(G_WIN + j, b0)
                else:
                    dense(G_WIN + j, (b0, b0 + 1))
            pe.wait_ge(ev_a, EV_A[G_WIN + N_WIN - 1])
            pe.wait_ge(ev_v, EV_V[G_WIN + N_WIN - 1])

            for half in range(2):
                if half:
                    pe.wait_ge(sb_ol, 2)
                for i in range(4):
                    hd = 4 * half + i
                    r, m = slice((hd % 2) * 64, (hd % 2) * 64 + 64), hd // 2
                    pe.matmul(bank(i)[:, 0:T], kT[0][r, m, 0:P], qT[0][r, m, :], start=True, stop=True)
                    pe.matmul(bank(i)[:, T:384], kT[0][r, m, P:T], qT[0][r, m, P:T], start=True, stop=True)\
                        .then_inc(sb_z, 1)
                pe.wait_ge(sb_r, half + 1)
                for i in range(4):
                    r0, r1 = l_sb[:, i * 384:i * 384 + T], l_sb[:, i * 384 + T:(i + 1) * 384]
                    pe.matmul(bank(4 + i)[:, T:384], tri, r1, start=True, stop=True)
                    pe.matmul(bank(4 + i)[:, 0:T], tri, r0, start=True, stop=False, skip_group_check=True)
                    pe.matmul(bank(4 + i)[:, P:T], ones[:, :], r1, start=False, stop=True, skip_group_check=True)\
                        .then_inc(sb_i, 1)
                pe.wait_ge(sb_a, half + 1)
                for i in range(4):
                    hd = 4 * half + i
                    out_ = bank(i // 2)[(hd % 2) * 64:(hd % 2) * 64 + 64, :]
                    vs = [v_tok[:, b, hd * HD:(hd + 1) * HD] for b in range(TB)]
                    pe.matmul(out_[:, 0:T], vs[0], p_sb[:, i * 384:i * 384 + T], start=True, stop=False,
                              skip_group_check=True)
                    last = pe.matmul(out_[:, P:T], vs[1], p_sb[:, i * 384 + T:(i + 1) * 384], start=False, stop=True,
                                     skip_group_check=True)
                    if i % 2:
                        last.then_inc(sb_o, 1)

            def mb_scores(hd, b):
                r, m = slice((hd % 2) * 64, (hd % 2) * 64 + 64), hd // 2
                return qT[1][r, m, b * P:(b + 1) * P], kT[1][r, m, 0:P * (b + 1)]

            softmaxes(0, lambda b: P * (b + 1), mb_scores,
                      lambda hd, c: v_tok[:, c, 512 + hd * HD:512 + (hd + 1) * HD])
            pe.wait_ge(s_fin, 16)
            pe.wait_ge(sb_ol, 4)
            for q in range(2):
                for m in (2 * q, 2 * q + 1):
                    for b in range(TB):
                        o = ((m % 2) * TB + b) * P
                        last = pe.transpose(bank(q)[:, o:o + P], o_mb[:, b, m * P:(m + 1) * P], ident)
                last.then_inc(ot_ps, 1)
            pe.wait_ge(ot_lo, 2)
            for t in range(2):
                for u in range(2):
                    pe.wait_ge(M.lo_g, 2 * (G_WB + t) + u + 1)
                    for b in range(TB):
                        for n in range(2):
                            last = rows(bank(4 * t + 2 * b + n), b, (4 * t + 2 * u, 4 * t + 2 * u + 1),
                                        lambda w, i: w[:, u, i * D + n * 512:i * D + (n + 1) * 512], 512,
                                        u == 0, u == 1)
                    last.then_inc(M.used_g, 1)
            transposes(1)
            pe.wait_ge(M.xt_lo, 8)
            for i in range(2):
                dense(G_WO + i, (4 + i, 6 + i))
            transposes(2)
            pe.wait_ge(M.xt_lo, 12)
            pe.wait_ge(in_["wrt"], 16)
            for b in range(TB):
                for c in range(DC):
                    for k, t in enumerate((xt_hi, xt_lo)):
                        last = pe.matmul(bank(7)[:, b * E:(b + 1) * E], t[:, c, b * P:(b + 1) * P].bitcast(F32),
                                         w_rt[:, c, :], start=c == 0 and k == 0, stop=c == DC - 1 and k == 1)
            last.then_inc(rt_ps, 1)
            zero_sums().then_inc(M.used_d, 1)
            gate_up(M, G_SH, 0, 0)
            gate_up(M, G_SH, 0, 1)
            pe.wait_ge(rt_sel, 1)
            before = con[:, C_MASK:C_MASK + P]
            pe.matmul(bank(7)[:, 0:E], before, rt[:, 8 * E:9 * E], start=True, stop=True)
            pe.matmul(bank(7)[:, E:2 * E], before, rt[:, 9 * E:10 * E], start=True, stop=False)
            pe.matmul(bank(7)[:, E:2 * E], ones[:, :], rt[:, 8 * E:9 * E], start=False, stop=True).then_inc(rt_pos, 1)
            turn(M, 0)
            pe.wait_ge(rt_cnt, 1)
            pe.matmul(bank(5)[0:1, 0:1], st[:, 52:53], ones[:, 0:1], start=True, stop=True).then_inc(rt_tot, 1)
            pe.wait_ge(rt_flag, 1)
            sparse_phase()

            def over():
                pe.wait_ge(h_again, 1)
                transposes(0, OV, 4)
                pe.wait_ge(OV.xt_lo, 4)
                pe.sem_inc(OV.used_d, 1)
                gated_phase("over")
                pe.wait_ge(OV.used_d, E + 1)

            if_over(pe, over)
            transposes(3)
            pe.wait_ge(M.xt_lo, 16)
            zero_sums()
            gated_phase("ff1")
            transposes(4)
            pe.wait_ge(M.xt_lo, 20)
            for j in range(4):
                b0 = 4 + 2 * (j % 2)
                if j >= 2:
                    pe.wait_ge(ev_a, EV_A[G_WIN2 + j - 2])
                    pe.wait_ge(ev_v, EV_V[G_WIN2 + j - 2])
                if j < 2:
                    features(G_WIN2 + j, b0)
                else:
                    dense(G_WIN2 + j, (b0, b0 + 1), 512 if j == 2 else SMALL)
            pe.wait_ge(ev_a, EV_A[G_WIN2 + 3])
            pe.wait_ge(ev_v, EV_V[G_WIN2 + 3])

            def na_scores(hd, b):
                r, m = slice((hd % 2) * 64, (hd % 2) * 64 + 64), hd // 2
                return qT2[r, m, b * P:(b + 1) * P], kT2[r, m, :]

            softmaxes(1, lambda b: T, na_scores, lambda hd, c: v2[:, c, hd * HD:(hd + 1) * HD])
            pe.wait_ge(cn_ready, 1)
            for q in range(2):
                for c in range(2 * q, min(2 * q + 2, 3)):
                    for b in range(TB):
                        o = ((c % 2) * TB + b) * P
                        last = pe.transpose(bank(q)[:, o:o + P], small[:, b, c * P:(c + 1) * P], ident)
                last.then_inc(cn_ps, 1)
            pe.wait_ge(cn_lo, 2)
            pe.wait_ge(s_fin, 32)
            for u, (base, cs, step, n) in enumerate(((0, (0, 1), QW, 384), (4, (2,), KVW, 512))):
                pe.wait_ge(M.lo_g, 2 * G_MLA + u + 1)
                for b in range(TB):
                    for j in range(2):
                        last = rows(bank(base + 2 * b + j)[:, 0:n], b, cs,
                                    lambda w, i: w[:, u, i * step + j * n:i * step + (j + 1) * n], n, True, True)
                last.then_inc(M.used_g, 1)
            pe.wait_ge(roped, 2)
            for q in range(8):
                src = (q_tok, k_full)[q // 4]
                if q >= 4:
                    pe.wait_ge((mt_ev_a, mt_ev_v)[q % 2], (q - 4) // 2 + 1)
                for j in range(2):
                    hd = (q % 4) * 2 + j
                    for b in range(TB):
                        o = (j * TB + b) * P
                        last = pe.transpose(bank(q % 4)[0:96, o:o + P], src[:, b, hd * 96:(hd + 1) * 96], ident)
                last.then_inc(mt_ps, 1)
            pe.wait_ge(mt_ev_a, 4)
            pe.wait_ge(mt_ev_v, 4)
            softmaxes(2, lambda b: T, lambda hd, b: (qTm[0:96, hd, b * P:(b + 1) * P], kTm[0:96, hd, :]),
                      lambda hd, c: kv_tok[:, c, hd * 128 + 64:hd * 128 + 128])
            transposes(5)
            pe.wait_ge(M.xt_lo, 24)
            for i in range(2):
                dense(G_WO2 + i, (4 + i, 6 + i))
            transposes(6)
            pe.wait_ge(M.xt_lo, 28)
            zero_sums()
            gated_phase("ff2")


def distance_buckets():
    dist = 255 - np.arange(BX)
    n = np.maximum(dist, 0)
    large = 16 + (np.log(np.maximum(n, 1).astype(np.float32) / np.float32(16)) / np.float32(math.log(8.0))
                  * np.float32(16)).astype(np.int32)
    bucket = np.where(n < 16, n, np.minimum(large, 31))
    rows = np.zeros((33, BX), np.float32)
    rows[bucket, np.arange(BX)] = dist >= 0
    rows[32] = np.where(dist >= 0, 0.0, -BIG)
    return rows


def constants():
    con = np.zeros((P, C_END), np.float32)
    i = np.arange(P)
    con[:, C_ID:C_ID + P] = np.eye(P)
    con[:, C_TRI:C_TRI + P] = i[:, None] >= i[None, :]
    past = i[:, None] < i[None, :]
    con[:, C_MASK:C_MASK + P] = past
    con[:, C_MIN:C_MIN + P] = np.where(past, BIG, -BIG)
    c = np.arange(64)
    first = np.clip(c - 8, 0, 48)[:, None]
    inside = (c[None, :] >= first) & (c[None, :] < first + 16)
    con[:, C_IOTA:C_IOTA + P] = i[None, :]
    con[:, C_NA:C_NA + 64] = np.tile(np.where(inside, 0.0, -BIG), (2, 1))
    freq = (1.0 / (np.float32(10000.0) ** (np.arange(8, dtype=np.float32) / np.float32(8)))).astype(np.float32)
    t = np.arange(T)
    ang = np.concatenate([(t // 64).astype(np.float32)[:, None] * freq, (t % 64).astype(np.float32)[:, None] * freq], 1)
    for b in range(TB):
        con[:, C_COS + 16 * b:C_COS + 16 * (b + 1)] = np.cos(ang[b * P:(b + 1) * P])
        con[:, C_SIN + 16 * b:C_SIN + 16 * (b + 1)] = np.sin(ang[b * P:(b + 1) * P])
    return con


INPUTS = ["x", "c", "norm1_g", "norm2_g", "w_ada", "b_ada", "w_in", "w_branch_sb", "w_branch_mb", "w_out", "w_router",
          "router_bias", "w_gate_e", "w_up_e", "w_down_e", "w_gate_sh", "w_up_sh", "w_down_sh", "final_g",
          "ffn1_pre_g_2", "ffn1_w_gu_2", "ffn1_w_down_2", "ffn1_post_g_2", "mix_pre_g_2", "w_in_2", "na_rpb_2",
          "mla_q_norm_g_2", "mla_w_uq_2", "mla_kv_norm_g_2", "mla_w_ukv_2", "na_out_norm_g_2", "mla_out_norm_g_2",
          "w_out_2", "mix_post_g_2", "ffn2_pre_g_2", "ffn2_w_gu_2", "ffn2_w_down_2", "ffn2_post_g_2"]


def kernel(**inputs):
    from concourse import bacc
    from concourse.bass_utils import run_bass_kernel_spmd

    nc = bacc.Bacc("TRN2", target_bir_lowering=False, num_devices=1)
    arrays = {n: np.ascontiguousarray(inputs[n]) for n in INPUTS}
    arrays["rel_bias_t"] = np.ascontiguousarray(np.asarray(inputs["rel_bias"]).T)
    arrays["con"] = constants()
    arrays["buckets"] = distance_buckets()
    a = {n: nc.dram_tensor("in_" + n, v.shape, mybir.dt.from_np(v.dtype), kind="ExternalInput").ap()
         for n, v in arrays.items()}
    out = nc.dram_tensor("out", (1, T, D), F32, kind="ExternalOutput").ap()
    build(nc, a, out)
    r = run_bass_kernel_spmd(nc, [{"in_" + n: v for n, v in arrays.items()}], core_ids=[0])
    return r.results[0]["out"]
```

```python
import math
from contextlib import ExitStack

import concourse.bass as bass
import numpy as np
from concourse import mybir

ALU = mybir.AluOpType
ACT = mybir.ActivationFunctionType
F32 = mybir.dt.float32
F32R = mybir.dt.float32r
BF16 = mybir.dt.bfloat16
AX = mybir.AxisListType.X

P = 128
T = 256
TB = T // P
D = 1024
DC = D // P
HD = 64
NH = 8
E = 64
NGRP = 8
FF = 256
D_FF = 2816
EPS = 1e-6
BIG = 1e30
QW = 768
KVW = 1024
SMALL = 416
UNIT = 2048

N_ADA, N_WIN, N_FF = 12, 10, D_FF // FF
G_ADA = 0
G_WIN = G_ADA + N_ADA
G_WB = G_WIN + N_WIN
G_WO = G_WB + 2
G_SH = G_WO + 2
G_SP = G_SH + 1
G_FF1 = G_SP + E
G_WIN2 = G_FF1 + N_FF
G_MLA = G_WIN2 + 4
G_WO2 = G_MLA + 1
G_FF2 = G_WO2 + 2
D_SH, D_SP, D_FF1, D_FF2 = 0, 1, E + 1, E + 1 + N_FF
CAP = 96

C_ID, C_TRI, C_MASK, C_MIN, C_NA, C_COS, C_SIN, C_IOTA, C_END = 0, 128, 256, 384, 512, 576, 608, 640, 768
BX = 384
NR = 7 * 128


def at(const, it, per):
    return const if it is None else it * per + const


def build(nc, a, out):
    ctx = ExitStack()
    with ctx:
        def sb(name, shape, dt=F32):
            return ctx.enter_context(nc.sbuf_tensor(name, shape, dt))

        def sem(name):
            return ctx.enter_context(nc.semaphore(name))

        raw_g = sb("raw_g", [P, 2, 2 * UNIT])
        raw_d = sb("raw_d", [P, 2, UNIT])
        g_hi = sb("g_hi", [P, 2, UNIT], F32R)
        g_lo = sb("g_lo", [P, 2, UNIT], F32R)
        d_hi = sb("d_hi", [P, UNIT], F32R)
        d_lo = sb("d_lo", [P, UNIT], F32R)
        xt_hi = sb("xt_hi", [P, DC, T], F32R)
        xt_lo = sb("xt_lo", [P, DC, T], F32R)
        at_hi = sb("at_hi", [P, 2, T], F32R)
        at_lo = sb("at_lo", [P, 2, T], F32R)
        x = sb("x_res", [P, TB, D])
        h = sb("h_tok", [P, TB, D])
        h_end = nc.sbuf_base
        att = sb("att", [P, 3072])
        att_end = nc.sbuf_base
        arena = sb("arena", [P, 14 * 1024])
        arena_end = nc.sbuf_base
        con = sb("con", [P, C_END])
        ones = sb("ones", [P, P])
        zeros = sb("zeros", [P, 512], BF16)
        over_i = sb("over_i", [1, 4], mybir.dt.int32)
        st = sb("stats", [P, 64])

        def lay(base, end, *wanted):
            made = []
            for name, shape in wanted:
                made.append(nc.alloc_sbuf_tensor_at(name, shape, F32R, offset=base))
                base += 4 * int(np.prod(shape[1:]))
            assert base <= end
            return made

        arena_at = arena_end - 4 * 14 * 1024
        xg_shape = [P, 2, DC, 2, CAP]
        xg_lo, = lay(att_end - 4 * 3072, att_end, ("xg_lo", xg_shape))
        y_hi, y_lo = lay(h_end - 4 * TB * D, h_end, ("y_hi", [P, D]), ("y_lo", [P, D]))
        xg_hi, pick, pickT, w_hl = lay(arena_at, arena_at + 20 * 1024, ("xg_hi", xg_shape),
                                       ("pick", [P, 2, TB, 2, CAP]),
                                       ("pickT", [P, 2, T]),
                                       ("w_hl", [P, TB, E, 2]))

        K = 256

        def area(kib, n):
            return arena[:, int(kib * K):int(kib * K) + n]

        shift1, gain1 = area(0, D), area(4, D)
        v_tok = area(0, TB * D).rearrange("p (b n) -> p b n", b=TB)
        gate1, shift2, gain2, gate2 = area(8, D), area(12, D), area(16, D), area(20, D)
        b_ada_row = area(24, 6 * D)
        g1_in, g2_in = area(48, D), area(52, D)
        qT, kT = ([area(24 + 4 * i, 4 * T).rearrange("p (m t) -> p m t", m=4) for i in (0, 2)],
                  [area(28 + 4 * i, 4 * T).rearrange("p (m t) -> p m t", m=4) for i in (0, 2)])
        sig = area(40, TB * 2 * D).rearrange("p (b n) -> p b n", b=TB)
        mb_bias = raw_d[:, 1, :].rearrange("p (h k) -> p h k", h=NH)
        a_sb = area(24, 2 * FF).rearrange("p (b n) -> p b n", b=TB)
        silu = area(26, 2 * FF).rearrange("p (b n) -> p b n", b=TB)
        w_rt = area(28, DC * E).rearrange("p (c e) -> p c e", c=DC)
        rt = area(30, 4 * E * 4)
        w_over = area(34, TB * E).rearrange("p (b e) -> p b e", b=TB)
        row_of = area(34.5, TB * E).rearrange("p (b e) -> p b e", b=TB)
        rbias = area(35, E)
        w_rt_hl = [t[:, :, :].rearrange("p c t -> p (c t)").rearrange("p (c e) -> p c e", c=DC) for t in (at_hi, at_lo)]
        final_g, pre1, post1 = area(36, D), area(40, D), area(44, D)
        mixpre, mixpost = area(48, D), area(52, D)
        outg = area(12, D)
        qn_g, kvn_g = area(16, 256), area(17, 128)
        pre2, post2 = area(0, D), area(8, D)
        na_bias = [area(0, NH * T).rearrange("p (h k) -> p h k", h=NH),
                   att[:, 1024:3072].rearrange("p (h k) -> p h k", h=NH)]
        v2 = area(8, TB * 512).rearrange("p (b n) -> p b n", b=TB)
        small = area(18, TB * SMALL).rearrange("p (b n) -> p b n", b=TB)
        qT2 = area(28, 4 * T).rearrange("p (m t) -> p m t", m=4)
        kT2 = area(32, 4 * T).rearrange("p (m t) -> p m t", m=4)
        q_tok = area(36, TB * QW).rearrange("p (b n) -> p b n", b=TB)
        kv_tok = area(42, TB * KVW).rearrange("p (b n) -> p b n", b=TB)
        k_full = area(28, TB * QW).rearrange("p (b n) -> p b n", b=TB)
        qTm = area(0, NH * T).rearrange("p (h t) -> p h t", h=NH)
        kTm = att[:, 1024:3072].rearrange("p (h t) -> p h t", h=NH)
        rope_t = area(24, 4 * TB * NH * 16).rearrange("p (i b n) -> p i b n", i=4, b=TB)

        SB_OUT = (0, 2, 0, 1)

        def of_group(t, g):
            return t[:, g % 2 * 768:(g % 2 + 1) * 768]

        z_sb = h[:, :, :].rearrange("p b n -> p (b n)")[:, 0:4 * 384]
        l_sb = att[:, 0:1536]
        p_sb = att[:, 1536:3072]
        s_buf = [att[:, i * 2 * T:(i + 1) * 2 * T].rearrange("p (h k) -> p h k", h=2) for i in range(2)]

        def pT_sb(k, n):
            return (area(24, 4 * T) if k else att[:, 1024:2048])[:, (n % 2) * 2 * T:(n % 2 + 1) * 2 * T]

        def pair_heads(hp):
            return 4 * (hp // 2) + hp % 2, 4 * (hp // 2) + hp % 2 + 2

        def of_pair(t, hp):
            first = pair_heads(hp)[0]
            return t.rearrange("p (h d) -> p h d", h=NH)[:, first:first + 3:2, :]

        o_mb = att[:, 2048:3072].rearrange("p (b n) -> p b n", b=TB)
        relb_in, bucket_in = att[0:33, 0:NH], att[0:33, 16:16 + BX]
        t_bias = att[0:NH, 512:512 + BX]
        rpb_pad = raw_d[0:NH, 0, 0:NR]
        c_col, c_sil = st[:, 0:8], st[:, 8:16]

        ps = [ctx.enter_context(nc.psum_tensor(f"bank{i}_{j}", [P, 2, 512], F32))
              for i, j in ((0, 1), (2, 3), (4, 5), (6, 7))]

        def bank(i):
            return ps[i // 2][:, i % 2, :]

        ident = con[:, C_ID:C_ID + P]
        tri = con[:, C_TRI:C_TRI + P]

        t_dram = nc.dram_tensor("t_scratch", (P, NH, BX), F32, kind="Internal").ap()
        n_dram = nc.dram_tensor("n_scratch", (64, NH, NR), F32, kind="Internal").ap()

        class Stream:

            def __init__(self, tag):
                self.landed_g = [[sem(f"{tag}landed_g{i}{j}") for j in range(2)] for i in range(2)]
                self.landed_d = [sem(tag + "landed_d0"), sem(tag + "landed_d1")]
                self.hi_g, self.lo_g, self.used_g = sem(tag + "hi_g"), sem(tag + "lo_g"), sem(tag + "used_g")
                self.hi_d, self.lo_d, self.used_d = sem(tag + "hi_d"), sem(tag + "lo_d"), sem(tag + "used_d")
                self.silu_done, self.gated, self.tr_done = sem(tag + "silu"), sem(tag + "gated"), sem(tag + "tr")
                self.at_hi, self.at_lo = sem(tag + "at_hi"), sem(tag + "at_lo")
                self.xt_ps, self.xt_hi, self.xt_lo = sem(tag + "xt_ps"), sem(tag + "xt_hi"), sem(tag + "xt_lo")

        M, OV = Stream("m_"), Stream("o_")
        h_ready, x_ready = sem("h_ready"), sem("x_ready")
        in_ = {n: sem("in_" + n) for n in ("c", "x", "con", "bada", "g1", "g2", "relb", "bucket", "rpb",
                                           "tb", "nb", "tw", "nw", "wrt", "rbias", "gains", "post",
                                           "outg", "ff2g")}
        chain_v, chain_a, chain_p = sem("chain_v"), sem("chain_a"), sem("chain_p")
        set_up = sem("set_up")
        c_silu, c_bc = sem("c_silu"), sem("c_bc")
        ada_ev = sem("ada_ev")
        tb_ps, tb_sb = sem("tb_ps"), sem("tb_sb")
        ev_a, ev_v = sem("ev_a"), sem("ev_v")
        ss_a, root_p = sem("ss_a"), sem("root_p")
        sb_z, sb_zc, sb_ab, sb_ln, sb_r = sem("sb_z"), sem("sb_zc"), sem("sb_ab"), sem("sb_ln"), sem("sb_r")
        sb_i, sb_t, sb_a, sb_o, sb_oh, sb_ol = (sem("sb_i"), sem("sb_t"), sem("sb_a"), sem("sb_o"),
                                                sem("sb_oh"), sem("sb_ol"))
        s_ps, s_max, s_exp, s_pt, s_ptc, s_o, s_fin = (sem("s_ps"), sem("s_max"), sem("s_exp"),
                                                       sem("s_pt"), sem("s_ptc"), sem("s_o"), sem("s_fin"))
        ot_ps, ot_hi, ot_lo = sem("ot_ps"), sem("ot_hi"), sem("ot_lo")
        rt_whi, rt_wlo = sem("rt_whi"), sem("rt_wlo")
        rt_ps, rt_sc, rt_sel, rt_pos = sem("rt_ps"), sem("rt_sc"), sem("rt_sel"), sem("rt_pos")
        rt_cnt, rt_tot, rt_flag = sem("rt_cnt"), sem("rt_tot"), sem("rt_flag")
        tok_hi, tok_lo = sem("tok_hi"), sem("tok_lo")
        picked, ga_ps, xg_a, xg_v = sem("picked"), sem("ga_ps"), sem("xg_a"), sem("xg_v")
        pt_ps, pt_sb, w_row = sem("pt_ps"), sem("pt_sb"), sem("w_row")
        sp_silu, sp_gate, y_ps, y_a, y_v = sem("sp_silu"), sem("sp_gate"), sem("y_ps"), sem("y_a"), sem("y_v")
        summed, h_again = sem("summed"), sem("h_again")
        cn_ready, cn_ps, cn_hi, cn_lo = sem("cn_ready"), sem("cn_ps"), sem("cn_hi"), sem("cn_lo")
        na_ready, roped, mt_ps, mt_ev_a, mt_ev_v = (sem("na_ready"), sem("roped"), sem("mt_ps"),
                                                    sem("mt_ev_a"), sem("mt_ev_v"))
        s_out = sem("s_out")

        block = ctx.enter_context(nc.Block())

        def raw_dense(g, u):
            return raw_g[:, g % 2, u * UNIT:(u + 1) * UNIT]

        def raw_gated(g, u):
            return raw_g[:, g % 2, :].rearrange("p (g c n) -> p c g n", g=2, c=DC)[:, 4 * u:4 * u + 4, :, :]

        def dense_w(buf, u, c4, lo, n):
            return buf[:, u, c4 * 512 + lo:c4 * 512 + lo + n]

        EV_A, EV_V = {}, {}
        n_a = n_v = 0
        for g in [*range(G_WIN, G_WIN + N_WIN), *range(G_WIN2, G_WIN2 + 4), G_MLA]:
            gate = G_WIN + 6 <= g < G_WIN + N_WIN
            n_a += 4 if g == G_MLA else 2 if gate else 1
            n_v += 4 if g == G_MLA else 0 if gate else 1
            EV_A[g], EV_V[g] = n_a, n_v

        PHASES = {"sh": (M, G_SH, D_SH, 0, 1), "over": (OV, 0, 0, 0, E), "ff1": (M, G_FF1, D_FF1, 1, N_FF),
                  "ff2": (M, G_FF2, D_FF2, 1 + N_FF, N_FF)}
        tok = [t[:, :, :].rearrange("p c t -> p (c t)").rearrange("p (b c n) -> p b c n", b=TB, c=DC)
               for t in (xt_hi, xt_lo)]

        def fill_bank(s, k):
            return bank(7 if s >= 0 else 7 - k)

        h_chunks = h[:, :, :].rearrange("p b (n c) -> p b c n", c=DC)

        def quarter(t, q):
            return t[:, 4 * (q % 2):4 * (q % 2) + 4, (q // 2) * P:(q // 2 + 1) * P]

        def quarter_bank(base, q):
            return bank(base + q).rearrange("p (c t) -> p c t", c=4)

        def if_over(eng, body):
            eng.wait_ge(rt_flag, 1)
            beyond = eng.value_load(over_i[0:1, 0:1], min_val=0, max_val=T * E)
            with eng.If(beyond > 0):
                body()

        def turns(eng, n, first=0, by=2, rest=3):
            q = (n - first - rest) // by
            if q > 0:
                with eng.Fori(0, q) as it:
                    for j in range(by):
                        yield first + j, it
            for s in range(first + by * max(q, 0), n):
                yield s, None

        @block.sync
        def _(sp):
            def free_g(g, it=None, S=M, u=1):
                if g >= 2:
                    sp.wait_ge(S.lo_g, at(2 * g - 3 + u, it, 4))

            def dense_before(g):
                return g < G_SH or g >= G_WIN2 + 2

            def load_dense(g, src, width=512, chunks=DC):
                half = chunks // 2
                for u in range(2):
                    free_g(g, u=u if dense_before(g) else 1)
                    dst = raw_dense(g, u)[:, 0:half * width].rearrange("p (c n) -> p c n", c=half)
                    sp.dma_start(dst, src[:, u * half:(u + 1) * half, :]).then_inc(M.landed_g[g % 2][u], 16)

            def load_gated(g, gate, up, it=None, S=M):
                free_g(g, it, S)
                for k, src in enumerate((gate, up)):
                    dst = raw_g[:, g % 2, k * UNIT:(k + 1) * UNIT].rearrange("p (c n) -> p c n", c=DC)
                    sp.dma_start(dst, src.rearrange("(p c) n -> p c n", c=DC)).then_inc(S.landed_g[g % 2][k], 16)

            def load_down(d, src, it=None, S=M):
                if S is M and d == D_SH:
                    sp.wait_ge(in_["nw"], 16)
                if d >= 2:
                    sp.wait_ge(S.lo_d, at(d - 1, it, 2))
                dst = raw_d[:, d % 2, :].rearrange("p (c n) -> p c n", c=2)
                sp.dma_start(dst, src.rearrange("(p c) n -> p c n", c=2)).then_inc(S.landed_d[d % 2], 16)

            def one(src, i):
                return src[bass.ds(i, 1)].rearrange("e k n -> (e k) n") if not isinstance(i, int) else src[i]

            def gated_stream(S, g0, d0, n, gate_up, down):
                for s in range(min(n, 2)):
                    load_gated(g0 + s, *gate_up(s, None), S=S)
                    load_down(d0 + s, down(s, None), S=S)
                if n > 2:
                    for s, it in turns(sp, n, 2):
                        load_gated(g0 + s, *gate_up(s, it), it, S)
                        load_down(d0 + s, down(s, it), it, S)

            w_ada = a["w_ada"][0].rearrange("(p c) n -> p c n", c=DC)
            w_in = a["w_in"][0].rearrange("(p c) n -> p c n", c=DC)
            for t in range(N_ADA):
                load_dense(G_ADA + t, w_ada[:, :, t * 512:(t + 1) * 512])
            for t in range(N_WIN):
                load_dense(G_WIN + t, w_in[:, :, t * 512:(t + 1) * 512])
                if t == 2:
                    sp.wait_ge(in_["tw"], 16)
                    sp.dma_start(mb_bias, bass.AP(t_dram.tensor, 127, [[NH * BX - 1, P], [BX, NH], [1, T]]))\
                        .then_inc(in_["tb"], 16)
            for i, n in enumerate(("w_branch_sb", "w_branch_mb")):
                load_dense(G_WB + i, a[n][0].rearrange("(c p) n -> p c n", p=P), D, 4)
            w_out = a["w_out"][0].rearrange("(p c) n -> p c n", c=DC)
            for i in range(2):
                load_dense(G_WO + i, w_out[:, :, i * 512:(i + 1) * 512])
            sp.wait_ge(h_ready, 4)
            sp.dma_start(w_rt, a["w_router"][0].rearrange("(p c) n -> p c n", c=DC)).then_inc(in_["wrt"], 16)
            sp.dma_start(rbias, a["router_bias"].to_broadcast([P, E])).then_inc(in_["rbias"], 16)

            def moe_gate_up(s, it):
                i = at(s, it, 2)
                return one(a["w_gate_e"][0], i), one(a["w_up_e"][0], i)

            def moe_down(s, it):
                return one(a["w_down_e"][0], at(s, it, 2))

            def ff_stream(w_gu, w_down):
                def gate_up(s, it):
                    if it is None:
                        return w_gu[:, s * FF:(s + 1) * FF], w_gu[:, D_FF + s * FF:D_FF + (s + 1) * FF]
                    return (w_gu[:, bass.ds(it * (2 * FF) + s * FF, FF)],
                            w_gu[:, bass.ds(it * (2 * FF) + (D_FF + s * FF), FF)])

                def down(s, it):
                    if it is None:
                        return w_down[s * FF:(s + 1) * FF, :]
                    return w_down[bass.ds(it * (2 * FF) + s * FF, FF), :]
                return gate_up, down

            gated_stream(M, G_SH, D_SH, 1, lambda s, it: (a["w_gate_sh"][0], a["w_up_sh"][0]),
                         lambda s, it: a["w_down_sh"][0])
            for dst, n in ((final_g, "final_g"), (pre1, "ffn1_pre_g_2"), (post1, "ffn1_post_g_2"),
                           (mixpre, "mix_pre_g_2"), (mixpost, "mix_post_g_2")):
                src = a[n].rearrange("(o n) -> o n", o=1) if n == "final_g" else a[n]
                sp.dma_start(dst, src.to_broadcast([P, D])).then_inc(in_["gains"], 16)
            gated_stream(M, G_SP, D_SP, E, moe_gate_up, moe_down)

            def over():
                sp.wait_ge(summed, E)
                gated_stream(OV, 0, 0, E, moe_gate_up, moe_down)
                sp.wait_ge(OV.used_d, E + 1)

            if_over(sp, over)
            gated_stream(M, G_FF1, D_FF1, N_FF, *ff_stream(a["ffn1_w_gu_2"][0], a["ffn1_w_down_2"][0]))
            w_in2 = a["w_in_2"][0].rearrange("(p c) n -> p c n", c=DC)
            for t in range(4):
                w = 512 if t < 3 else SMALL
                load_dense(G_WIN2 + t, w_in2[:, :, t * 512:t * 512 + w], w)
            for b in range(TB):
                for rl in range(2):
                    for r in range(4):
                        off = (3 + r - 2 * b - rl) * P + 63
                        sp.dma_start(na_bias[b][rl * 64:(rl + 1) * 64, :, r * 64:(r + 1) * 64],
                                     bass.AP(n_dram.tensor, off, [[NH * NR - 1, 64], [NR, NH], [1, 64]]))\
                            .then_inc(in_["nb"], 16)
            for i, n in enumerate(("na_out_norm_g_2", "mla_out_norm_g_2")):
                sp.dma_start(outg[:, i * 512:(i + 1) * 512], a[n].to_broadcast([P, 512])).then_inc(in_["outg"], 16)
            sp.dma_start(qn_g, a["mla_q_norm_g_2"].to_broadcast([P, 256])).then_inc(in_["outg"], 16)
            sp.dma_start(kvn_g, a["mla_kv_norm_g_2"].to_broadcast([P, 128])).then_inc(in_["outg"], 16)
            g = G_MLA
            free_g(g)
            sp.dma_start(raw_g[:, g % 2, 0:2 * QW].rearrange("p (c n) -> p c n", c=2),
                         a["mla_w_uq_2"][0].rearrange("(c p) n -> p c n", p=P)).then_inc(M.landed_g[g % 2][0], 16)
            sp.dma_start(raw_g[:, g % 2, UNIT:UNIT + KVW], a["mla_w_ukv_2"][0]).then_inc(M.landed_g[g % 2][1], 16)
            w_out2 = a["w_out_2"][0].rearrange("(p c) n -> p c n", c=DC)
            for i in range(2):
                load_dense(G_WO2 + i, w_out2[:, :, i * 512:(i + 1) * 512])
            sp.wait_ge(s_fin, 24)
            sp.dma_start(pre2, a["ffn2_pre_g_2"].to_broadcast([P, D])).then_inc(in_["ff2g"], 16)
            sp.dma_start(post2, a["ffn2_post_g_2"].to_broadcast([P, D])).then_inc(in_["ff2g"], 16)
            gated_stream(M, G_FF2, D_FF2, N_FF, *ff_stream(a["ffn2_w_gu_2"][0], a["ffn2_w_down_2"][0]))
            for b in range(TB):
                sp.wait_ge(x_ready, 10 + b + 1)
                sp.dma_start(out.rearrange("o (b p) n -> p (o b) n", p=P)[:, b, :], x[:, b, :]).then_inc(s_out, 16)
            sp.wait_ge(s_out, 16 * TB)

        @block.gpsimd
        def _(pool):
            pool.memset(ones[:, :], 1.0).then_inc(set_up, 1)
            pool.wait_ge(set_up, 1)
            pool.memset(zeros[:, :], 0.0).then_inc(set_up, 1)
            pool.wait_ge(set_up, 2)
            pool.memset(relb_in[32:33, :], 1.0).then_inc(set_up, 1)
            pool.wait_ge(set_up, 3)
            pool.wait_ge(tb_sb, 1)
            pool.dma_start(t_dram.rearrange("q h x -> h q x"), t_bias.unsqueeze(1).to_broadcast([NH, P, BX]))\
                .then_inc(in_["tw"], 16)
            pool.wait_ge(in_["tw"], 16)

            steps = [0]

            def link(ins):
                steps[0] += 1
                ins.then_inc(chain_p, 1)
                pool.wait_ge(chain_p, steps[0])

            def roots(k, widths):
                n = len(widths)
                pool.wait_ge(ss_a, k + 1)
                kinds = len(set(widths))
                for i in range(kinds):
                    link(pool.tensor_scalar(st[:, 20 + i:20 + n:kinds], st[:, 16 + i:16 + n:kinds], 1.0 / widths[i], EPS,
                                            ALU.mult, ALU.add))
                pool.tensor_tensor(st[:, 28:28 + n], st[:, 20:20 + n], st[:, 60:60 + n], ALU.pow).then_inc(root_p, 1)

            link(pool.memset(st[:, 60:64], -0.5))
            roots(0, [D, D])
            pool.wait_ge(M.used_g, 2 * G_WIN + 4)
            link(pool.memset(rpb_pad, 0.0))
            pool.dma_start(rpb_pad.rearrange("h (r c) -> h r c", r=7)[:, :, 48:79], a["na_rpb_2"][0][:, 4:11, :])\
                .then_inc(in_["rpb"], 16)
            pool.wait_ge(in_["rpb"], 16)
            pool.dma_start(n_dram.rearrange("q h x -> h q x"), rpb_pad.unsqueeze(1).to_broadcast([NH, 64, NR]))\
                .then_inc(in_["nw"], 16)
            pool.wait_ge(in_["nw"], 16)
            for k in range(1, 6):
                roots(k, [D, D])
            pool.wait_ge(in_["nb"], 256)
            for b in range(TB):
                v = na_bias[b].rearrange("p h (r c) -> p (h r) c", r=4)
                m = con[:, C_NA:C_NA + 64].unsqueeze(1).to_broadcast([P, 4 * NH, 64])
                pool.tensor_tensor(v, v, m, ALU.add).then_inc(na_ready, 1)
            pool.wait_ge(na_ready, 2)
            roots(6, [256, 128, 256, 128])
            roots(7, [512] * 4)
            for k in range(8, 11):
                roots(k, [D, D])

        @block.scalar
        def _(act):
            act.dma_start(c_col, a["c"].rearrange("o (p c) -> p (o c)", c=DC)).then_inc(in_["c"], 16)
            act.dma_start(con[:, :], a["con"]).then_inc(in_["con"], 16)
            act.dma_start(x[:, :, :], a["x"].rearrange("o (b p) n -> p (o b) n", p=P)).then_inc(in_["x"], 16)
            act.dma_start(b_ada_row[0:1, :], a["b_ada"]).then_inc(in_["bada"], 16)
            act.dma_start(relb_in[0:32, :], a["rel_bias_t"]).then_inc(in_["relb"], 16)
            act.dma_start(bucket_in, a["buckets"]).then_inc(in_["bucket"], 16)
            act.dma_start(g1_in, a["norm1_g"].to_broadcast([P, D])).then_inc(in_["g1"], 16)
            act.dma_start(g2_in, a["norm2_g"].to_broadcast([P, D])).then_inc(in_["g2"], 16)

            def split_hi(g, u, gated_tile=False, it=None, cols=UNIT, S=M, by=2):
                for half in ((0, 1) if gated_tile and u == 0 else () if gated_tile else (u,)):
                    act.wait_ge(S.landed_g[g % 2][half], at(16 * (g // 2 + 1), it, 8 * by))
                if g:
                    act.wait_ge(S.used_g, at(2 * g + u - 1, it, 2 * by))
                if gated_tile:
                    dst = g_hi[:, u, :].rearrange("p (c g n) -> p c g n", c=4, g=2)
                    act.activation(dst, raw_gated(g, u), ACT.Copy).then_inc(S.hi_g, 1)
                else:
                    act.activation(g_hi[:, u, 0:cols], raw_dense(g, u)[:, 0:cols], ACT.Copy).then_inc(S.hi_g, 1)

            def transposed(k, S=M, base=0):
                for q in range(4):
                    act.wait_ge(S.xt_ps, 4 * k + q + 1)
                    act.activation(quarter(xt_hi, q), quarter_bank(base, q), ACT.Copy).then_inc(S.xt_hi, 1)

            def squares(k, srcs, after, count, scratch):
                for i, src in enumerate(srcs):
                    act.wait_ge(after, count if isinstance(count, int) else count[i])
                    ins = act.activation(scratch(i), src, ACT.Square, accum_out=st[:, 16 + i:17 + i])
                ins.then_inc(ss_a, 1)

            def hi_down(d, it=None, S=M, by=2):
                act.wait_ge(S.landed_d[d % 2], at(16 * (d // 2 + 1), it, 8 * by))
                act.wait_ge(S.used_d, at(d + 1, it, by))
                act.activation(d_hi[:, :], raw_d[:, d % 2, :], ACT.Copy).then_inc(S.hi_d, 1)

            def hi_gated(d, it=None, S=M):
                act.wait_ge(S.tr_done, at(d + 1, it, 2))
                act.activation(at_hi[:, :, :].rearrange("p c t -> p (c t)"), bank(6), ACT.Copy)\
                    .then_inc(S.at_hi, 1)

            def gated_phase(name, early=0):
                S, g0, d0, q0, n = PHASES[name]

                def silus(s, it=None):
                    act.wait_ge(S.used_g, at(2 * (g0 + s) + 2, it, 4))
                    for b in range(TB):
                        if q0 + s:
                            act.wait_ge(S.gated, at(2 * (q0 + s) - 1 + b, it, 4))
                        act.activation(silu[:, b, :], bank(4 + b)[:, 0:FF], ACT.Silu).then_inc(S.silu_done, 1)

                for u in range(early, 2):
                    split_hi(g0, u, True, S=S)
                if n > 1:
                    split_hi(g0 + 1, 0, True, S=S)
                silus(0)
                if n > 1:
                    split_hi(g0 + 1, 1, True, S=S)
                for s, it in turns(act, n):
                    hi_down(d0 + s, it, S)
                    hi_gated(d0 + s, it, S)
                    if s + 2 < n:
                        split_hi(g0 + s + 2, 0, True, it, S=S)
                    if s + 1 < n:
                        silus(s + 1, it)
                    if s + 2 < n:
                        split_hi(g0 + s + 2, 1, True, it, S=S)

            def sparse_phase():
                def gathered(s, k, it=None):
                    act.wait_ge(ga_ps, at(8 + 4 * s + k + 1, it, 16))
                    pair, c = s // 2 + 1, 4 * (s % 2) + k
                    act.activation(xg_hi[:, pair % 2, c:c + 2, :, :].rearrange("p c e r -> p (c e r)"),
                                   fill_bank(s, k)[:, 0:4 * CAP], ACT.Copy).then_inc(xg_a, 1)

                act.wait_ge(M.used_g, 2 * G_SH + 2)
                for b in range(TB):
                    ins = act.activation(tok[0][:, b, :, :], h_chunks[:, b, :, :], ACT.Copy)
                ins.then_inc(tok_hi, 1)
                hi_gated(D_SH)
                split_hi(G_SP, 1, True)
                for s in (-2, -1):
                    for k in (0, 2):
                        gathered(s, k)

                def rows_down(s, it=None):
                    for n in range(2):
                        if n:
                            act.wait_ge(M.used_d, at(D_SP + s + 2, it, 4))
                        else:
                            act.wait_ge(y_ps, at(s + 1, it, 4))
                        act.activation(y_hi[0:CAP, n * 512:(n + 1) * 512], bank(5 + n)[0:CAP, :], ACT.Copy)\
                            .then_inc(y_a, 1)

                def rows_t(s, it=None):
                    act.wait_ge(M.tr_done, at(D_SP + s + 1, it, 4))
                    act.activation(at_hi[:, :, 0:CAP], bank(5)[:, 0:2 * CAP].rearrange("p (c r) -> p c r", c=2),
                                   ACT.Copy).then_inc(M.at_hi, 1)

                def body(s, it=None):
                    g = G_SP + s
                    if s + 1 < E:
                        split_hi(g + 1, 0, True, it, by=4)
                    if s:
                        rows_t(s - 1, it)
                    act.wait_ge(w_row, at(s + 1, it, 4))
                    act.activation(pickT[0:CAP, s % 2, :], bank(6)[0:CAP, 0:T], ACT.Copy).then_inc(pt_sb, 1)
                    if s + 2 < E or it is not None:
                        gathered(s, 0, it)
                    act.wait_ge(M.used_g, at(2 * g + 2, it, 8))
                    act.activation(silu[0:CAP, 0, :], bank(4)[0:CAP, 0:FF], ACT.Silu).then_inc(sp_silu, 1)
                    if s + 1 < E:
                        split_hi(g + 1, 1, True, it, by=4)
                    if s:
                        rows_down(s - 1, it)
                    if s + 2 < E or it is not None:
                        gathered(s, 2, it)
                    hi_down(D_SP + s, it, by=4)

                body(0)
                for s, it in turns(act, E, 1, 4):
                    body(s, it)
                rows_t(E - 1)
                rows_down(E - 1)

            def softmaxes(k, kw):
                def copy_pt(n):
                    i = n - 8 * k
                    act.wait_ge(s_pt, n + 1)
                    if n >= 2:
                        act.wait_ge(s_o, n - 1)
                    w = 2 * kw(i % 2)
                    act.activation(pT_sb(k, n)[:, 0:w], bank(4 + n % 2)[:, 0:w], ACT.Copy).then_inc(s_ptc, 1)

                for i in range(8):
                    n = 8 * k + i
                    w = kw(i % 2)
                    act.wait_ge(s_max, n + 1)
                    if n >= 4:
                        act.wait_ge(s_fin, n - 3)
                    for j in range(2):
                        col = 2 * (n % 4) + j
                        ins = act.activation(s_buf[n % 2][:, j, 0:w], s_buf[n % 2][:, j, 0:w], ACT.Exp,
                                             bias=st[:, 32 + col:33 + col], accum_out=st[:, 40 + col:41 + col])
                    ins.then_inc(s_exp, 1)
                    if i:
                        copy_pt(n - 1)
                copy_pt(8 * k + 7)

            act.wait_ge(in_["c"], 16)
            act.activation(c_sil, c_col, ACT.Silu).then_inc(c_silu, 1)
            mods = (shift1, gain1, gate1, shift2, gain2, gate2)
            squares(0, [x[:, b, :] for b in range(TB)], in_["x"], 16, lambda i: h[:, i, :])

            def ada_out(t):
                act.wait_ge(M.used_g, 2 * t + 2)
                act.activation(mods[t // 2][:, (t % 2) * 512:(t % 2 + 1) * 512], bank(4 + t % 4), ACT.Copy)\
                    .then_inc(ada_ev, 1)

            for t in range(N_ADA):
                split_hi(G_ADA + t, 0)
                split_hi(G_ADA + t, 1)
                if t:
                    ada_out(t - 1)
            split_hi(G_WIN, 0)
            ada_out(N_ADA - 1)
            split_hi(G_WIN, 1)
            transposed(0)

            def win_out(j):
                act.wait_ge(M.used_g, 2 * (G_WIN + j) + 2)
                b0 = 4 + 2 * (j % 2)
                if j in (0, 1, 3, 4):
                    dst = (qT, kT)[j % 3][j // 3][:, 0:2, :].rearrange("p m t -> p (m t)")
                    act.activation(dst, bank(b0), ACT.Copy, scale=0.125 if j % 3 == 0 else 1.0).then_inc(ev_a, 1)
                elif j in (2, 5):
                    act.wait_ge(h_ready, 2)
                    act.activation(v_tok[:, 0, (j // 3) * 512:(j // 3 + 1) * 512], bank(b0), ACT.Copy)\
                        .then_inc(ev_a, 1)
                else:
                    for b in range(TB):
                        act.activation(sig[:, b, (j - 6) * 512:(j - 5) * 512], bank(b0 + b), ACT.Sigmoid)\
                            .then_inc(ev_a, 1)

            for j in range(N_WIN):
                if j:
                    split_hi(G_WIN + j, 0)
                    split_hi(G_WIN + j, 1)
                    win_out(j - 1)
            win_out(N_WIN - 1)

            def sb_scores(g):
                for i in range(2):
                    act.wait_ge(sb_z, 2 * g + i + 1)
                    act.activation(of_group(z_sb, g)[:, i * 384:(i + 1) * 384], bank(2 * (g % 2) + i)[:, 0:384],
                                   ACT.Copy).then_inc(sb_zc, 1)

            def sb_out(g):
                act.wait_ge(sb_o, g + 1)
                act.activation(xt_hi[:, g, :], bank(SB_OUT[g])[:, 0:T], ACT.Copy).then_inc(sb_oh, 1)

            for half in range(2):
                pair = (2 * half, 2 * half + 1)
                for g in pair:
                    if half:
                        sb_out(g - 2)
                    sb_scores(g)
                for g in pair:
                    act.wait_ge(sb_ab, g + 1)
                    ins = act.activation(of_group(l_sb, g), of_group(l_sb, g), ACT.Exp)
                    ins.then_inc(chain_a, 1)
                for g in pair:
                    act.wait_ge(chain_a, g + 1)
                    act.activation(of_group(l_sb, g), of_group(l_sb, g), ACT.Ln, bias=1.0).then_inc(sb_ln, 1)
                for g in pair:
                    act.wait_ge(sb_t, g + 1)
                    act.activation(of_group(p_sb, g), of_group(p_sb, g), ACT.Exp).then_inc(sb_a, 1)
            sb_out(2)
            sb_out(3)
            split_hi(G_WB, 0)
            split_hi(G_WB, 1)
            softmaxes(0, lambda b: P * (b + 1))

            def heads_t(k, base, count):
                for q in range(count):
                    act.wait_ge(ot_ps, k + q + 1)
                    act.activation(xt_hi[:, base + 2 * q:base + 2 * q + 2, :].rearrange("p c t -> p (c t)"),
                                   bank(q), ACT.Copy).then_inc(ot_hi, 1)

            heads_t(0, 4, 2)
            split_hi(G_WB + 1, 0)
            split_hi(G_WB + 1, 1)
            split_hi(G_WO, 0)
            split_hi(G_WO, 1)
            transposed(1)
            split_hi(G_WO + 1, 0)
            split_hi(G_WO + 1, 1)
            act.wait_ge(in_["wrt"], 16)
            act.activation(w_rt_hl[0], w_rt, ACT.Copy).then_inc(rt_whi, 1)
            squares(1, [x[:, b, :] for b in range(TB)], x_ready, (1, 2), lambda i: h[:, i, :])
            split_hi(G_SH, 0, True)
            transposed(2)
            split_hi(G_SH, 1, True)
            act.wait_ge(rt_ps, 1)
            act.activation(rt[:, 0:2 * E], bank(7)[:, 0:2 * E], ACT.Sigmoid).then_inc(rt_sc, 1)
            hi_down(D_SH)
            split_hi(G_SP, 0, True)
            act.wait_ge(M.used_g, 2 * G_SH + 2)
            for b in range(TB):
                act.activation(silu[:, b, :], bank(4 + b)[:, 0:FF], ACT.Silu).then_inc(M.silu_done, 1)
            sparse_phase()

            def over():
                act.wait_ge(summed, E)
                transposed(0, OV, 4)
                gated_phase("over")
                act.wait_ge(OV.used_d, E + 1)

            if_over(act, over)
            squares(2, [x[:, b, :] for b in range(TB)], x_ready, (3, 4), lambda i: h[:, i, :])
            split_hi(G_FF1, 0, True)
            squares(3, [x[:, b, :] for b in range(TB)], x_ready, (5, 6), lambda i: h[:, i, :])
            split_hi(G_FF1, 1, True)
            transposed(3)
            gated_phase("ff1", 2)
            squares(4, [ps[b][:, :, :].rearrange("p a n -> p (a n)") for b in range(TB)], M.used_d, D_FF1 + N_FF + 1,
                    lambda i: h[:, i, :])
            split_hi(G_WIN2, 0)
            squares(5, [x[:, b, :] for b in range(TB)], x_ready, (7, 8), lambda i: h[:, i, :])
            split_hi(G_WIN2, 1)
            transposed(4)

            def win2_out(j):
                act.wait_ge(M.used_g, 2 * (G_WIN2 + j) + 2)
                b0 = 4 + 2 * (j % 2)
                if j < 2:
                    dst = (qT2, kT2)[j][:, 0:2, :].rearrange("p m t -> p (m t)")
                    act.activation(dst, bank(b0), ACT.Copy, scale=0.125 if j == 0 else 1.0).then_inc(ev_a, 1)
                elif j == 2:
                    act.activation(v2[:, 0, :], bank(b0), ACT.Copy).then_inc(ev_a, 1)
                else:
                    act.activation(small[:, 0, :], bank(b0)[:, 0:SMALL], ACT.Copy).then_inc(ev_a, 1)

            for j in range(4):
                cols = UNIT if j < 3 else 4 * SMALL
                if j:
                    split_hi(G_WIN2 + j, 0, cols=cols)
                    split_hi(G_WIN2 + j, 1, cols=cols)
                if j:
                    win2_out(j - 1)
            win2_out(3)
            srcs = [small[:, b, lo:hi] for b in range(TB) for lo, hi in ((0, 256), (256, 384))]
            act.wait_ge(ev_a, EV_A[G_WIN2 + 3])
            squares(6, srcs, ev_v, EV_V[G_WIN2 + 3], lambda i: att[:, i * 256:i * 256 + srcs[i].shape[-1]])
            split_hi(G_MLA, 0, cols=2 * QW)
            split_hi(G_MLA, 1, cols=KVW)
            softmaxes(1, lambda b: T)
            for q in range(2):
                act.wait_ge(cn_ps, q + 1)
                w = 512 if q == 0 else 256
                act.activation(xt_hi[:, 2 * q:2 * q + w // T, :].rearrange("p c t -> p (c t)"), bank(q)[:, 0:w],
                               ACT.Copy).then_inc(cn_hi, 1)
            act.wait_ge(M.used_g, 2 * G_MLA + 2)
            for i in range(4):
                act.activation(q_tok[:, i // 2, (i % 2) * 384:(i % 2 + 1) * 384], bank(i)[:, 0:384], ACT.Copy)\
                    .then_inc(ev_a, 1)
            for q in range(0, 8, 2):
                act.wait_ge(mt_ps, q + 1)
                dst = (qTm, kTm)[q // 4][0:96, (q % 4) * 2:(q % 4) * 2 + 2, :].rearrange("p h t -> p (h t)")
                act.activation(dst, bank(q % 4)[0:96, :], ACT.Copy).then_inc(mt_ev_a, 1)
            split_hi(G_WO2, 0)
            split_hi(G_WO2, 1)
            softmaxes(2, lambda b: T)
            srcs2 = [h[:, b, i * 512:(i + 1) * 512] for b in range(TB) for i in range(2)]
            squares(7, srcs2, s_fin, 24, lambda i: att[:, i * 512:(i + 1) * 512])
            transposed(5)
            split_hi(G_WO2 + 1, 0)
            split_hi(G_WO2 + 1, 1)
            squares(8, [ps[2 + b][:, :, :].rearrange("p a n -> p (a n)") for b in range(TB)], M.used_g,
                    2 * (G_WO2 + 1) + 2, lambda i: h[:, i, :])
            split_hi(G_FF2, 0, True)
            squares(9, [x[:, b, :] for b in range(TB)], x_ready, (9, 10), lambda i: h[:, i, :])
            split_hi(G_FF2, 1, True)
            transposed(6)
            gated_phase("ff2", 2)
            squares(10, [ps[b][:, :, :].rearrange("p a n -> p (a n)") for b in range(TB)], M.used_d, D_FF2 + N_FF + 1,
                    lambda i: h[:, i, :])

        @block.vector
        def _(dve):
            chain = [0]

            def link(ins):
                chain[0] += 1
                ins.then_inc(chain_v, 1)
                dve.wait_ge(chain_v, chain[0])

            def split_lo(g, u, gated_tile=False, it=None, cols=UNIT, S=M, by=2):
                dve.wait_ge(S.hi_g, at(2 * g + u + 1, it, 2 * by))
                if gated_tile:
                    hi, lo = (t[:, u, :].rearrange("p (c g n) -> p c g n", c=4, g=2) for t in (g_hi, g_lo))
                    raw = raw_gated(g, u)
                else:
                    hi, lo, raw = g_hi[:, u, 0:cols], g_lo[:, u, 0:cols], raw_dense(g, u)[:, 0:cols]
                dve.tensor_tensor(lo, raw, hi.bitcast(F32), ALU.subtract).then_inc(S.lo_g, 1)

            def transposed(k, S=M, base=0):
                for q in range(4):
                    dve.wait_ge(S.xt_hi, 4 * k + q + 1)
                    dve.tensor_tensor(quarter(xt_lo, q), quarter_bank(base, q), quarter(xt_hi, q).bitcast(F32),
                                      ALU.subtract).then_inc(S.xt_lo, 1)

            def roots(k):
                dve.wait_ge(root_p, k + 1)

            def scaled(dst, src, i, gain):
                return dve.scalar_tensor_tensor(out=dst, in0=src, scalar=st[:, 28 + i:29 + i], in1=gain,
                                                op0=ALU.mult, op1=ALU.mult)

            def lo_down(d, it=None, S=M, by=2):
                dve.wait_ge(S.hi_d, at(d + 1, it, by))
                dve.tensor_tensor(d_lo[:, :], raw_d[:, d % 2, :], d_hi[:, :].bitcast(F32), ALU.subtract)\
                    .then_inc(S.lo_d, 1)

            def lo_gated(d, it=None, S=M):
                dve.wait_ge(S.at_hi, at(d + 1, it, 2))
                hi, lo = (t[:, :, :].rearrange("p c t -> p (c t)") for t in (at_hi, at_lo))
                dve.tensor_tensor(lo, bank(6), hi.bitcast(F32), ALU.subtract).then_inc(S.at_lo, 1)

            def gate(S, q, s, weight=None, it=None):
                for b in range(TB):
                    w = 1.0
                    if weight is not None:
                        w = weight[:, b, s:s + 1] if it is None else weight[:, b, bass.ds(it * 2 + s, 1)]
                    dve.wait_ge(S.silu_done, at(2 * q + b + 1, it, 4))
                    dve.scalar_tensor_tensor(out=a_sb[:, b, :], in0=silu[:, b, :], scalar=w,
                                             in1=bank(4 + b)[:, FF:2 * FF], op0=ALU.mult, op1=ALU.mult)\
                        .then_inc(S.gated, 1)

            def gated_phase(name, weight=None, early=0):
                S, g0, d0, q0, n = PHASES[name]
                for u in range(early, 2):
                    split_lo(g0, u, True, S=S)
                split_lo(g0 + 1, 0, True, S=S)
                gate(S, q0, 0, weight)
                split_lo(g0 + 1, 1, True, S=S)
                for s, it in turns(dve, n):
                    lo_down(d0 + s, it, S)
                    lo_gated(d0 + s, it, S)
                    if s + 2 < n:
                        split_lo(g0 + s + 2, 0, True, it, S=S)
                    if s + 1 < n:
                        gate(S, q0 + s + 1, s + 1, weight, it)
                    if s + 2 < n:
                        split_lo(g0 + s + 2, 1, True, it, S=S)

            def pick_rows(pair, it=None):
                if pair >= 2:
                    dve.wait_ge(pt_ps, at(2 * pair - 2, it, 4))
                for e in range(2):
                    for b in range(TB):
                        s = 2 * pair + e
                        r = row_of[:, b, s:s + 1] if it is None else row_of[:, b, bass.ds(it * 4 + s, 1)]
                        ins = dve.tensor_scalar(pick[:, pair % 2, b, e, :], con[:, C_IOTA:C_IOTA + CAP], r, None,
                                                ALU.is_equal)
                ins.then_inc(picked, 1)

            def sparse_phase():
                def gathered(s, k, it=None):
                    dve.wait_ge(ga_ps, at(8 + 4 * s + k + 1, it, 16))
                    pair, c = s // 2 + 1, 4 * (s % 2) + k - 1
                    dve.tensor_copy(xg_lo[:, pair % 2, c:c + 2, :, :].rearrange("p c e r -> p (c e r)"),
                                    fill_bank(s, k)[:, 0:4 * CAP]).then_inc(xg_v, 1)

                split_lo(G_SP, 1, True)
                for s in (-2, -1):
                    for k in (1, 3):
                        gathered(s, k)
                pick_rows(1)

                def rows_down(s, it=None):
                    for n in range(2):
                        dve.wait_ge(y_a, at(2 * s + n + 1, it, 8))
                        hi, lo = (t[0:CAP, n * 512:(n + 1) * 512] for t in (y_hi, y_lo))
                        dve.tensor_tensor(lo, bank(5 + n)[0:CAP, :], hi.bitcast(F32), ALU.subtract).then_inc(y_v, 1)

                def rows_t(s, it=None):
                    dve.wait_ge(M.at_hi, at(D_SP + s + 1, it, 4))
                    dve.tensor_tensor(at_lo[:, :, 0:CAP], bank(5)[:, 0:2 * CAP].rearrange("p (c r) -> p c r", c=2),
                                      at_hi[:, :, 0:CAP].bitcast(F32), ALU.subtract).then_inc(M.at_lo, 1)

                def body(s, it=None):
                    g = G_SP + s
                    dve.wait_ge(pt_ps, at(s + 1, it, 4))
                    dve.reduce_sum(st[0:CAP, 48 + s % 2:49 + s % 2], bank(6)[0:CAP, T:T + 2], AX).then_inc(w_row, 1)
                    if s:
                        rows_t(s - 1, it)
                    if s + 1 < E:
                        split_lo(g + 1, 0, True, it, by=4)
                    if s + 2 < E or it is not None:
                        gathered(s, 1, it)
                    dve.wait_ge(sp_silu, at(s + 1, it, 4))
                    dve.wait_ge(w_row, at(s + 1, it, 4))
                    dve.scalar_tensor_tensor(out=a_sb[0:CAP, 0, :], in0=silu[0:CAP, 0, :],
                                             scalar=st[0:CAP, 48 + s % 2:49 + s % 2], in1=bank(4)[0:CAP, FF:2 * FF],
                                             op0=ALU.mult, op1=ALU.mult).then_inc(sp_gate, 1)
                    if s % 2 and (s + 3 < E or it is not None):
                        pick_rows(s // 2 + 2, it)
                    if s:
                        rows_down(s - 1, it)
                    if s + 1 < E:
                        split_lo(g + 1, 1, True, it, by=4)
                    if s + 2 < E or it is not None:
                        gathered(s, 3, it)
                    lo_down(D_SP + s, it, by=4)

                body(0)
                for s, it in turns(dve, E, 1, 4):
                    body(s, it)
                rows_t(E - 1)
                rows_down(E - 1)

            def softmaxes(k, kw, bias, scale, dest):
                def finish(n):
                    i = n - 8 * k
                    dve.wait_ge(s_o, n + 1)
                    inv = st[:, 48 + 2 * (n % 4):50 + 2 * (n % 4)]
                    link(dve.reciprocal(inv, st[:, 40 + 2 * (n % 4):42 + 2 * (n % 4)]))
                    dve.tensor_tensor(dest(i // 2, i % 2),
                                      bank(6 + n % 2)[:, 0:2 * HD].rearrange("p (h d) -> p h d", h=2),
                                      inv.unsqueeze(2).to_broadcast([P, 2, HD]), ALU.mult).then_inc(s_fin, 1)

                for i in range(8):
                    n = 8 * k + i
                    w = kw(i % 2)
                    dve.wait_ge(s_ps, n + 1)
                    if n >= 2:
                        dve.wait_ge(s_pt, n - 1)
                    s = s_buf[n % 2][:, :, 0:w]
                    z = bank(2 + n % 2)[:, 0:2 * w].rearrange("p (h k) -> p h k", h=2)
                    if bias is None:
                        link(dve.tensor_scalar(s, z, scale, None, ALU.mult))
                    else:
                        link(dve.tensor_tensor(s, z, bias(i // 2, i % 2), ALU.add))
                    dve.reduce_max(st[:, 32 + 2 * (n % 4):34 + 2 * (n % 4)], s, AX, negate=True).then_inc(s_max, 1)
                    if i >= 2:
                        finish(n - 2)
                finish(8 * k + 6)
                finish(8 * k + 7)

            dve.wait_ge(c_silu, 1)
            c_all = c_sil.unsqueeze(2).to_broadcast([P, DC, P])
            link(dve.tensor_copy(xt_hi[:, :, 0:P], c_all))
            dve.tensor_tensor(xt_lo[:, :, 0:P], c_all, xt_hi[:, :, 0:P].bitcast(F32), ALU.subtract).then_inc(c_bc, 1)
            dve.wait_ge(tb_ps, 1)
            dve.tensor_copy(t_bias, bank(0)[0:NH, 0:BX]).then_inc(tb_sb, 1)
            for t in range(N_ADA):
                split_lo(G_ADA + t, 0)
                split_lo(G_ADA + t, 1)
                if t == 5:
                    roots(0)
                    dve.wait_ge(ada_ev, 4)
                    dve.wait_ge(in_["g1"], 16)
                    link(dve.scalar_tensor_tensor(out=gain1, in0=gain1, scalar=1.0, in1=g1_in,
                                                  op0=ALU.add, op1=ALU.mult))
                elif t in (6, 8):
                    link(scaled(h[:, (t - 6) // 2, :], x[:, (t - 6) // 2, :], (t - 6) // 2, gain1))
                elif t in (7, 9):
                    dve.tensor_tensor(h[:, (t - 7) // 2, :], h[:, (t - 7) // 2, :], shift1, ALU.add).then_inc(h_ready, 1)
            dve.wait_ge(ada_ev, 10)
            dve.wait_ge(in_["g2"], 16)
            dve.scalar_tensor_tensor(out=gain2, in0=gain2, scalar=1.0, in1=g2_in, op0=ALU.add, op1=ALU.mult)
            split_lo(G_WIN, 0)
            split_lo(G_WIN, 1)
            transposed(0)

            def win_out(j):
                dve.wait_ge(M.used_g, 2 * (G_WIN + j) + 2)
                src = bank(5 + 2 * (j % 2))
                if j in (0, 1, 3, 4):
                    dst = (qT, kT)[j % 3][j // 3][:, 2:4, :].rearrange("p m t -> p (m t)")
                    dve.tensor_scalar(dst, src, 0.125 if j % 3 == 0 else 1.0, None, ALU.mult).then_inc(ev_v, 1)
                else:
                    dve.tensor_copy(v_tok[:, 1, (j // 3) * 512:(j // 3 + 1) * 512], src).then_inc(ev_v, 1)

            for j in range(N_WIN):
                if j:
                    split_lo(G_WIN + j, 0)
                    split_lo(G_WIN + j, 1)
                    if j <= 6:
                        win_out(j - 1)

            dve.wait_ge(in_["tw"], 16)
            def sb_out(g):
                dve.wait_ge(sb_oh, g + 1)
                dve.tensor_tensor(xt_lo[:, g, :], bank(SB_OUT[g])[:, 0:T], xt_hi[:, g, :].bitcast(F32),
                                  ALU.subtract).then_inc(sb_ol, 1)

            def masked(t, g, mask, op):
                for c in (0, 2):
                    d3 = of_group(t, g).rearrange("p (i c q) -> p i c q", i=2, c=3)[:, :, c, :]
                    ins = dve.tensor_tensor(d3, d3, con[:, mask:mask + P].unsqueeze(1).to_broadcast([P, 2, P]), op)
                return ins

            for half in range(2):
                pair = (2 * half, 2 * half + 1)
                for g in pair:
                    if half:
                        sb_out(g - 2)
                    z, l = of_group(z_sb, g), of_group(l_sb, g)
                    dve.wait_ge(sb_zc, 2 * g + 2)
                    dve.scalar_tensor_tensor(out=l, in0=z, scalar=-1.0, in1=z, op0=ALU.mult, op1=ALU.min)\
                        .then_inc(sb_ab, 1)
                for g in pair:
                    z, l = of_group(z_sb, g), of_group(l_sb, g)
                    dve.wait_ge(sb_ln, g + 1)
                    link(dve.scalar_tensor_tensor(out=l, in0=z, scalar=0.0, in1=l, op0=ALU.max, op1=ALU.add))
                    masked(l_sb, g, C_MASK, ALU.mult).then_inc(sb_r, 1)
                for g in pair:
                    for i in range(2):
                        dve.wait_ge(sb_i, 2 * g + i + 1)
                        lo = i * 384
                        ins = dve.scalar_tensor_tensor(out=of_group(p_sb, g)[:, lo:lo + 384],
                                                       in0=bank(4 + 2 * (g % 2) + i)[:, 0:384], scalar=-1.0,
                                                       in1=of_group(z_sb, g)[:, lo:lo + 384],
                                                       op0=ALU.mult, op1=ALU.add)
                    link(ins)
                    masked(p_sb, g, C_MIN, ALU.min).then_inc(sb_t, 1)
            sb_out(2)
            sb_out(3)
            split_lo(G_WB, 0)
            split_lo(G_WB, 1)

            dve.wait_ge(in_["tb"], 16)
            softmaxes(0, lambda b: P * (b + 1), lambda hp, b: mb_bias[:, pair_heads(hp)[0]:pair_heads(hp)[1] + 1:2, P * (1 - b):T], None,
                      lambda hp, b: of_pair(o_mb[:, b, :], hp))
            for q in range(2):
                dve.wait_ge(ot_hi, q + 1)
                hi, lo = (t[:, 4 + 2 * q:6 + 2 * q, :].rearrange("p c t -> p (c t)") for t in (xt_hi, xt_lo))
                dve.tensor_tensor(lo, bank(q), hi.bitcast(F32), ALU.subtract).then_inc(ot_lo, 1)
            split_lo(G_WB + 1, 0)
            split_lo(G_WB + 1, 1)
            for b in range(TB):
                dve.wait_ge(M.used_g, 2 * G_WB + 2)
                link(dve.tensor_tensor(h[:, b, :], ps[b][:, :, :].rearrange("p a n -> p (a n)"), sig[:, b, 0:D],
                                       ALU.mult))
            split_lo(G_WO, 0)
            dve.wait_ge(M.used_g, 2 * (G_WB + 1) + 2)
            for b in range(TB):
                tmp = att[:, b * D:(b + 1) * D]
                link(dve.tensor_tensor(tmp, ps[2 + b][:, :, :].rearrange("p a n -> p (a n)"), sig[:, b, D:2 * D],
                                       ALU.mult))
                dve.tensor_tensor(h[:, b, :], h[:, b, :], tmp, ALU.add).then_inc(h_ready, 1)
            transposed(1)
            split_lo(G_WO, 1)
            split_lo(G_WO + 1, 0)
            split_lo(G_WO + 1, 1)
            dve.wait_ge(rt_whi, 1)
            dve.tensor_tensor(w_rt_hl[1], w_rt, w_rt_hl[0].bitcast(F32), ALU.subtract).then_inc(rt_wlo, 1)

            def add_gated(gate, banks, sem_, count):
                dve.wait_ge(sem_, count)
                for b in range(TB):
                    link(dve.tensor_tensor(h[:, b, :], ps[banks // 2 + b][:, :, :].rearrange("p a n -> p (a n)"), gate,
                                           ALU.mult))
                    dve.tensor_tensor(x[:, b, :], x[:, b, :], h[:, b, :], ALU.add).then_inc(x_ready, 1)

            for n in range(2):
                dve.wait_ge(M.used_g, 2 * (G_WO + n) + 2)
                half = slice(n * 512, (n + 1) * 512)
                for b in range(TB):
                    link(dve.tensor_tensor(h[:, b, half], bank(4 + 2 * b + n), gate1[:, half], ALU.mult))
                    ins = dve.tensor_tensor(x[:, b, half], x[:, b, half], h[:, b, half], ALU.add)
                    if n:
                        ins.then_inc(x_ready, 1)
            roots(1)
            for b in range(TB):
                link(scaled(h[:, b, :], x[:, b, :], b, gain2))
                dve.tensor_tensor(h[:, b, :], h[:, b, :], shift2, ALU.add).then_inc(h_ready, 1)
            transposed(2)

            split_lo(G_SH, 0, True)
            split_lo(G_SH, 1, True)
            dve.wait_ge(rt_sc, 1)
            dve.wait_ge(in_["rbias"], 16)

            def sel01(b):
                return rt[:, (8 + b) * E:(9 + b) * E]

            def weight(b):
                return rt[:, (10 + b) * E:(11 + b) * E]

            def route(b):
                sc = rt[:, b * E:(b + 1) * E]
                ch, cm, sel = (rt[:, i * E:(i + 1) * E] for i in (2, 3, 4))
                top2 = rt[:, 5 * E:6 * E]
                gs, m8, gr = rt[:, 6 * E:6 * E + 12], rt[:, 6 * E + 16:6 * E + 24], rt[:, 6 * E + 32:6 * E + 44]
                pen, tot = rt[:, 7 * E:7 * E + 8], rt[:, 7 * E + 8:7 * E + 10]
                link(dve.tensor_tensor(ch, sc, rbias, ALU.add))
                for i in range(NGRP):
                    ins = dve.max(top2[:, 8 * i:8 * i + 8], ch[:, 8 * i:8 * i + 8])
                link(ins)
                t3 = top2.rearrange("p (g k) -> p g k", g=NGRP)
                dve.tensor_tensor(gs[:, 0:8].unsqueeze(2), t3[:, :, 0:1], t3[:, :, 1:2], ALU.add)
                link(dve.memset(gs[:, 8:12], 3e38))
                link(dve.max(m8, gs))
                link(dve.match_replace(gr, m8, gs, -3e38))
                link(dve.tensor_scalar(pen, gr[:, 0:8], -2e38, BIG, ALU.is_lt, ALU.mult))
                link(dve.tensor_scalar(pen, pen, BIG, None, ALU.subtract))
                link(dve.tensor_tensor(cm.rearrange("p (g k) -> p g k", g=NGRP),
                                       ch.rearrange("p (g k) -> p g k", g=NGRP),
                                       pen.unsqueeze(2).to_broadcast([P, NGRP, 8]), ALU.add))
                link(dve.max(m8, cm))
                link(dve.match_replace(sel, m8, cm, -3e38))
                link(dve.tensor_scalar(sel01(b), sel, -2e38, None, ALU.is_lt))
                link(dve.tensor_tensor(sel, sel01(b), sc, ALU.mult))
                link(dve.reduce_sum(tot[:, 0:1], sel, AX))
                link(dve.reciprocal(tot[:, 1:2], tot[:, 0:1]))
                return dve.tensor_scalar(weight(b), sel, tot[:, 1:2], 2.5, ALU.mult, ALU.mult)

            link(route(0))
            route(1).then_inc(rt_sel, 1)
            lo_down(D_SH)
            split_lo(G_SP, 0, True)
            gate(M, 0, 0)
            dve.wait_ge(tok_hi, 1)
            for b in range(TB):
                ins = dve.tensor_tensor(tok[1][:, b, :, :], h_chunks[:, b, :, :], tok[0][:, b, :, :].bitcast(F32),
                                        ALU.subtract)
            ins.then_inc(tok_lo, 1)
            lo_gated(D_SH)
            dve.wait_ge(rt_pos, 1)
            for b in range(TB):
                pos = bank(7)[:, b * E:(b + 1) * E]
                fits, beyond = rt[:, (12 + b) * E:(13 + b) * E], rt[:, (14 + b) * E:(15 + b) * E]
                row, w, wf = row_of[:, b, :], weight(b), rt[:, (2 + b) * E:(3 + b) * E]
                link(dve.scalar_tensor_tensor(out=fits, in0=pos, scalar=float(CAP), in1=sel01(b),
                                              op0=ALU.is_lt, op1=ALU.mult))
                dve.tensor_tensor(beyond, sel01(b), fits, ALU.subtract)
                dve.tensor_tensor(wf, w, fits, ALU.mult)
                link(dve.scalar_tensor_tensor(out=row, in0=pos, scalar=1.0, in1=fits, op0=ALU.add, op1=ALU.mult))
                dve.tensor_scalar(row, row, 1.0, None, ALU.subtract)
                link(dve.tensor_copy(w_hl[:, b, :, 0:1], wf.unsqueeze(2)))
                dve.tensor_tensor(w_hl[:, b, :, 1:2], wf.unsqueeze(2), w_hl[:, b, :, 0:1].bitcast(F32), ALU.subtract)
                ins = dve.tensor_tensor(w_over[:, b, :], w, wf, ALU.subtract)
            link(ins)
            dve.reduce_sum(st[:, 52:53], rt[:, 14 * E:16 * E], AX).then_inc(rt_cnt, 1)
            pick_rows(0)
            dve.wait_ge(rt_tot, 1)
            dve.tensor_copy(over_i[0:1, 0:1], bank(5)[0:1, 0:1]).then_inc(rt_flag, 1)
            sparse_phase()

            def over():
                dve.wait_ge(summed, E)
                for b in range(TB):
                    ins = dve.tensor_tensor(h_chunks[:, b, :, :], tok[0][:, b, :, :].bitcast(F32),
                                            tok[1][:, b, :, :].bitcast(F32), ALU.add)
                ins.then_inc(h_again, 1)
                transposed(0, OV, 4)
                gated_phase("over", w_over)
                dve.wait_ge(OV.used_d, E + 1)

            if_over(dve, over)

            add_gated(gate2, 0, summed, E)
            dve.wait_ge(in_["gains"], 80)
            roots(2)
            for b in range(TB):
                scaled(x[:, b, :], x[:, b, :], b, final_g).then_inc(x_ready, 1)

            def normed(k, gain):
                roots(k)
                for b in range(TB):
                    scaled(h[:, b, :], x[:, b, :], b, gain).then_inc(h_ready, 1)

            def add_normed(k, base, gain, factor):
                roots(k)
                for b in range(TB):
                    src = ps[base + b][:, :, :].rearrange("p a n -> p (a n)")
                    link(scaled(h[:, b, :], src, b, gain))
                    dve.scalar_tensor_tensor(out=x[:, b, :], in0=h[:, b, :], scalar=factor, in1=x[:, b, :],
                                             op0=ALU.mult, op1=ALU.add).then_inc(x_ready, 1)

            split_lo(G_FF1, 0, True)
            normed(3, pre1)
            transposed(3)
            gated_phase("ff1", early=1)
            add_normed(4, 0, post1, 0.5)
            split_lo(G_WIN2, 0)
            normed(5, mixpre)
            transposed(4)

            def win2_out(j):
                dve.wait_ge(M.used_g, 2 * (G_WIN2 + j) + 2)
                src = bank(5 + 2 * (j % 2))
                if j < 2:
                    dst = (qT2, kT2)[j][:, 2:4, :].rearrange("p m t -> p (m t)")
                    dve.tensor_scalar(dst, src, 0.125 if j == 0 else 1.0, None, ALU.mult).then_inc(ev_v, 1)
                elif j == 2:
                    dve.tensor_copy(v2[:, 1, :], src).then_inc(ev_v, 1)
                else:
                    dve.tensor_copy(small[:, 1, :], src[:, 0:SMALL]).then_inc(ev_v, 1)

            for j in range(4):
                cols = UNIT if j < 3 else 4 * SMALL
                if j:
                    split_lo(G_WIN2 + j, 0, cols=cols)
                split_lo(G_WIN2 + j, 1, cols=cols)
                if j:
                    win2_out(j - 1)
            win2_out(3)
            split_lo(G_MLA, 0, cols=2 * QW)
            split_lo(G_MLA, 1, cols=KVW)
            dve.wait_ge(in_["outg"], 64)
            roots(6)
            for b in range(TB):
                scaled(small[:, b, 0:256], small[:, b, 0:256], 2 * b, qn_g)
                ins = scaled(small[:, b, 256:384], small[:, b, 256:384], 2 * b + 1, kvn_g)
            ins.then_inc(cn_ready, 1)
            dve.wait_ge(na_ready, 2)
            softmaxes(1, lambda b: T, lambda hp, b: na_bias[b][:, pair_heads(hp)[0]:pair_heads(hp)[1] + 1:2, :], None,
                      lambda hp, b: of_pair(h[:, b, 0:512], hp))
            for q in range(2):
                dve.wait_ge(cn_hi, q + 1)
                w = 512 if q == 0 else 256
                hi, lo = (t[:, 2 * q:2 * q + w // T, :].rearrange("p c t -> p (c t)") for t in (xt_hi, xt_lo))
                dve.tensor_tensor(lo, bank(q)[:, 0:w], hi.bitcast(F32), ALU.subtract).then_inc(cn_lo, 1)
            dve.wait_ge(M.used_g, 2 * G_MLA + 2)
            for i in range(4):
                dve.tensor_copy(kv_tok[:, i // 2, (i % 2) * 512:(i % 2 + 1) * 512], bank(4 + i)).then_inc(ev_v, 1)
            dve.wait_ge(ev_a, EV_A[G_MLA])
            dve.wait_ge(ev_v, EV_V[G_MLA])
            for b in range(TB):
                q3 = q_tok[:, b, :].rearrange("p (h n) -> p h n", h=NH)
                k3 = k_full[:, b, :].rearrange("p (h n) -> p h n", h=NH)
                kv3 = kv_tok[:, b, :].rearrange("p (h n) -> p h n", h=NH)
                cos, sin = (con[:, c + 16 * b:c + 16 * b + 16] for c in (C_COS, C_SIN))

                def wide(t):
                    return t.unsqueeze(1).to_broadcast([P, NH, 16])

                tmp = [rope_t[:, i, b, :].rearrange("p (h n) -> p h n", h=NH) for i in range(4)]
                q1, q2 = q3[:, :, 64:80], q3[:, :, 80:96]
                dve.tensor_tensor(tmp[0], q1, wide(cos), ALU.mult)
                dve.tensor_tensor(tmp[1], q2, wide(sin), ALU.mult)
                dve.tensor_tensor(tmp[2], q2, wide(cos), ALU.mult)
                link(dve.tensor_tensor(tmp[3], q1, wide(sin), ALU.mult))
                dve.tensor_tensor(q1, tmp[0], tmp[1], ALU.subtract)
                link(dve.tensor_tensor(q2, tmp[2], tmp[3], ALU.add))
                dve.tensor_copy(k3[:, :, 0:64], kv3[:, :, 0:64])
                k1, k2 = small[:, b, 384:400], small[:, b, 400:416]
                t16 = [rope_t[:, i, b, 0:16] for i in range(4)]
                dve.tensor_tensor(t16[0], k1, cos, ALU.mult)
                dve.tensor_tensor(t16[1], k2, sin, ALU.mult)
                dve.tensor_tensor(t16[2], k2, cos, ALU.mult)
                link(dve.tensor_tensor(t16[3], k1, sin, ALU.mult))
                dve.tensor_tensor(k3[:, :, 64:80], wide(t16[0]), wide(t16[1]), ALU.subtract)
                dve.tensor_tensor(k3[:, :, 80:96], wide(t16[2]), wide(t16[3]), ALU.add).then_inc(roped, 1)
            for q in range(1, 8, 2):
                dve.wait_ge(mt_ps, q + 1)
                dst = (qTm, kTm)[q // 4][0:96, (q % 4) * 2:(q % 4) * 2 + 2, :].rearrange("p h t -> p (h t)")
                dve.tensor_copy(dst, bank(q % 4)[0:96, :]).then_inc(mt_ev_v, 1)
            softmaxes(2, lambda b: T, None, 96.0 ** -0.5, lambda hp, b: of_pair(h[:, b, 512:1024], hp))
            split_lo(G_WO2, 0)
            roots(7)
            for i in range(4):
                hv = h[:, i // 2, (i % 2) * 512:(i % 2 + 1) * 512]
                ins = scaled(hv, hv, i, outg[:, (i % 2) * 512:(i % 2 + 1) * 512])
                if i % 2:
                    ins.then_inc(h_ready, 1)
            transposed(5)
            split_lo(G_WO2, 1)
            split_lo(G_WO2 + 1, 0)
            split_lo(G_WO2 + 1, 1)
            add_normed(8, 2, mixpost, 1.0)
            dve.wait_ge(in_["ff2g"], 32)
            split_lo(G_FF2, 0, True)
            normed(9, pre2)
            transposed(6)
            gated_phase("ff2", early=1)
            add_normed(10, 0, post2, 0.5)

        @block.tensor
        def _(pe):
            PASSES = ((0, 0), (0, 1), (1, 0))

            def transposes(k, S=M, base=0):
                for q in range(4):
                    b = q // 2
                    if S is M:
                        pe.wait_ge(h_ready, 2 * k + b + 1)
                    for i in range(4):
                        ins = pe.transpose(bank(base + q)[:, i * P:(i + 1) * P], h[:, b, 4 * (q % 2) + i:D:DC], ident)
                    ins.then_inc(S.xt_ps, 1)

            def fresh(k, b, u):
                if k is not None:
                    pe.wait_ge(M.xt_lo, 4 * k + 2 * b + u + 1)

            def rows(out_, b, cs, w, n, start, stop):
                last = None
                for i, c in enumerate(cs):
                    for k, (s, m) in enumerate(PASSES):
                        last = pe.matmul(out_, (xt_hi, xt_lo)[s][:, c, b * P:(b + 1) * P], w((g_hi, g_lo)[m], i),
                                         start=start and i == 0 and k == 0,
                                         stop=stop and i == len(cs) - 1 and k == 2, skip_group_check=True)
                return last

            def dense(g, banks, n=512, k=None):
                for u in range(2):
                    pe.wait_ge(M.lo_g, 2 * g + u + 1)
                    for b in range(TB):
                        fresh(k, b, u)
                        last = rows(bank(banks[b])[:, 0:n], b, range(4 * u, 4 * u + 4),
                                    lambda t, i: t[:, u, i * n:(i + 1) * n], n, u == 0, u == 1)
                    last.then_inc(M.used_g, 1)

            def features(g, b0):
                for u in range(2):
                    pe.wait_ge(M.lo_g, 2 * g + u + 1)
                    for m in range(4):
                        for c in range(4):
                            for k, (s, w) in enumerate(PASSES):
                                last = pe.matmul(bank(b0 + m // 2)[:, (m % 2) * T:(m % 2 + 1) * T],
                                                 (g_hi, g_lo)[w][:, u, c * 512 + m * P:c * 512 + (m + 1) * P],
                                                 (xt_hi, xt_lo)[s][:, 4 * u + c, :],
                                                 start=u == 0 and c == 0 and k == 0 and m % 2 == 0,
                                                 stop=u == 1 and c == 3 and k == 2, skip_group_check=True)
                    last.then_inc(M.used_g, 1)

            def gate_up(S, g, q, u, it=None, k=None):
                pe.wait_ge(S.lo_g, at(2 * g + u + 1, it, 4))
                if u == 0 and q:
                    pe.wait_ge(S.gated, at(2 * q, it, 4))
                for b in range(TB):
                    fresh(k, b, u)
                    last = rows(bank(4 + b), b, range(4 * u, 4 * u + 4),
                                lambda t, i: t[:, u, i * 512:(i + 1) * 512], 512, u == 0, u == 1)
                last.then_inc(S.used_g, 1)

            def turn(S, q, it=None):
                pe.wait_ge(S.gated, at(2 * q + 2, it, 4))
                for c in range(2):
                    for b in range(TB):
                        o = (c * TB + b) * P
                        last = pe.transpose(bank(6)[:, o:o + P], a_sb[:, b, c:FF:2], ident)
                last.then_inc(S.tr_done, 1)

            def down(S, d, b, it=None, stop=False):
                pe.wait_ge(S.at_lo, at(d + 1, it, 2))
                pe.wait_ge(S.lo_d, at(d + 1, it, 2))
                for m in range(2):
                    for c in range(2):
                        for k, (i, w) in enumerate(PASSES):
                            last = pe.matmul(bank(2 * b + m), (at_hi, at_lo)[i][:, c, b * P:(b + 1) * P],
                                             (d_hi, d_lo)[w][:, c * D + m * 512:c * D + (m + 1) * 512],
                                             start=False, stop=stop and c == 1 and k == 2, skip_group_check=True)
                if b == TB - 1:
                    last.then_inc(S.used_d, 1)

            def zero_sums():
                for i in range(4):
                    last = pe.matmul(bank(i), zeros[:, 0:P], zeros[:, :], start=True, stop=False,
                                     skip_group_check=True)
                return last

            def gated_phase(name, k=None):
                S, g0, d0, q0, n = PHASES[name]
                gate_up(S, g0, q0, 0, k=k)
                gate_up(S, g0, q0, 1, k=k)
                for s, it in turns(pe, n):
                    if s + 1 < n:
                        gate_up(S, g0 + s + 1, q0 + s + 1, 0, it)
                    turn(S, q0 + s, it)
                    if s + 1 < n:
                        gate_up(S, g0 + s + 1, q0 + s + 1, 1, it)
                    for b in range(TB):
                        down(S, d0 + s, b, it, stop=s == n - 1)

            def sparse_phase():
                def fill(s, k, it=None):
                    pair, c = s // 2 + 1, 4 * (s % 2) + k - k % 2
                    n = 8 + 4 * s + k
                    if s == -1:
                        pe.wait_ge((xg_a, xg_v)[k % 2], k // 2 + 1)
                    elif s >= 0 and k % 2:
                        pe.wait_ge(xg_a, at((n + 1) // 2, it, 8))
                    elif s >= 0:
                        pe.wait_ge(xg_v, at(n // 2, it, 8))
                    if s % 2 == 0 and k == 0:
                        pe.wait_ge(picked, at(pair + 1, it, 2))
                    for i in range(2):
                        for b in range(TB):
                            last = pe.matmul(fill_bank(s, k)[:, i * 2 * CAP:(i + 1) * 2 * CAP], tok[k % 2][:, b, c + i, :],
                                             pick[:, pair % 2, b, :, :].rearrange("p e r -> p (e r)"),
                                             start=b == 0, stop=b == TB - 1)
                    last.then_inc(ga_ps, 1)

                def rows_t(s, it=None):
                    pe.wait_ge(sp_gate, at(s + 1, it, 4))
                    if s:
                        pe.wait_ge(y_v, at(2 * s, it, 8))
                    for c in range(2):
                        last = pe.transpose(bank(5)[:, c * CAP:(c + 1) * CAP], a_sb[0:CAP, 0, c:FF:2],
                                            ident[0:CAP, 0:CAP])
                    last.then_inc(M.tr_done, 1)

                def rows_down(s, it=None):
                    pe.wait_ge(M.at_lo, at(D_SP + s + 1, it, 4))
                    pe.wait_ge(M.lo_d, at(D_SP + s + 1, it, 4))
                    for m in range(2):
                        for c in range(2):
                            for k, (i, w) in enumerate(PASSES):
                                last = pe.matmul(bank(5 + m)[0:CAP, :], (at_hi, at_lo)[i][:, c, 0:CAP],
                                                 (d_hi, d_lo)[w][:, c * D + m * 512:c * D + (m + 1) * 512],
                                                 start=c == 0 and k == 0, stop=c == 1 and k == 2)
                        last.then_inc(M.used_d if m else y_ps, 1)

                def scatter(s, it=None):
                    for m in range(2):
                        pe.wait_ge(y_v, at(2 * s + m + 1, it, 8))
                        for b in range(TB):
                            for k, t in enumerate((y_hi, y_lo)):
                                last = pe.matmul(bank(2 * b + m), pickT[0:CAP, s % 2, b * P:(b + 1) * P],
                                                 t[0:CAP, m * 512:(m + 1) * 512], start=False,
                                                 stop=it is None and s == E - 1 and k == 1, skip_group_check=True)
                    last.then_inc(summed, 1)

                def body(s, it=None):
                    g = G_SP + s
                    more = s + 2 < E or it is not None
                    for u in range(2):
                        pe.wait_ge(M.lo_g, at(2 * g + u + 1, it, 8))
                        if s % 2 == 0:
                            n = 4 if s == 0 else 2 * s + 2 + 2 * u
                            pe.wait_ge(xg_a, at(n, it, 8))
                            pe.wait_ge(xg_v, at(n, it, 8))
                        if u == 0:
                            if s:
                                pe.wait_ge(sp_gate, at(s, it, 4))
                        for i in range(4):
                            for k, (j, w) in enumerate(PASSES):
                                last = pe.matmul(bank(4)[0:CAP, :], (xg_hi, xg_lo)[j][:, s // 2 % 2, 4 * u + i, s % 2, :],
                                                 (g_hi, g_lo)[w][:, u, i * 512:(i + 1) * 512],
                                                 start=u == 0 and i == 0 and k == 0, stop=u == 1 and i == 3 and k == 2)
                        last.then_inc(M.used_g, 1)
                        if u == 0:
                            if s and (s + 1 < E or it is not None):
                                fill(s - 1, 3, it)
                            if s >= 2:
                                scatter(s - 2, it)
                            if s:
                                rows_t(s - 1, it)
                            if s:
                                pe.wait_ge(pt_sb, at(s, it, 4))
                            for b in range(TB):
                                pe.transpose(bank(6)[0:CAP, b * P:(b + 1) * P],
                                             pick[:, s // 2 % 2, b, s % 2, :].bitcast(F32), ident)
                            for b in range(TB):
                                w = w_hl[:, b, s, :] if it is None else \
                                    w_hl[:, b, bass.ds(it * 4 + s, 1), :].rearrange("p e k -> p (e k)")
                                last = pe.matmul(bank(6)[0:CAP, T:T + 2], pick[:, s // 2 % 2, b, s % 2, :], w,
                                                 start=b == 0, stop=b == TB - 1)
                            last.then_inc(pt_ps, 1)
                        if more:
                            fill(s, u, it)
                    if s:
                        pe.wait_ge(pt_sb, at(s + 1, it, 4))
                        rows_down(s - 1, it)
                    if more:
                        fill(s, 2, it)

                pe.wait_ge(tok_lo, 1)
                for s in (-2, -1):
                    for k in range(4):
                        fill(s, k)
                body(0)
                body(1)
                for s, it in turns(pe, E, 2, 4, 2):
                    body(s, it)
                scatter(E - 2)
                rows_t(E - 1)
                rows_down(E - 1)
                scatter(E - 1)

            def softmaxes(k, kw, scores, values):
                def score(n):
                    i = n - 8 * k
                    if i >= 2:
                        pe.wait_ge(s_max, n - 1)
                    w = kw(i % 2)
                    for j in range(2):
                        lhsT, rhs = scores(pair_heads(i // 2)[j], i % 2)
                        last = pe.matmul(bank(2 + n % 2)[:, j * w:(j + 1) * w], lhsT, rhs, start=True, stop=True)
                    last.then_inc(s_ps, 1)

                def turn(n):
                    i = n - 8 * k
                    pe.wait_ge(s_exp, n + 1)
                    if i >= 2:
                        pe.wait_ge(s_ptc, n - 1)
                    cs = kw(i % 2) // P
                    for j in range(2):
                        for c in range(cs):
                            o = (j * cs + c) * P
                            last = pe.transpose(bank(4 + n % 2)[:, o:o + P], s_buf[n % 2][:, j, c * P:(c + 1) * P],
                                                ident)
                    last.then_inc(s_pt, 1)

                def output(n):
                    i = n - 8 * k
                    pe.wait_ge(s_ptc, n + 1)
                    if i >= 2:
                        pe.wait_ge(s_fin, n - 1)
                    cs = kw(i % 2) // P
                    for j in range(2):
                        for c in range(cs):
                            o = (j * cs + c) * P
                            last = pe.matmul(bank(6 + n % 2)[:, j * HD:(j + 1) * HD], pT_sb(k, n)[:, o:o + P],
                                             values(pair_heads(i // 2)[j], c), start=c == 0, stop=c == cs - 1)
                    last.then_inc(s_o, 1)

                score(8 * k)
                for i in range(8):
                    if i < 7:
                        score(8 * k + i + 1)
                    turn(8 * k + i)
                    if i:
                        output(8 * k + i - 1)
                output(8 * k + 7)

            pe.wait_ge(in_["relb"], 16)
            pe.wait_ge(in_["bucket"], 16)
            pe.wait_ge(set_up, 3)
            pe.matmul(bank(0)[0:NH, 0:BX], relb_in, bucket_in, start=True, stop=True).then_inc(tb_ps, 1)
            pe.wait_ge(in_["bada"], 16)
            pe.wait_ge(c_bc, 1)
            for t in range(N_ADA):
                out_ = bank(4 + t % 4)
                if t >= 4:
                    pe.wait_ge(ada_ev, t - 3)
                pe.matmul(out_, ones[0:1, :], b_ada_row[0:1, t * 512:(t + 1) * 512], start=True, stop=False,
                          skip_group_check=True)
                for u in range(2):
                    pe.wait_ge(M.lo_g, 2 * t + u + 1)
                    last = rows(out_, 0, range(4 * u, 4 * u + 4), lambda w, i: w[:, u, i * 512:(i + 1) * 512],
                                512, False, u == 1)
                    last.then_inc(M.used_g, 1)

            pe.wait_ge(in_["con"], 16)
            pe.wait_ge(tb_sb, 1)
            transposes(0)
            pe.wait_ge(M.xt_lo, 4)
            pe.wait_ge(ada_ev, N_ADA)
            for j in range(N_WIN):
                b0 = 4 + 2 * (j % 2)
                if j >= 2:
                    pe.wait_ge(ev_a, EV_A[G_WIN + j - 2])
                    pe.wait_ge(ev_v, EV_V[G_WIN + j - 2])
                if j in (0, 1, 3, 4):
                    features(G_WIN + j, b0)
                else:
                    dense(G_WIN + j, (b0, b0 + 1))
            pe.wait_ge(ev_a, EV_A[G_WIN + N_WIN - 1])
            pe.wait_ge(ev_v, EV_V[G_WIN + N_WIN - 1])

            def sb_scores(g):
                if g >= 2:
                    pe.wait_ge(sb_ol, g - 1)
                for i in range(2):
                    r = slice(i * 64, i * 64 + 64)
                    out_ = bank(2 * (g % 2) + i)
                    pe.matmul(out_[:, 0:T], kT[0][r, g, 0:P], qT[0][r, g, :], start=True, stop=True)
                    pe.matmul(out_[:, T:384], kT[0][r, g, P:T], qT[0][r, g, P:T], start=True, stop=True)\
                        .then_inc(sb_z, 1)

            def sb_sums(g):
                pe.wait_ge(sb_r, g + 1)
                for i in range(2):
                    r0, r1 = (of_group(l_sb, g)[:, i * 384 + lo:i * 384 + hi] for lo, hi in ((0, T), (T, 384)))
                    out_ = bank(4 + 2 * (g % 2) + i)
                    pe.matmul(out_[:, T:384], tri, r1, start=True, stop=True)
                    pe.matmul(out_[:, 0:T], tri, r0, start=True, stop=False, skip_group_check=True)
                    pe.matmul(out_[:, P:T], ones[:, :], r1, start=False, stop=True, skip_group_check=True)\
                        .then_inc(sb_i, 1)

            def sb_out(g):
                pe.wait_ge(sb_a, g + 1)
                for i in range(2):
                    hd = 2 * g + i
                    out_ = bank(SB_OUT[g])[i * 64:i * 64 + 64, :]
                    vs = [v_tok[:, b, hd * HD:(hd + 1) * HD] for b in range(TB)]
                    p = of_group(p_sb, g)[:, i * 384:(i + 1) * 384]
                    pe.matmul(out_[:, 0:T], vs[0], p[:, 0:T], start=True, stop=False, skip_group_check=True)
                    last = pe.matmul(out_[:, P:T], vs[1], p[:, T:384], start=False, stop=True, skip_group_check=True)
                last.then_inc(sb_o, 1)

            for half in range(2):
                pair = (2 * half, 2 * half + 1)
                for g in pair:
                    if half:
                        sb_out(g - 2)
                    sb_scores(g)
                for g in pair:
                    sb_sums(g)
            sb_out(2)
            sb_out(3)

            def mb_scores(hd, b):
                r, m = slice((hd % 2) * 64, (hd % 2) * 64 + 64), hd // 2
                return qT[1][r, m, b * P:(b + 1) * P], kT[1][r, m, 0:P * (b + 1)]

            softmaxes(0, lambda b: P * (b + 1), mb_scores,
                      lambda hd, c: v_tok[:, c, 512 + hd * HD:512 + (hd + 1) * HD])
            pe.wait_ge(s_fin, 8)
            pe.wait_ge(sb_ol, 4)
            for q in range(2):
                for m in (2 * q, 2 * q + 1):
                    for b in range(TB):
                        o = ((m % 2) * TB + b) * P
                        last = pe.transpose(bank(q)[:, o:o + P], o_mb[:, b, m * P:(m + 1) * P], ident)
                last.then_inc(ot_ps, 1)
            pe.wait_ge(ot_lo, 2)
            for t in range(2):
                for u in range(2):
                    pe.wait_ge(M.lo_g, 2 * (G_WB + t) + u + 1)
                    for b in range(TB):
                        for n in range(2):
                            last = rows(bank(4 * t + 2 * b + n), b, (4 * t + 2 * u, 4 * t + 2 * u + 1),
                                        lambda w, i: w[:, u, i * D + n * 512:i * D + (n + 1) * 512], 512,
                                        u == 0, u == 1)
                    last.then_inc(M.used_g, 1)
            transposes(1)
            for i in range(2):
                dense(G_WO + i, (4 + i, 6 + i), k=(1, None)[i])
            transposes(2)
            pe.wait_ge(rt_wlo, 1)
            for b in range(TB):
                pe.wait_ge(M.xt_lo, 8 + 2 * b + 2)
                for c in range(DC):
                    for k, (i, w) in enumerate(PASSES):
                        last = pe.matmul(bank(7)[:, b * E:(b + 1) * E], (xt_hi, xt_lo)[i][:, c, b * P:(b + 1) * P],
                                         w_rt_hl[w][:, c, :], start=c == 0 and k == 0, stop=c == DC - 1 and k == 2)
            last.then_inc(rt_ps, 1)
            zero_sums().then_inc(M.used_d, 1)
            gate_up(M, G_SH, 0, 0)
            gate_up(M, G_SH, 0, 1)
            pe.wait_ge(rt_sel, 1)
            before = con[:, C_MASK:C_MASK + P]
            pe.matmul(bank(7)[:, 0:E], before, rt[:, 8 * E:9 * E], start=True, stop=True)
            pe.matmul(bank(7)[:, E:2 * E], before, rt[:, 9 * E:10 * E], start=True, stop=False)
            pe.matmul(bank(7)[:, E:2 * E], ones[:, :], rt[:, 8 * E:9 * E], start=False, stop=True).then_inc(rt_pos, 1)
            turn(M, 0)
            for b in range(TB):
                down(M, D_SH, b)
            pe.wait_ge(rt_cnt, 1)
            pe.matmul(bank(5)[0:1, 0:1], st[:, 52:53], ones[:, 0:1], start=True, stop=True).then_inc(rt_tot, 1)
            pe.wait_ge(rt_flag, 1)
            sparse_phase()

            def over():
                pe.wait_ge(h_again, 1)
                transposes(0, OV, 4)
                pe.wait_ge(OV.xt_lo, 4)
                pe.sem_inc(OV.used_d, 1)
                gated_phase("over")
                pe.wait_ge(OV.used_d, E + 1)

            if_over(pe, over)
            transposes(3)
            pe.wait_ge(M.xt_lo, 16)
            zero_sums()
            gated_phase("ff1")
            transposes(4)
            pe.wait_ge(M.xt_lo, 20)
            for j in range(4):
                b0 = 4 + 2 * (j % 2)
                if j >= 2:
                    pe.wait_ge(ev_a, EV_A[G_WIN2 + j - 2])
                    pe.wait_ge(ev_v, EV_V[G_WIN2 + j - 2])
                if j < 2:
                    features(G_WIN2 + j, b0)
                else:
                    dense(G_WIN2 + j, (b0, b0 + 1), 512 if j == 2 else SMALL)
            pe.wait_ge(ev_a, EV_A[G_WIN2 + 3])
            pe.wait_ge(ev_v, EV_V[G_WIN2 + 3])

            def na_scores(hd, b):
                r, m = slice((hd % 2) * 64, (hd % 2) * 64 + 64), hd // 2
                return qT2[r, m, b * P:(b + 1) * P], kT2[r, m, :]

            softmaxes(1, lambda b: T, na_scores, lambda hd, c: v2[:, c, hd * HD:(hd + 1) * HD])
            pe.wait_ge(cn_ready, 1)
            for q in range(2):
                for c in range(2 * q, min(2 * q + 2, 3)):
                    for b in range(TB):
                        o = ((c % 2) * TB + b) * P
                        last = pe.transpose(bank(q)[:, o:o + P], small[:, b, c * P:(c + 1) * P], ident)
                last.then_inc(cn_ps, 1)
            pe.wait_ge(cn_lo, 2)
            pe.wait_ge(s_fin, 16)
            for u, (base, cs, step, n) in enumerate(((0, (0, 1), QW, 384), (4, (2,), KVW, 512))):
                pe.wait_ge(M.lo_g, 2 * G_MLA + u + 1)
                for b in range(TB):
                    for j in range(2):
                        last = rows(bank(base + 2 * b + j)[:, 0:n], b, cs,
                                    lambda w, i: w[:, u, i * step + j * n:i * step + (j + 1) * n], n, True, True)
                last.then_inc(M.used_g, 1)
            pe.wait_ge(roped, 2)
            for q in range(8):
                src = (q_tok, k_full)[q // 4]
                if q >= 4:
                    pe.wait_ge((mt_ev_a, mt_ev_v)[q % 2], (q - 4) // 2 + 1)
                for j in range(2):
                    hd = (q % 4) * 2 + j
                    for b in range(TB):
                        o = (j * TB + b) * P
                        last = pe.transpose(bank(q % 4)[0:96, o:o + P], src[:, b, hd * 96:(hd + 1) * 96], ident)
                last.then_inc(mt_ps, 1)
            pe.wait_ge(mt_ev_a, 4)
            pe.wait_ge(mt_ev_v, 4)
            softmaxes(2, lambda b: T, lambda hd, b: (qTm[0:96, hd, b * P:(b + 1) * P], kTm[0:96, hd, :]),
                      lambda hd, c: kv_tok[:, c, hd * 128 + 64:hd * 128 + 128])
            transposes(5)
            for i in range(2):
                dense(G_WO2 + i, (4 + i, 6 + i), k=(5, None)[i])
            transposes(6)
            pe.wait_ge(M.xt_lo, 28)
            zero_sums()
            gated_phase("ff2")


def distance_buckets():
    dist = 255 - np.arange(BX)
    n = np.maximum(dist, 0)
    large = 16 + (np.log(np.maximum(n, 1).astype(np.float32) / np.float32(16)) / np.float32(math.log(8.0))
                  * np.float32(16)).astype(np.int32)
    bucket = np.where(n < 16, n, np.minimum(large, 31))
    rows = np.zeros((33, BX), np.float32)
    rows[bucket, np.arange(BX)] = dist >= 0
    rows[32] = np.where(dist >= 0, 0.0, -BIG)
    return rows


def constants():
    con = np.zeros((P, C_END), np.float32)
    i = np.arange(P)
    con[:, C_ID:C_ID + P] = np.eye(P)
    con[:, C_TRI:C_TRI + P] = i[:, None] >= i[None, :]
    past = i[:, None] < i[None, :]
    con[:, C_MASK:C_MASK + P] = past
    con[:, C_MIN:C_MIN + P] = np.where(past, BIG, -BIG)
    c = np.arange(64)
    first = np.clip(c - 8, 0, 48)[:, None]
    inside = (c[None, :] >= first) & (c[None, :] < first + 16)
    con[:, C_IOTA:C_IOTA + P] = i[None, :]
    con[:, C_NA:C_NA + 64] = np.tile(np.where(inside, 0.0, -BIG), (2, 1))
    freq = (1.0 / (np.float32(10000.0) ** (np.arange(8, dtype=np.float32) / np.float32(8)))).astype(np.float32)
    t = np.arange(T)
    ang = np.concatenate([(t // 64).astype(np.float32)[:, None] * freq, (t % 64).astype(np.float32)[:, None] * freq], 1)
    for b in range(TB):
        con[:, C_COS + 16 * b:C_COS + 16 * (b + 1)] = np.cos(ang[b * P:(b + 1) * P])
        con[:, C_SIN + 16 * b:C_SIN + 16 * (b + 1)] = np.sin(ang[b * P:(b + 1) * P])
    return con


INPUTS = ["x", "c", "norm1_g", "norm2_g", "w_ada", "b_ada", "w_in", "w_branch_sb", "w_branch_mb", "w_out", "w_router",
          "router_bias", "w_gate_e", "w_up_e", "w_down_e", "w_gate_sh", "w_up_sh", "w_down_sh", "final_g",
          "ffn1_pre_g_2", "ffn1_w_gu_2", "ffn1_w_down_2", "ffn1_post_g_2", "mix_pre_g_2", "w_in_2", "na_rpb_2",
          "mla_q_norm_g_2", "mla_w_uq_2", "mla_kv_norm_g_2", "mla_w_ukv_2", "na_out_norm_g_2", "mla_out_norm_g_2",
          "w_out_2", "mix_post_g_2", "ffn2_pre_g_2", "ffn2_w_gu_2", "ffn2_w_down_2", "ffn2_post_g_2"]


def kernel(**inputs):
    from concourse import bacc
    from concourse.bass_utils import run_bass_kernel_spmd

    nc = bacc.Bacc("TRN2", target_bir_lowering=False, num_devices=1)
    arrays = {n: np.ascontiguousarray(inputs[n]) for n in INPUTS}
    arrays["rel_bias_t"] = np.ascontiguousarray(np.asarray(inputs["rel_bias"]).T)
    arrays["con"] = constants()
    arrays["buckets"] = distance_buckets()
    a = {n: nc.dram_tensor("in_" + n, v.shape, mybir.dt.from_np(v.dtype), kind="ExternalInput").ap()
         for n, v in arrays.items()}
    out = nc.dram_tensor("out", (1, T, D), F32, kind="ExternalOutput").ap()
    build(nc, a, out)
    r = run_bass_kernel_spmd(nc, [{"in_" + n: v for n, v in arrays.items()}], core_ids=[0])
    return r.results[0]["out"]
```
